# Optimizing a Trainium2 kernel written in Bass

```python
import jax, jax.numpy as jnp
from jax import lax
import numpy as np

D_MODEL = 1024
BATCH = 1
SEQ = 256
DEPTH = 2
DEC_BATCH = 8
DEC_SEQ = 4
PAST_LEN = 2048
PAGE_SIZE = 128

N_A_LAYERS = (DEPTH + 1) // 2
N_B_LAYERS = DEPTH // 2
N_VRES = max(N_B_LAYERS - 1, 0)
CHUNK = 128
A_WIDTH = 2 * D_MODEL
A_GROUPS = 8
A_GROUP_DIM = A_WIDTH // A_GROUPS
HEAD_DIM = 64
N_HEADS = D_MODEL // HEAD_DIM
LORA_W = 64
LORA_A = 64
LORA_V = 32
LORA_G = 160
D_FF = 2816
N_EXPERTS = 8
TOP_K = 2
RMS_EPS = 1e-6
LN_EPS = 1e-5
GN_EPS = 64e-5

kernel_name = "gmlp_chunk_rwkv7_hybrid_step"

def _rmsnorm(x, g):
    xf = x.astype(jnp.float32)
    y = xf * lax.rsqrt(jnp.mean(xf * xf, axis=-1, keepdims=True) + RMS_EPS)
    return (y * g.astype(jnp.float32)).astype(x.dtype)

def _layernorm(x, g, b):
    xf = x.astype(jnp.float32)
    xc = xf - jnp.mean(xf, axis=-1, keepdims=True)
    y = xc * lax.rsqrt(jnp.mean(xc * xc, axis=-1, keepdims=True) + LN_EPS)
    return (y * g.astype(jnp.float32) + b.astype(jnp.float32)).astype(x.dtype)

def _chunk_sgu_mix(h, w_in, b_in, ln_g, ln_b, w_s, b_s, w_out):
    bsz, t, _ = h.shape
    L = min(t, CHUNK)
    n_chunks = t // L
    z = jax.nn.gelu(h @ w_in + b_in, approximate=False)
    u, v = jnp.split(z, 2, axis=-1)
    v = _layernorm(v, ln_g, ln_b)
    mask = jnp.tril(jnp.ones((L, L), dtype=bool))
    w_c = jnp.where(mask, w_s[:, :L, :L], 0).astype(v.dtype)
    vc = v.reshape(bsz, n_chunks, L, A_GROUPS, A_GROUP_DIM)
    mixed = jnp.einsum("gts,bcsgd->bctgd", w_c, vc) + b_s[:, :L].T[:, :, None].astype(v.dtype)
    out = u * mixed.reshape(bsz, t, A_WIDTH)
    return out @ w_out, v

def _wkv7_scan(r, decay, k, v, kk, alpha, s0):
    def step(s, inp):
        r_t, w_t, k_t, v_t, kk_t, a_t = inp
        s_kk = jnp.einsum("bhij,bhj->bhi", s, kk_t)
        s = (s * w_t[:, :, None, :]
             - s_kk[..., None] * (kk_t * a_t)[:, :, None, :]
             + v_t[..., None] * k_t[:, :, None, :])
        y = jnp.einsum("bhij,bhj->bhi", s, r_t)
        return s, y
    xs = tuple(jnp.swapaxes(z, 0, 1) for z in (r, decay, k, v, kk, alpha))
    s_last, ys = lax.scan(step, s0, xs)
    return jnp.swapaxes(ys, 0, 1), s_last

def _rwkv7_mix(h, shift0, wkv0, v_first, vres, mu, w_rkv, w0, w1, w2, a0, a1, a2,
               g1, g2, k_k, k_a, r_k, lnx_g, lnx_b, w_out):
    bsz, t, _ = h.shape
    h_prev = jnp.concatenate([shift0[:, None, :].astype(h.dtype), h[:, :-1]], axis=1)
    xx = h_prev - h
    mixed = h[None] + xx[None] * mu[:, None, None, :]
    r, k, v = jnp.einsum("sbtd,sde->sbte", mixed[:3], w_rkv)
    xv, xw, xa, xg = mixed[2], mixed[3], mixed[4], mixed[5]
    w_log = -jax.nn.softplus(-(w0 + jnp.tanh(xw @ w1) @ w2)) - 0.5
    decay = jnp.exp(-jnp.exp(w_log.astype(jnp.float32)))
    if vres is None:
        v_first = v
    else:
        v0, v1, v2 = vres
        v = v + (v_first - v) * jax.nn.sigmoid(v0 + (xv @ v1) @ v2)
    alpha = jax.nn.sigmoid(a0 + (xa @ a1) @ a2)
    g = jax.nn.sigmoid(xg @ g1) @ g2

    def heads(z):
        return z.reshape(bsz, t, N_HEADS, HEAD_DIM).astype(jnp.float32)

    kk = heads(k * k_k)
    kk = kk / jnp.maximum(jnp.sqrt(jnp.sum(kk * kk, axis=-1, keepdims=True)), 1e-12)
    k = k * (1 + (alpha - 1) * k_a)
    rh, kh, vh, ah, wh = heads(r), heads(k), heads(v), heads(alpha), heads(decay)
    y, s_last = _wkv7_scan(rh, wh, kh, vh, kk, ah, wkv0.astype(jnp.float32))
    yc = y - jnp.mean(y, axis=-1, keepdims=True)
    y = yc * lax.rsqrt(jnp.mean(yc * yc, axis=-1, keepdims=True) + GN_EPS)
    y = y.reshape(bsz, t, D_MODEL) * lnx_g.astype(jnp.float32) + lnx_b.astype(jnp.float32)
    bonus = jnp.sum(rh * kh * r_k.astype(jnp.float32), axis=-1, keepdims=True) * vh
    y = (y + bonus.reshape(bsz, t, D_MODEL)).astype(h.dtype)
    out = (y * g) @ w_out
    return out, h[:, -1].astype(shift0.dtype), s_last.astype(wkv0.dtype), v_first

def _swiglu(h, wg, wu, wd):
    return (jax.nn.silu(h @ wg) * (h @ wu)) @ wd

def _moe(h, router, wg, wu, wd):
    shp = h.shape
    xt = h.reshape(-1, D_MODEL)
    logits = (xt @ router).astype(jnp.float32)
    top_v, top_i = lax.top_k(logits, TOP_K)
    top_w = jax.nn.softmax(top_v, axis=-1)
    gates = jnp.sum(jax.nn.one_hot(top_i, N_EXPERTS, dtype=jnp.float32) * top_w[..., None],
                    axis=1).astype(h.dtype)
    y = jnp.zeros_like(xt)
    for e in range(N_EXPERTS):
        y = y + gates[:, e:e + 1] * _swiglu(xt, wg[e], wu[e], wd[e])
    return y.reshape(shp)

def _trunk(x, shift_in, wkv_in, p):
    chunk_v, shift_out, wkv_out = [], [], []
    v_first = None
    for i in range(DEPTH):
        j = i // 2
        h = _rmsnorm(x, p["norm_mix_g"][i])
        if i % 2 == 0:
            y, v_rows = _chunk_sgu_mix(h, p["a_w_in"][j], p["a_b_in"][j], p["a_ln_g"][j],
                                       p["a_ln_b"][j], p["a_w_s"][j], p["a_b_s"][j],
                                       p["a_w_out"][j])
            chunk_v.append(v_rows)
        else:
            vres = None if j == 0 else (p["b_v0"][j - 1], p["b_v1"][j - 1], p["b_v2"][j - 1])
            y, s_row, s_wkv, v_first = _rwkv7_mix(
                h, shift_in[j], wkv_in[j], v_first, vres, p["b_mu"][j], p["b_w_rkv"][j],
                p["b_w0"][j], p["b_w1"][j], p["b_w2"][j], p["b_a0"][j], p["b_a1"][j],
                p["b_a2"][j], p["b_g1"][j], p["b_g2"][j], p["b_k_k"][j], p["b_k_a"][j],
                p["b_r_k"][j], p["b_lnx_g"][j], p["b_lnx_b"][j], p["b_w_out"][j])
            shift_out.append(s_row)
            wkv_out.append(s_wkv)
        x = x + y
        h = _rmsnorm(x, p["norm_ffn_g"][i])
        if i % 2 == 0:
            x = x + _swiglu(h, p["f_w_gate"][j], p["f_w_up"][j], p["f_w_down"][j])
        else:
            x = x + _moe(h, p["m_router"][j], p["m_w_gate"][j], p["m_w_up"][j], p["m_w_down"][j])
    return _rmsnorm(x, p["norm_out_g"]), chunk_v, shift_out, wkv_out

def setup_inputs(seed: int = 0) -> dict:
    key = jax.random.key(seed)
    ks = iter(jax.random.split(key, 64))
    D = D_MODEL

    def nrm(shape, scale):
        return jax.random.normal(next(ks), shape, jnp.float32) * scale

    def uni(shape, lo, hi):
        return jax.random.uniform(next(ks), shape, jnp.float32, lo, hi)

    return {
        "x_prompt": nrm((BATCH, SEQ, D), 1.0),
        "x_sample": nrm((DEC_BATCH, DEC_SEQ, D), 1.0),
        "state_shift": nrm((N_B_LAYERS, DEC_BATCH, D), 1.0),
        "state_wkv": nrm((N_B_LAYERS, DEC_BATCH, N_HEADS, HEAD_DIM, HEAD_DIM), 0.3),
        "norm_mix_g": 1.0 + nrm((DEPTH, D), 0.02),
        "norm_ffn_g": 1.0 + nrm((DEPTH, D), 0.02),
        "norm_out_g": 1.0 + nrm((D,), 0.02),
        "a_w_in": nrm((N_A_LAYERS, D, 2 * A_WIDTH), D ** -0.5),
        "a_b_in": nrm((N_A_LAYERS, 2 * A_WIDTH), 0.02),
        "a_ln_g": 1.0 + nrm((N_A_LAYERS, A_WIDTH), 0.02),
        "a_ln_b": nrm((N_A_LAYERS, A_WIDTH), 0.02),
        "a_w_s": nrm((N_A_LAYERS, A_GROUPS, CHUNK, CHUNK), 0.5 * CHUNK ** -0.5),
        "a_b_s": 1.0 + nrm((N_A_LAYERS, A_GROUPS, CHUNK), 0.1),
        "a_w_out": nrm((N_A_LAYERS, A_WIDTH, D), A_WIDTH ** -0.5),
        "b_mu": uni((N_B_LAYERS, 6, D), 0.0, 1.0),
        "b_w_rkv": nrm((N_B_LAYERS, 3, D, D), D ** -0.5),
        "b_w0": uni((N_B_LAYERS, D), -6.0, -1.0),
        "b_w1": nrm((N_B_LAYERS, D, LORA_W), D ** -0.5),
        "b_w2": nrm((N_B_LAYERS, LORA_W, D), 0.5 * LORA_W ** -0.5),
        "b_a0": nrm((N_B_LAYERS, D), 0.1),
        "b_a1": nrm((N_B_LAYERS, D, LORA_A), D ** -0.5),
        "b_a2": nrm((N_B_LAYERS, LORA_A, D), 0.5 * LORA_A ** -0.5),
        "b_v0": 1.0 + nrm((N_VRES, D), 0.1),
        "b_v1": nrm((N_VRES, D, LORA_V), D ** -0.5),
        "b_v2": nrm((N_VRES, LORA_V, D), 0.5 * LORA_V ** -0.5),
        "b_g1": nrm((N_B_LAYERS, D, LORA_G), D ** -0.5),
        "b_g2": nrm((N_B_LAYERS, LORA_G, D), LORA_G ** -0.5),
        "b_k_k": 0.85 + nrm((N_B_LAYERS, D), 0.02),
        "b_k_a": 1.0 + nrm((N_B_LAYERS, D), 0.02),
        "b_r_k": nrm((N_B_LAYERS, N_HEADS, HEAD_DIM), 0.1),
        "b_lnx_g": 1.0 + nrm((N_B_LAYERS, D), 0.02),
        "b_lnx_b": nrm((N_B_LAYERS, D), 0.02),
        "b_w_out": nrm((N_B_LAYERS, D, D), D ** -0.5),
        "f_w_gate": nrm((N_A_LAYERS, D, D_FF), D ** -0.5),
        "f_w_up": nrm((N_A_LAYERS, D, D_FF), D ** -0.5),
        "f_w_down": nrm((N_A_LAYERS, D_FF, D), D_FF ** -0.5),
        "m_router": nrm((N_B_LAYERS, D, N_EXPERTS), D ** -0.5),
        "m_w_gate": nrm((N_B_LAYERS, N_EXPERTS, D, D_FF), D ** -0.5),
        "m_w_up": nrm((N_B_LAYERS, N_EXPERTS, D, D_FF), D ** -0.5),
        "m_w_down": nrm((N_B_LAYERS, N_EXPERTS, D_FF, D), D_FF ** -0.5),
    }

def reference(x_prompt, x_sample, state_shift, state_wkv, norm_mix_g, norm_ffn_g, norm_out_g,
              a_w_in, a_b_in, a_ln_g, a_ln_b, a_w_s, a_b_s, a_w_out,
              b_mu, b_w_rkv, b_w0, b_w1, b_w2, b_a0, b_a1, b_a2, b_v0, b_v1, b_v2,
              b_g1, b_g2, b_k_k, b_k_a, b_r_k, b_lnx_g, b_lnx_b, b_w_out,
              f_w_gate, f_w_up, f_w_down, m_router, m_w_gate, m_w_up, m_w_down):
    p = dict(norm_mix_g=norm_mix_g, norm_ffn_g=norm_ffn_g, norm_out_g=norm_out_g,
             a_w_in=a_w_in, a_b_in=a_b_in, a_ln_g=a_ln_g, a_ln_b=a_ln_b, a_w_s=a_w_s,
             a_b_s=a_b_s, a_w_out=a_w_out, b_mu=b_mu, b_w_rkv=b_w_rkv, b_w0=b_w0, b_w1=b_w1,
             b_w2=b_w2, b_a0=b_a0, b_a1=b_a1, b_a2=b_a2, b_v0=b_v0, b_v1=b_v1, b_v2=b_v2,
             b_g1=b_g1, b_g2=b_g2, b_k_k=b_k_k, b_k_a=b_k_a, b_r_k=b_r_k, b_lnx_g=b_lnx_g,
             b_lnx_b=b_lnx_b, b_w_out=b_w_out, f_w_gate=f_w_gate, f_w_up=f_w_up,
             f_w_down=f_w_down, m_router=m_router, m_w_gate=m_w_gate, m_w_up=m_w_up,
             m_w_down=m_w_down)
    shift_zero = jnp.zeros((N_B_LAYERS, BATCH, D_MODEL), state_shift.dtype)
    wkv_zero = jnp.zeros((N_B_LAYERS, BATCH, N_HEADS, HEAD_DIM, HEAD_DIM), state_wkv.dtype)
    y_prompt, _, shift_p, wkv_p = _trunk(x_prompt, shift_zero, wkv_zero, p)
    y_sample, chunk_v_s, shift_s, wkv_s = _trunk(x_sample, state_shift, state_wkv, p)
    chunk_v_sample = jnp.stack(chunk_v_s)
    shift_prompt = jnp.stack(shift_p)
    wkv_prompt = jnp.stack(wkv_p)
    shift_sample = jnp.stack(shift_s)
    wkv_sample = jnp.stack(wkv_s)
    return (y_prompt, y_sample, chunk_v_sample, shift_prompt, wkv_prompt, shift_sample, wkv_sample)


_drawn_inputs = setup_inputs


def setup_inputs(seed=0):
    import zlib

    import numpy as np

    out = dict(_drawn_inputs(seed))
    spreads = {}
    factors = {'norm_out_g': 20.319,
     'a_ln_g': 7.74,
     'a_ln_b': 7.889,
     'b_lnx_g': 8.532,
     'b_lnx_b': 18.253,
     'b_k_k': 3.043}
    for name, (base, spread) in spreads.items():
        noise = np.random.default_rng([zlib.crc32(name.encode()), seed]).standard_normal(out[name].shape)
        drawn = base * np.exp(spread * noise) if base else spread * noise
        out[name] = __import__('jax').numpy.asarray(drawn.astype(out[name].dtype))
    for name, factor in factors.items():
        out[name] = (out[name] * factor).astype(out[name].dtype)
    return out
```

```python
from contextlib import ExitStack

import concourse.bass as bass
from concourse import mybir

ALU = mybir.AluOpType
ACT = mybir.ActivationFunctionType
AX_X = mybir.AxisListType.X
F32 = mybir.dt.float32
I32 = mybir.dt.int32
U32 = mybir.dt.uint32

P = 128
D, DC = 1024, 8
NP_, NB, NS = 256, 8, 4
SMP = NB * NS
T = NP_ + SMP
TILES = ((0, 128), (128, 128), (256, 32))
AW, AC = 2048, 16
G = 8
FF, FC = 2816, 22
H, HD = 16, 64
LW, LG = 64, 160
E_, CAP = 8, 96
CH = 64
RMS_EPS, LN_EPS, GN_EPS = 1e-6, 1e-5, 64e-5
DECAY = 0.6065306597126334
LEVELS = (1, 2, 4, 8, 16, 32)

SLOT = 2048
RING = 4
MRING = 11
EPIECES = 33


def trunk_kernel(nc, a, out):
    with ExitStack() as ctx:
        def sb(name, shape, dt=F32):
            return ctx.enter_context(nc.sbuf_tensor(name, shape, dt))

        def sem(name):
            return ctx.enter_context(nc.semaphore(name))

        banks = [ctx.enter_context(nc.psum_tensor(f"bank{i}", [P, 512], F32)) for i in range(8)]

        xT = sb("xT", [P, DC, T])
        vec = sb("vec", [P, 256])
        vecrows = sb("vecrows", [P, 2, P])
        omka = sb("omka", [P, DC])
        ident = sb("ident", [P, P])
        ones = sb("ones", [P, P])
        halves = sb("halves", [P, P])
        eps = sb("eps", [P, 3])
        rt = sb("rt", [P, T])
        rinv = sb("rinv", [P, T])
        arena = sb("arena", [P, 49328])

        def view(off, n, pattern=None, parts=P, **kw):
            v = arena[0:parts, off:off + n]
            return v.rearrange(pattern, **kw) if pattern else v

        def tokens(off, chunks=DC):
            return view(off, chunks * T, "p (c t) -> p c t", c=chunks)

        def slot(i, pattern, parts=P, n=SLOT, off=0, **kw):
            return view(i * SLOT + off, n, pattern, parts=parts, **kw)

        B = [RING * SLOT + DC * T * k for k in range(10)]
        TOK = B[9] + DC * T
        CHN = TOK + 9 * D

        VEC_ROWS = [("norm_mix_g", 16), ("norm_ffn_g", 16), ("norm_out_g", 8), ("a_b_in", 32),
                    ("b_mu", 48), ("b_w0", 8), ("b_a0", 8), ("b_k_k", 8), ("b_k_a", 8), ("b_r_k", 8),
                    ("b_lnx_g", 8), ("b_lnx_b", 8), ("state_shift", 64)]
        col, at = {}, 0
        for name, n in VEC_ROWS:
            col[name] = at
            at += n
        VEC_N = at

        def vcol(name, c):
            return vec[:, col[name] + c:col[name] + c + 1]

        hT = tokens(B[0])
        uT = tokens(B[3], AC)
        vT = tokens(B[5], AC)
        mixT = tokens(B[1])
        lnG = view(B[7], AW)
        lnB = view(B[7] + AW, AW)
        bsB = tokens(B[9])
        vtok = view(TOK, 3 * AW, "p (i n) -> p i n", i=3)
        xtok = view(TOK + 3 * AW, 3 * D, "p (i n) -> p i n", i=3)
        wsT = view(CHN, G * P, "p (g t) -> p g t", g=G)
        wsraw = view(CHN + G * P, G * P, "p (g t) -> p g t", g=G)
        wsS = view(CHN + 2 * G * P, G * SMP, "p (g t) -> p g t", g=G)
        lnst = view(CHN + 2 * G * P + G * SMP, 3 * 4 * 6, "p (i q s) -> p i q s", i=3, q=4)
        lnmv = view(CHN + 2 * G * P + G * SMP + 72, 6, "p (i s) -> p i s", i=3)
        lnrs = view(CHN + 2 * G * P + G * SMP + 78, 6, "p (i s) -> p i s", i=3)
        hF = tokens(B[3], FC)
        sgF = view(B[1], 4 * T, "p (b t) -> p b t", b=4)

        xxT, m0T, m1T = tokens(B[1]), tokens(B[2]), tokens(B[3])
        mixbuf = (m0T, m1T)
        QR = view(B[4], 2 * DC * T, "p (c r t) -> p c r t", c=DC, r=2)
        kT, vfT, aT, dT = tokens(B[6]), tokens(B[7]), tokens(B[8]), tokens(B[9])
        kkT = tokens(B[1])
        t1T = tokens(B[0])
        rkT = tokens(B[2])
        bonT = tokens(B[3])
        yT = tokens(B[7])
        KtT, BtT = tokens(B[1]), tokens(B[9])
        tok = view(TOK, 9 * D, "p (m i n) -> p m i n", m=3, i=3)
        Vk, Kk, Bk = tok[:, 0], tok[:, 1], tok[:, 2]
        MS = view(B[0], 8 * 512, "p (h m t) -> p h m t", h=8, m=4)
        XX = view(B[0] + 4096, 8 * 256, "p (h x t) -> p h x t", h=8, x=2)
        KL, KA, BL, BA = range(4)
        Sbd = view(CHN, 2 * D, "p (b c i) -> p b c i", b=2, c=DC)
        W1 = view(CHN + 2048, 512)
        Us = view(CHN + 2560, 512)
        mskA = view(CHN + 3072, 512, "p (m t) -> p m t", m=4)
        lvl = view(CHN + 3584, 6 * 256, "p (l x t) -> p l x t", l=6, x=2)
        T1 = view(CHN + 5120, 1024, "p (b h t) -> p b h t", b=2, h=4)
        lw1 = view(CHN + 5120, T, parts=LW)
        la1 = view(CHN + 5120 + T, T, parts=LW)
        lg1 = view(CHN + 6144, 2 * T, "p (k t) -> p k t", k=2)
        segm = view(CHN + 6144 + 2 * T, T)
        pc = view(CHN + 7008, 96, "p (c s) -> p c s", c=DC)
        pcn = view(CHN + 7104, 96, "p (c s) -> p c s", c=DC)
        W1Tq = view(CHN + 7200, 32)
        W1q = view(CHN + 7232, P, parts=SMP)
        T1q = view(CHN + 7360, 64, "p (h t) -> p h t", parts=SMP, h=2)
        mskS = view(CHN + 7424, 128, "p (m t) -> p m t", parts=SMP, m=4)
        bmask = view(CHN + 7552, NB, parts=SMP)
        router = view(CHN + 7560, 64, "p (k e) -> p k e", k=DC)
        S0bd = view(CHN + 7680, NB * P, "p (b i) -> p b i", b=NB)
        lastc = view(CHN, 72, "p (c n) -> p c n", c=DC)
        shrow = view(CHN + 128, D, parts=1 + NB)
        nat = view(B[9], 1024, "p (b j) -> p b j", parts=HD, b=NB)
        Uexp = view(B[9], 1024, "p (h b i) -> p h b i", parts=SMP, h=2, b=NB)
        Vexp = view(B[9] + 1024, 1024, "p (h b i) -> p h b i", parts=SMP, h=2, b=NB)
        Sout = view(B[9] + 1024, 1024, "p (b j) -> p b j", parts=HD, b=NB)
        MSq = view(B[9] + 2048, 256, "p (h m t) -> p h m t", parts=SMP, h=2, m=4)
        Send = view(B[0] + 6144, 512, "p (b i) -> p b i", b=NB)
        XXq = view(B[0] + 6656, 128, "p (h x t) -> p h x t", parts=SMP, h=2, x=2)
        Uq = view(B[0] + 6784, P, parts=SMP)
        wkvo = view(B[0], 8 * P, "p (c j) -> p c j", c=DC)

        h3T = tokens(B[8])
        htok = view(TOK, 3 * D, "p (i n) -> p i n", i=3)
        hE = view(TOK + 3072, FC * CAP, "p (c s) -> p c s", c=FC)
        xgE = view(TOK + 5184, DC * CAP, "p (c s) -> p c s", c=DC)
        sgE = view(TOK + 5952, 4 * CAP, "p (b j s) -> p b j s", b=2, j=2)
        yE = view(TOK + 6336, DC * CAP, "p (c s) -> p c s", c=DC)
        yS = view(TOK + 7104, D, parts=CAP)
        GT = view(TOK + 8128, T, parts=CAP)
        Sx = view(TOK + 8416, 3 * CAP, "p (i s) -> p i s", i=3)
        Sg = view(TOK + 8704, 3 * CAP, "p (i s) -> p i s", i=3)
        tri = view(CHN, P)
        slots_i = view(CHN + 128, CAP)
        exp_i = view(CHN + 224, E_)
        rbase = CHN + 256

        def rt3(k, dt=F32):
            v_ = view(rbase + 32 * k, 27, "p (i e) -> p i e", i=3)
            return v_ if dt is F32 else v_.bitcast(dt)

        logit, top, topi, topf = rt3(0), rt3(1), rt3(2, U32), rt3(3)
        oh1, gate, chosen, place, wts = rt3(4), rt3(5), rt3(6), rt3(7), rt3(8)
        most = view(rbase + 300, 2)
        most_i = view(rbase + 302, 1).bitcast(I32)

        S = {}
        for name in """const pool_order vec_in x_in ws_in wsS_in router_in vec_ready vec_tr tr_ready xt_ready sq_ready
            norm_sum rms_ready rinv_ready h_ready omka_ready ws_tr ws_copied ws_masked z_ready gelu_done
            v_tr v_evac v_aggr v_std v_rstd v_norm mix_ready mix_add mix_done ao_ready ffg_ready ffu_ready
            sg_ready hf_ready fd_ready masks memz last_cols last_tr last_rows shift_out xx_ready mx_ready
            lo1_ready lo1_done lo2_ready lo2_done kvr_ready kvr_done kk_raw kk_sq kn_ready kn_root kk_chain
            rk_ready rb_ready bon_ready scan_ready pc_ready tk_tr tk_act tk_dve sc_ready ms_ready xt0_ready
            xt_tr x0_ready t1_ready t1_done x_ready x_done w1_ready w1_done u_ready u_done s_ready s_scaled
            s_done y_ready y_done st_tr st_row st_out nat_in q_vx q_ux q_out gn_mean gn_yc gn_sq gn_var
            gn_root g_ready yg_ready wo_ready r_const r_logit r_chain r_exp r_e r_sel r_pos r_most r_gate
            h_tr h_act h_dve e_sx e_xg e_xga e_xgd e_piece e_sg e_he e_yta e_ytd e_sgx e_ytr e_gtr e_ya e_yd
            e_gt e_sc e_xt o_iota chunkv_out y_out q_pe q_act q_dve exp_ready scaled rows_in gn_chain""".split():
            S[name] = sem(name)
        landed = [sem(f"landed{i}") for i in range(RING)]

        eland = [sem(f"expert_landed{i}") for i in range(MRING)]

        pieces = []

        def piece(loads, sem_name, value):
            pieces.append((loads, sem_name, value))

        w_in = a["a_w_in"][0].rearrange("(k p) n -> p k n", p=P)
        for n in range(16):
            q = (n + 8) % 16
            piece([(lambda s: slot(s, "p (k n) -> p k n", k=DC), w_in[:, :, 256 * q:256 * q + 256])],
                  "z_ready", 2 * n + 2)
        w_ao = a["a_w_out"][0].rearrange("(k p) n -> p k n", p=P)
        for c in range(DC):
            piece([(lambda s: slot(s, "p (k n) -> p k n", k=AC), w_ao[:, :, P * c:P * c + P])],
                  "ao_ready", c + 1)
        w_g = a["f_w_gate"][0].rearrange("(k p) n -> p k n", p=P)
        w_u = a["f_w_up"][0].rearrange("(k p) n -> p k n", p=P)
        for q in range(11):
            for w, name in ((w_g, "ffg_ready"), (w_u, "ffu_ready")):
                piece([(lambda s: slot(s, "p (k n) -> p k n", k=DC), w[:, :, 256 * q:256 * q + 256])],
                      name, 2 * q + 2)
        w_d = a["f_w_down"][0].rearrange("(k p) n -> p k n", p=P)
        for c in range(DC):
            for hf in range(2):
                piece([(lambda s: slot(s, "p (k n) -> p k n", k=11, n=11 * P),
                        w_d[:, 11 * hf:11 * hf + 11, P * c:P * c + P])], "fd_ready", 2 * c + hf + 1)
        piece([(lambda s: slot(s, "p (k n) -> p k n", n=512, k=DC), a["b_w1"][0].rearrange("(k p) n -> p k n", p=P)),
               (lambda s: slot(s, "p (k n) -> p k n", n=512, off=512, k=DC),
                a["b_a1"][0].rearrange("(k p) n -> p k n", p=P))], "lo1_ready", 2)
        piece([(lambda s: slot(s, "p (k n) -> p k n", n=DC * LG, k=DC), a["b_g1"][0].rearrange("(k p) n -> p k n", p=P))],
              "lo1_ready", 3)
        piece([(lambda s: slot(s, None, parts=LW, n=D), a["b_w2"][0]),
               (lambda s: slot(s, None, parts=LW, n=D, off=D), a["b_a2"][0])], "lo2_ready", 16)
        for m, i in enumerate((1, 2, 0)):
            w = a["b_w_rkv"][0, i].rearrange("(k p) n -> p k n", p=P)
            for q in range(4):
                piece([(lambda s: slot(s, "p (k n) -> p k n", k=DC), w[:, :, 256 * q:256 * q + 256])],
                      "kvr_ready", 8 * m + 2 * q + 2)
        piece([(lambda s: slot(s, None, n=D), a["b_g2"][0, 0:P]),
               (lambda s: slot(s, None, parts=LG - P, n=D, off=D), a["b_g2"][0, P:LG])], "g_ready", DC)
        w = a["b_w_out"][0].rearrange("(k p) n -> p k n", p=P)
        for q in range(4):
            piece([(lambda s: slot(s, "p (k n) -> p k n", k=DC), w[:, :, 256 * q:256 * q + 256])],
                  "wo_ready", 2 * q + 2)
        sums, arrival = [0] * RING, []
        for n, (loads, _, _) in enumerate(pieces):
            sums[n % RING] += 16 * len(loads)
            arrival.append(sums[n % RING])
        A_IN, A_OUT, F_GU, F_D = 0, 16, 24, 46

        def norm_pe(k, sq):
            for c in range(DC):
                nc.tensor.wait_ge(S["sq_ready"], DC * k + c + 1)
                mm = nc.tensor.matmul(banks[6][:, 0:T], ones[:, :], sq[:, c, :],
                                      start=(c == 0), stop=(c == DC - 1))
            mm.then_inc(S["norm_sum"], 1)

        def norm_act(k, sq):
            for c in range(DC):
                nc.scalar.wait_ge(S["xt_ready"], DC * k + c + 1)
                nc.scalar.activation(sq[:, c, :], xT[:, c, :], ACT.Square).then_inc(S["sq_ready"], 1)
            nc.scalar.wait_ge(S["norm_sum"], k + 1)
            nc.scalar.activation(rt[:, :], banks[6][:, 0:T], ACT.Sqrt, bias=eps[:, 0:1],
                                 scale=1.0 / D).then_inc(S["rms_ready"], 1)

        def norm_dve(k, gain, dst):
            nc.vector.wait_ge(S["rms_ready"], k + 1)
            nc.vector.reciprocal(rinv[:, :], rt[:, :]).then_inc(S["rinv_ready"], 1)
            nc.vector.wait_ge(S["rinv_ready"], k + 1)
            for c in range(DC):
                nc.vector.scalar_tensor_tensor(
                    out=dst[:, c, :], in0=xT[:, c, :], scalar=vec[:, gain + c:gain + c + 1],
                    in1=rinv[:, :], op0=ALU.mult, op1=ALU.mult).then_inc(S["h_ready"], 1)

        steps = []
        q_steps = [(kind, p) for p in range(DC)
                   for kind in ("q_score", "q_s0", "q_x0", "q_qs", "q_t1", "q_x2", "q_w1", "q_u", "q_y", "q_st", "q_out")]
        q_at = [0]

        def gap():
            if q_at[0] < len(q_steps):
                steps.append(q_steps[q_at[0]])
                q_at[0] += 1

        u_ = 0
        for f in range(2):
            for i in range(2):
                steps.append(("score", u_, f, i))
                gap()
                steps.append(("x0", u_, f, i))
                gap()
                for m in range(1, 6):
                    steps.append(("t1", u_, m))
                    gap()
                    steps.append(("xl", u_, m))
                    gap()
                for c in (2 * i, 2 * i + 1):
                    steps.append(("w1", u_, f, i, c))
                    gap()
                    steps.append(("u", u_, f, i, c))
                    gap()
                    steps.append(("s", u_, f, i, c))
                    steps.append(("y", u_, f, i, c))
                    gap()
                u_ += 1
        while q_at[0] < len(q_steps):
            gap()

        def expert_load(sp, e, i, used=None):
            dst = slot(i % MRING, "p (k n) -> p k n", k=DC if i < 22 else 2)
            if i < 22:
                w = a["m_w_up" if i % 2 else "m_w_gate"][0, e].rearrange("(k p) n -> p k n", p=P)
                src = w[:, :, 256 * (i // 2):256 * (i // 2) + 256]
            else:
                src = a["m_w_down"][0].rearrange("e (r k p) n -> (e r) p k n", k=2, p=P)[e * 11 + (i - 22)]
            if used is not None:
                sp.wait_ge(S["e_piece"], used)
            sp.dma_start(dst, src).then_inc(eland[i % MRING], 16)

        Q_PE = ("q_score", "q_score", "q_s0t", "q_xtr", "q_qs", "q_t1", "q_xt2", "q_w1r", "q_u", "q_y", "q_st", "q_otr")
        Q_ACT = ("q_s0", "q_s0", "q_x", "q_w1t", "q_t1c", "q_w1", "q_uc", "q_yc", "q_oc", "q_oc")
        Q_DVE = ("q_ms", "q_ms", "q_xt0", "q_xt0", "q_xt2c", "q_stm", "q_stm", "q_send")

        def q_wait(eng, what, p, nth=0):
            for name, order in (("q_pe", Q_PE), ("q_act", Q_ACT), ("q_dve", Q_DVE)):
                if what in order:
                    eng.wait_ge(S[name], len(order) * p + order.index(what) + nth + 1)

        def hrows(h2):
            return slice(64 * h2, 64 * h2 + 64)

        def bc(ap, axis, shape):
            return ap.unsqueeze(axis).to_broadcast(shape)

        block = ctx.enter_context(nc.Block())

        @block.sync
        def _(sp):
            sp.dma_start(xtok[:, 0, :], a["x_prompt"][0, 0:128, :]).then_inc(S["x_in"], 16)
            sp.dma_start(xtok[:, 1, :], a["x_prompt"][0, 128:256, :]).then_inc(S["x_in"], 16)
            sp.dma_start(xtok[0:SMP, 2, :], a["x_sample"].rearrange("b t d -> (b t) d")).then_inc(S["x_in"], 16)
            def stream(lo, hi):
                for n in range(lo, hi):
                    if n >= RING:
                        _, name, value = pieces[n - RING]
                        sp.wait_ge(S[name], value)
                    for dst, src in pieces[n][0]:
                        sp.dma_start(dst(n % RING), src).then_inc(landed[n % RING], 16)

            stream(0, 24)
            sp.wait_ge(S["v_norm"], 3)
            sp.dma_start(out["chunk_v"].rearrange("a b t n -> (a b t) n"), vtok[0:SMP, 2, :]).then_inc(S["chunkv_out"], 16)
            stream(24, 65)
            sp.wait_ge(S["last_rows"], 2)
            sp.dma_start(out["shift_prompt"].rearrange("a b d -> (a b) d"), shrow[0:1, :]).then_inc(S["shift_out"], 16)
            sp.dma_start(out["shift_sample"].rearrange("a b d -> (a b) d"), shrow[1:1 + NB, :]).then_inc(S["shift_out"], 16)
            stream(65, len(pieces) - 1)
            for st in steps:
                if st[0] == "q_score":
                    p = st[1]
                    if p:
                        q_wait(sp, "q_st", p - 1)
                    else:
                        sp.wait_ge(S["tk_act"], 9)
                        sp.wait_ge(S["tk_dve"], 9)
                    for h2 in range(2):
                        sp.dma_start(nat[:, :, 64 * h2:64 * h2 + 64],
                                     a["state_wkv"][0, :, 2 * p + h2].rearrange("b i j -> i b j")).then_inc(S["nat_in"], 16)
                if st[0] == "q_out":
                    p = st[1]
                    q_wait(sp, "q_oc", p, 1)
                    for h2 in range(2):
                        sp.dma_start(out["wkv_sample"][0, :, 2 * p + h2].rearrange("b i j -> i b j"),
                                     Sout[:, :, 64 * h2:64 * h2 + 64]).then_inc(S["q_out"], 16)
            sp.wait_ge(S["st_row"], 2)
            for h2 in range(2):
                sp.dma_start(out["wkv_prompt"][0, 0].rearrange("(c h) i j -> h i c j", h=2)[h2],
                             wkvo[64 * h2:64 * h2 + 64, :, 64 * h2:64 * h2 + 64]).then_inc(S["st_out"], 16)
            stream(len(pieces) - 1, len(pieces))
            sp.wait_ge(S["wo_ready"], DC)
            sp.wait_ge(S["yg_ready"], DC)
            for i in range(MRING):
                expert_load(sp, 0, i)
            with sp.Fori(0, E_ - 1) as e:
                for i in range(MRING, EPIECES + MRING):
                    expert_load(sp, e + i // EPIECES, i % EPIECES, e * EPIECES + (i - MRING + 1))
            for i in range(MRING, EPIECES):
                expert_load(sp, E_ - 1, i, (E_ - 1) * EPIECES + i - MRING + 1)
            sp.wait_ge(S["r_most"], 2)
            with sp.If(sp.value_load(most_i[0:1, 0:1], min_val=0, max_val=T) > CAP):
                with sp.Fori(0, 2) as ps:
                    with sp.Fori(0, E_) as e:
                        for i in range(EPIECES):
                            expert_load(sp, e, i, (ps * E_ + e) * EPIECES + (E_ * EPIECES + i - MRING + 1))
            for n in range(6):
                sp.wait_ge(S["h_act" if n % 2 == 0 else "h_dve"], 3 + n // 2 + 1)
                i, q = n // 2, n % 2
                dst = out["y_sample"].rearrange("b t d -> (b t) d") if i == 2 else out["y_prompt"][0, P * i:P * i + P, :]
                sp.dma_start(dst[:, 512 * q:512 * q + 512], htok[0:TILES[i][1], i, 512 * q:512 * q + 512]) \
                    .then_inc(S["y_out"], 16)
            sp.wait_ge(S["chunkv_out"], 16)
            sp.wait_ge(S["shift_out"], 32)
            sp.wait_ge(S["q_out"], 16 * 2 * DC)
            sp.wait_ge(S["st_out"], 32)
            sp.wait_ge(S["y_out"], 16 * 6)

        @block.gpsimd
        def _(pool):
            g = nc.gpsimd
            count = [0]

            def step(ins):
                count[0] += 1
                ins.then_inc(S["pool_order"], 1)
                pool.wait_ge(S["pool_order"], count[0])

            step(g.memset(ident[:, :], 0.0))
            g.affine_select(out=ident[:, :], in_=ident[:, :], compare_op=ALU.not_equal, fill=1.0, base=0,
                            pattern=[[-1, P]], channel_multiplier=1).then_inc(S["const"], 1)
            g.memset(ones[:, :], 1.0).then_inc(S["const"], 1)
            g.memset(eps[:, 0:1], RMS_EPS).then_inc(S["const"], 1)
            g.memset(eps[:, 1:2], LN_EPS).then_inc(S["const"], 1)
            g.memset(eps[:, 2:3], GN_EPS).then_inc(S["const"], 1)
            step(g.memset(halves[:, :], 0.0))
            g.memset(halves[0:64, 0:64], 1.0).then_inc(S["const"], 1)
            g.memset(halves[64:128, 64:128], 1.0).then_inc(S["const"], 1)
            step(g.memset(wsS[0:SMP], 0.0))
            pool.wait_ge(S["ws_copied"], 2)
            g.affine_select(out=wsT, in_=wsT, compare_op=ALU.is_ge, fill=0.0, base=0,
                            pattern=[[0, G], [1, P]], channel_multiplier=-1).then_inc(S["ws_masked"], 1)
            pool.wait_ge(S["ws_masked"], 1)
            for b in range(NB):
                pool.dma_start(wsS[NS * b:NS * b + NS, :, NS * b:NS * b + NS],
                               wsT[0:NS, :, 0:NS]).then_inc(S["wsS_in"], 16)

            step(g.memset(lvl, 0.0))
            for l, m in enumerate(LEVELS):
                xs = lvl[:, l, 0, :].rearrange("p (n k s) -> p n k s", k=2, s=m)[:, :, 0, :]
                xt = lvl[:, l, 1, :].rearrange("p (n k s) -> p n k s", k=2, s=m)[:, :, 1, :]
                n = P // (2 * m)
                step(g.memset(xs, 1.0))
                step(g.memset(xt, 1.0))
                step(g.affine_select(out=xs, in_=xs, compare_op=ALU.is_ge, fill=0.0, base=-m,
                                     pattern=[[-2 * m, n], [0, m]], channel_multiplier=1))
                step(g.affine_select(out=xs, in_=xs, compare_op=ALU.is_ge, fill=0.0, base=2 * m - 1,
                                     pattern=[[2 * m, n], [0, m]], channel_multiplier=-1))
                step(g.affine_select(out=xt, in_=xt, compare_op=ALU.is_ge, fill=0.0, base=0,
                                     pattern=[[-2 * m, n], [0, m]], channel_multiplier=1))
                step(g.affine_select(out=xt, in_=xt, compare_op=ALU.is_ge, fill=0.0, base=m - 1,
                                     pattern=[[2 * m, n], [0, m]], channel_multiplier=-1))
            for msk, width, ch in ((mskA, P, CH), (mskS, SMP, NS)):
                step(g.memset(msk[:, 0:2, :], 1.0))
                step(g.memset(msk[:, 2:4, :], -1.0))
                v4 = msk.rearrange("p m (n s) -> p m n s", s=ch)
                for m in range(4):
                    step(g.affine_select(out=v4[:, m], in_=v4[:, m], compare_op=ALU.is_ge, fill=0.0,
                                         base=0, pattern=[[-ch, width // ch], [0, ch]], channel_multiplier=1))
                    step(g.affine_select(out=msk[:, m, :], in_=msk[:, m, :],
                                         compare_op=ALU.is_gt if m % 2 == 0 else ALU.is_ge, fill=0.0, base=0,
                                         pattern=[[1, width]], channel_multiplier=-1))
            step(g.memset(bmask, 1.0))
            step(g.affine_select(out=bmask, in_=bmask, compare_op=ALU.is_ge, fill=0.0, base=0,
                                 pattern=[[-NS, NB]], channel_multiplier=1))
            step(g.affine_select(out=bmask, in_=bmask, compare_op=ALU.is_ge, fill=0.0, base=NS - 1,
                                 pattern=[[NS, NB]], channel_multiplier=-1))
            step(g.memset(segm, 1.0))
            step(g.memset(segm[:, 0:NP_].rearrange("p (n s) -> p n s", s=CH)[:, :, 0:1], 0.0))
            step(g.memset(segm[:, NP_:T].rearrange("p (n s) -> p n s", s=NS)[:, :, 0:1], 0.0))
            g.memset(S0bd, 0.0).then_inc(S["masks"], 1)
            pool.wait_ge(S["shift_out"], 32)
            g.memset(Sbd, 0.0).then_inc(S["memz"], 1)
            g.memset(W1, 0.0).then_inc(S["memz"], 1)
            g.memset(Us, 0.0).then_inc(S["memz"], 1)
            for st in steps:
                if st[0] == "q_score":
                    p = st[1]
                    if p:
                        pool.wait_ge(S["q_out"], 16 * 2 * p)
                    else:
                        pool.wait_ge(S["tk_act"], 9)
                        pool.wait_ge(S["tk_dve"], 9)
                    for h2 in range(2):
                        vv = Vk[0:SMP, 2, P * p + 64 * h2:P * p + 64 * h2 + 64]
                        g.tensor_tensor(Vexp[:, h2], bc(vv, 1, [SMP, NB, HD]), bc(bmask, 2, [SMP, NB, HD]), ALU.mult) \
                            .then_inc(S["q_vx"], 1)
                if st[0] == "q_u":
                    p = st[1]
                    q_wait(pool, "q_uc", p)
                    for h2 in range(2):
                        uu = Uq[:, 64 * h2:64 * h2 + 64]
                        g.tensor_tensor(Uexp[:, h2], bc(uu, 1, [SMP, NB, HD]), bc(bmask, 2, [SMP, NB, HD]), ALU.mult) \
                            .then_inc(S["q_ux"], 1)

            pool.wait_ge(S["y_done"], 8)
            pool.wait_ge(S["st_tr"], 2)
            step(g.memset(tri, 1.0))
            step(g.affine_select(out=tri, in_=tri, compare_op=ALU.is_gt, fill=0.0, base=0,
                                 pattern=[[1, P]], channel_multiplier=-1))
            g.iota(slots_i, pattern=[[1, CAP]], base=0, channel_multiplier=0,
                   allow_small_or_imprecise_dtypes=True).then_inc(S["r_const"], 1)
            g.iota(exp_i, pattern=[[1, E_]], base=0, channel_multiplier=0,
                   allow_small_or_imprecise_dtypes=True).then_inc(S["r_const"], 1)
            g.memset(chosen, 0.0).then_inc(S["r_const"], 1)
            g.memset(place, 0.0).then_inc(S["r_const"], 1)

        @block.scalar
        def _(act):
            at = 0
            for name, n in VEC_ROWS:
                src = a[name]
                flat = {"b_mu": lambda: src.rearrange("a i (c p) -> (a i c) p", p=P),
                        "b_r_k": lambda: src.rearrange("a (c h) n -> (a c) (h n)", h=2),
                        "state_shift": lambda: src.rearrange("a b (c p) -> (a b c) p", p=P),
                        "norm_out_g": lambda: src.rearrange("(c p) -> c p", p=P)}.get(
                            name, lambda: src.rearrange("a (c p) -> (a c) p", p=P))()
                act.dma_start(vecrows[at % P:at % P + n, at // P, :], flat).then_inc(S["vec_in"], 16)
                at += n
            act.dma_start(wsraw, a["a_w_s"][0].rearrange("g t s -> t g s")).then_inc(S["ws_in"], 16)
            act.dma_start(lnG, a["a_ln_g"].to_broadcast([P, AW])).then_inc(S["rows_in"], 16)
            act.dma_start(lnB, a["a_ln_b"].to_broadcast([P, AW])).then_inc(S["rows_in"], 16)
            for i in range(2):
                act.dma_start(bsB[:, :, P * i:P * i + P],
                              a["a_b_s"].to_broadcast([P, G, P])).then_inc(S["rows_in"], 16)
            for b in range(NB):
                t0 = NP_ + NS * b
                act.dma_start(bsB[:, :, t0:t0 + NS],
                              a["a_b_s"][:, :, 0:NS].to_broadcast([P, G, NS])).then_inc(S["rows_in"], 16)
            act.dma_start(router, a["m_router"][0].rearrange("(k p) e -> p k e", p=P)).then_inc(S["router_in"], 16)
            act.wait_ge(S["const"], 7)
            norm_act(0, tokens(B[2]))
            for g_ in range(32):
                act.wait_ge(S["z_ready"], g_ + 1)
                c = (g_ + 16) % 32
                dst = uT[:, c, :] if c < 16 else vT[:, c - 16, :]
                nc.scalar.activation(dst, banks[g_ % 4][:, 0:T], ACT.Gelu,
                                     bias=vcol("a_b_in", c)).then_inc(S["gelu_done"], 1)
                if g_ == 20:
                    act.wait_ge(S["v_aggr"], 3)
                    for i, (_, n) in enumerate(TILES):
                        nc.scalar.activation(lnrs[0:n, i, 0:1], lnmv[0:n, i, 1:2], ACT.Sqrt,
                                             bias=eps[0:n, 1:2]).then_inc(S["v_std"], 1)
            norm_act(1, tokens(B[2]))
            for q in range(11):
                for j in range(2):
                    n = 2 * q + j
                    act.wait_ge(S["ffg_ready"], n + 1)
                    if n >= 4:
                        act.wait_ge(S["hf_ready"], n - 3)
                    nc.scalar.activation(sgF[:, n % 4, :], banks[j][:, 0:T], ACT.Silu).then_inc(S["sg_ready"], 1)
            norm_act(2, tokens(B[2]))
            s_ = nc.scalar
            for hf in range(2):
                act.wait_ge(S["last_tr"], hf + 1)
                s_.activation(shrow[:, 512 * hf:512 * hf + 512], banks[4 + hf][0:1 + NB, :], ACT.Copy) \
                    .then_inc(S["last_rows"], 1)
            act.wait_ge(S["lo1_ready"], 1)
            s_.activation(lw1, banks[0][0:LW, 0:T], ACT.Tanh).then_inc(S["lo1_done"], 1)
            act.wait_ge(S["lo1_ready"], 2)
            s_.activation(la1, banks[1][0:LW, 0:T], ACT.Copy).then_inc(S["lo1_done"], 1)
            act.wait_ge(S["lo1_ready"], 3)
            s_.activation(lg1[:, 0, :], banks[2][:, 0:T], ACT.Sigmoid).then_inc(S["lo1_done"], 1)
            s_.activation(lg1[0:LG - P, 1, :], banks[3][0:LG - P, 0:T], ACT.Sigmoid).then_inc(S["lo1_done"], 1)
            for n in range(16):
                act.wait_ge(S["lo2_ready"], n + 1)
                dst, name = (dT, "b_w0") if n < 8 else (aT, "b_a0")
                s_.activation(dst[:, n % 8, :], banks[4 + n % 4][:, 0:T], ACT.Sigmoid, bias=vcol(name, n % 8)) \
                    .then_inc(S["lo2_done"], 1)
            for n in range(24):
                act.wait_ge(S["kvr_ready"], n + 1)
                dst = (kT[:, n % 8, :], vfT[:, n % 8, :], QR[:, n % 8, 1, :])[n // 8]
                s_.activation(dst, banks[n % 4][:, 0:T], ACT.Copy).then_inc(S["kvr_done"], 1)
                if n == 15:
                    for c in range(DC):
                        act.wait_ge(S["kk_raw"], c + 1)
                        s_.activation(kkT[:, c, :], QR[:, c, 0, :], ACT.Square).then_inc(S["kk_sq"], 1)
            for c in range(DC):
                act.wait_ge(S["kn_ready"], c + 1)
                s_.activation(kkT[:, c, :], banks[4 + c % 4][:, 0:T], ACT.Sqrt).then_inc(S["kn_root"], 1)
            act.wait_ge(S["scan_ready"], DC + 1)
            act.wait_ge(S["rb_ready"], DC)
            s_.activation(rkT, t1T, ACT.Exp, scale=-DECAY).then_inc(S["exp_ready"], 1)
            s_.activation(dT, dT, ACT.Exp, scale=-DECAY).then_inc(S["exp_ready"], 1)
            act.wait_ge(S["exp_ready"], 1)
            s_.activation(t1T, t1T, ACT.Exp, scale=DECAY).then_inc(S["exp_ready"], 1)
            for n in range(0, 18, 2):
                act.wait_ge(S["tk_tr"], n + 1)
                m, i, q = n // 6, n % 6 // 2, n % 2
                rows = TILES[i][1]
                s_.activation(tok[0:rows, m, i, 512 * q:512 * q + 512], banks[n % 4][0:rows, :], ACT.Copy) \
                    .then_inc(S["tk_act"], 1)
            for st in steps:
                k = st[0]
                if k == "x0":
                    u = st[1]
                    for b in range(2):
                        act.wait_ge(S["xt_tr"], 2 * u + b + 1)
                        s_.activation(XX[:, 4 * b:4 * b + 4, 0, :], banks[b][:, :].rearrange("p (h t) -> p h t", h=4),
                                      ACT.Copy).then_inc(S["x0_ready"], 1)
                elif k == "t1":
                    n = 5 * st[1] + st[2] - 1
                    for b in range(2):
                        act.wait_ge(S["t1_ready"], 2 * n + b + 1)
                        s_.activation(T1[:, b], banks[b][:, :].rearrange("p (h t) -> p h t", h=4), ACT.Copy) \
                            .then_inc(S["t1_done"], 1)
                elif k == "w1":
                    _, u, f, i, c = st
                    n, tb = 4 * f + c, 64 * (c % 2)
                    act.wait_ge(S["w1_ready"], n + 1)
                    s_.activation(W1[tb:tb + 64, :], banks[0][tb:tb + 64, :], ACT.Copy).then_inc(S["w1_done"], 1)
                elif k == "y":
                    _, u, f, i, c = st
                    n = 4 * f + c
                    act.wait_ge(S["y_ready"], n + 1)
                    s_.activation(yT[:, 4 * f:4 * f + 4, CH * c:CH * c + CH],
                                  banks[3 + c % 2][:, 0:4 * CH].rearrange("p (c t) -> p c t", c=4), ACT.Copy) \
                        .then_inc(S["y_done"], 1)
                elif k == "q_s0":
                    p = st[1]
                    q_wait(act, "q_s0t", p)
                    if p == 0:
                        act.wait_ge(S["masks"], 1)
                    else:
                        q_wait(act, "q_send", p - 1)
                    for h2 in range(2):
                        s_.activation(S0bd[hrows(h2), :, 64 * h2:64 * h2 + 64],
                                      banks[6][hrows(h2), :].rearrange("p (b i) -> p b i", b=NB), ACT.Copy) \
                            .then_inc(S["q_act"], 1)
                elif k == "q_x0":
                    p = st[1]
                    q_wait(act, "q_xtr", p)
                    s_.activation(XXq[:, :, 0, :], banks[7][0:SMP, 0:64].rearrange("p (h t) -> p h t", h=2), ACT.Copy) \
                        .then_inc(S["q_act"], 1)
                elif k == "q_qs":
                    p = st[1]
                    q_wait(act, "q_qs", p)
                    s_.activation(W1Tq, banks[6][:, 0:SMP], ACT.Copy).then_inc(S["q_act"], 1)
                elif k == "q_t1":
                    p = st[1]
                    q_wait(act, "q_t1", p)
                    s_.activation(T1q, banks[7][0:SMP, 0:64].rearrange("p (h t) -> p h t", h=2), ACT.Copy) \
                        .then_inc(S["q_act"], 1)
                elif k == "q_w1":
                    p = st[1]
                    q_wait(act, "q_w1r", p)
                    s_.activation(W1q, banks[7][0:SMP, 0:P], ACT.Copy).then_inc(S["q_act"], 1)
                elif k == "q_u":
                    p = st[1]
                    q_wait(act, "q_u", p)
                    s_.activation(Uq, banks[7][0:SMP, 0:P], ACT.Copy).then_inc(S["q_act"], 1)
                elif k == "q_y":
                    p = st[1]
                    q_wait(act, "q_y", p)
                    s_.activation(yT[:, p, NP_:T], banks[6][:, SMP:2 * SMP], ACT.Copy).then_inc(S["q_act"], 1)
                elif k == "q_out":
                    p = st[1]
                    q_wait(act, "q_otr", p)
                    for hf in range(2):
                        s_.activation(Sout[:, 4 * hf:4 * hf + 4, :],
                                      banks[6 + hf][0:HD, :].rearrange("p (b j) -> p b j", b=4), ACT.Copy) \
                            .then_inc(S["q_act"], 1)
            for hf in range(2):
                act.wait_ge(S["st_tr"], hf + 1)
                s_.activation(wkvo[:, 4 * hf:4 * hf + 4, :], banks[hf][:, :].rearrange("p (c j) -> p c j", c=4), ACT.Copy) \
                    .then_inc(S["st_row"], 1)
            for c in range(DC):
                act.wait_ge(S["gn_yc"], c + 1)
                s_.activation(rkT[:, c, :], yT[:, c, :], ACT.Square).then_inc(S["gn_sq"], 1)
            act.wait_ge(S["st_out"], 32)
            for c in range(DC):
                act.wait_ge(S["gn_var"], c + 1)
                s_.activation(t1T[:, c, :], banks[4 + c % 2][:, 0:T], ACT.Sqrt, bias=eps[:, 2:3], scale=1.0 / HD) \
                    .then_inc(S["gn_root"], 1)
            act.wait_ge(S["q_out"], 16 * 2 * DC)
            norm_act(3, tokens(B[9]))
            for n in range(0, 6, 2):
                act.wait_ge(S["h_tr"], n + 1)
                i, q = n // 2, n % 2
                rows = TILES[i][1]
                s_.activation(htok[0:rows, i, 512 * q:512 * q + 512], banks[2 + n % 4][0:rows, :], ACT.Copy) \
                    .then_inc(S["h_act"], 1)
            act.wait_ge(S["r_e"], 3)
            for i, (_, n) in enumerate(TILES):
                s_.activation(wts[0:n, i, 1:2], wts[0:n, i, 0:1], ACT.Exp).then_inc(S["r_exp"], 1)

            def e_gather(n):
                act.wait_ge(S["e_xg"], 2 * n + 1)
                s_.activation(xgE[:, 0:4, :], banks[6][:, 0:4 * CAP].rearrange("p (c s) -> p c s", c=4), ACT.Copy) \
                    .then_inc(S["e_xga"], 1)

            def e_gate(n, q):
                act.wait_ge(S["e_piece"], n * EPIECES + (2 * q + 1))
                if q >= 2:
                    act.wait_ge(S["e_he"], n * 11 + (q - 1))
                s_.activation(sgE[:, q % 2], banks[q % 2][:, 0:2 * CAP].rearrange("p (j s) -> p j s", j=2), ACT.Silu) \
                    .then_inc(S["e_sg"], 1)

            def e_down(n):
                act.wait_ge(S["e_piece"], (n + 1) * EPIECES)
                s_.activation(yE[:, 0:4, :], banks[4][:, 0:4 * CAP].rearrange("p (c s) -> p c s", c=4), ACT.Copy) \
                    .then_inc(S["e_yta"], 1)

            def e_tail(n):
                act.wait_ge(S["e_ytr"], 2 * n + 1)
                s_.activation(yS[:, 0:512], banks[6][0:CAP, :], ACT.Copy).then_inc(S["e_ya"], 1)
                act.wait_ge(S["e_gtr"], n + 1)
                s_.activation(GT, banks[4][0:CAP, 0:T], ACT.Copy).then_inc(S["e_gt"], 1)

            def e_body(n, prev):
                e_gather(n)
                for q in range(11):
                    e_gate(n, q)
                    if q == 1 and prev is not None:
                        e_tail(prev)
                e_down(n)

            e_body(0, None)
            with act.Fori(1, E_) as e:
                e_body(e, e - 1)
            e_tail(E_ - 1)
            with act.If(act.value_load(most_i[0:1, 0:1], min_val=0, max_val=T) > CAP):
                with act.Fori(0, 2) as ps:
                    with act.Fori(0, E_) as e:
                        n = ps * E_ + e + E_
                        e_body(n, None)
                        e_tail(n)
                act.wait_ge(S["e_xt"], DC * 3 * E_)
            sq = tokens(B[9])
            for c in range(DC):
                act.wait_ge(S["e_xt"], DC * (E_ - 1) + c + 1)
                s_.activation(sq[:, c, :], xT[:, c, :], ACT.Square).then_inc(S["sq_ready"], 1)
            act.wait_ge(S["norm_sum"], 5)
            s_.activation(rt[:, :], banks[0][:, 0:T], ACT.Sqrt, bias=eps[:, 0:1], scale=1.0 / D).then_inc(S["rms_ready"], 1)
            for n in range(0, 6, 2):
                act.wait_ge(S["h_tr"], 6 + n + 1)
                i, q = n // 2, n % 2
                rows = TILES[i][1]
                s_.activation(htok[0:rows, i, 512 * q:512 * q + 512], banks[2 + n % 4][0:rows, :], ACT.Copy) \
                    .then_inc(S["h_act"], 1)

        @block.vector
        def _(dve):
            v = nc.vector
            v_tr = S["vec_tr"]
            dve.wait_ge(v_tr, 1)
            v.tensor_copy(vec[:, 0:VEC_N], banks[7][:, 0:VEC_N]).then_inc(S["vec_ready"], 1)
            for c in range(DC):
                dve.wait_ge(S["tr_ready"], c + 1)
                v.tensor_copy(xT[:, c, :], banks[c % 2][:, 0:T]).then_inc(S["xt_ready"], 1)
            for hf in range(2):
                dve.wait_ge(S["ws_tr"], hf + 1)
                v.tensor_copy(wsT[:, 4 * hf:4 * hf + 4, :], banks[4 + hf][:, :].rearrange("p (g t) -> p g t", g=4)) \
                    .then_inc(S["ws_copied"], 1)
            dve.wait_ge(S["vec_ready"], 1)
            v.tensor_scalar(omka[:, :], vec[:, col["b_k_a"]:col["b_k_a"] + DC], -1.0, 1.0, ALU.mult, ALU.add) \
                .then_inc(S["omka_ready"], 1)
            norm_dve(0, col["norm_mix_g"], hT)
            tb = (4, 5, 7)
            for q in range(4):
                dve.wait_ge(S["v_tr"], q + 1)
                for i, (_, n) in enumerate(TILES):
                    v.tensor_copy(vtok[0:n, i, 512 * q:512 * q + 512], banks[tb[i]][0:n, :])
                    v.bn_stats(lnst[0:n, i, q, :], banks[tb[i]][0:n, :]).then_inc(S["v_evac"], 1)
            dve.wait_ge(S["v_evac"], 12)
            for i, (_, n) in enumerate(TILES):
                v.bn_aggr(lnmv[0:n, i, :], lnst[0:n, i].rearrange("p q s -> p (q s)")).then_inc(S["v_aggr"], 1)
            dve.wait_ge(S["v_std"], 3)
            for i, (_, n) in enumerate(TILES):
                v.reciprocal(lnrs[0:n, i, 1:2], lnrs[0:n, i, 0:1]).then_inc(S["v_rstd"], 1)
            dve.wait_ge(S["rows_in"], 16 * (4 + NB))
            for i, (_, n) in enumerate(TILES):
                v.scalar_tensor_tensor(out=vtok[0:n, i, :], in0=vtok[0:n, i, :], scalar=lnmv[0:n, i, 0:1],
                                       in1=lnG[0:n, :], op0=ALU.subtract, op1=ALU.mult).then_inc(S["v_rstd"], 1)
                dve.wait_ge(S["v_rstd"], 4 + i)
                v.scalar_tensor_tensor(out=vtok[0:n, i, :], in0=vtok[0:n, i, :], scalar=lnrs[0:n, i, 1:2],
                                       in1=lnB[0:n, :], op0=ALU.mult, op1=ALU.add).then_inc(S["v_norm"], 1)
            dve.wait_ge(S["gelu_done"], 32)
            for c in range(AC):
                dve.wait_ge(S["mix_ready"], c + 1)
                v.tensor_tensor(mixT[:, c % 8, :], banks[c % 4][:, 0:T], bsB[:, c // 2, :], ALU.add) \
                    .then_inc(S["mix_add"], 1)
                if c:
                    dve.wait_ge(S["mix_add"], c)
                    v.tensor_tensor(vT[:, c - 1, :], mixT[:, (c - 1) % 8, :], uT[:, c - 1, :], ALU.mult) \
                        .then_inc(S["mix_done"], 1)
            dve.wait_ge(S["mix_add"], AC)
            v.tensor_tensor(vT[:, AC - 1, :], mixT[:, 7, :], uT[:, AC - 1, :], ALU.mult).then_inc(S["mix_done"], 1)
            for c in range(DC):
                dve.wait_ge(S["ao_ready"], c + 1)
                v.tensor_tensor(xT[:, c, :], banks[c % 4][:, 0:T], xT[:, c, :], ALU.add).then_inc(S["xt_ready"], 1)
            norm_dve(1, col["norm_ffn_g"], hT)
            for q in range(11):
                for j in range(2):
                    n = 2 * q + j
                    dve.wait_ge(S["ffu_ready"], n + 1)
                    dve.wait_ge(S["sg_ready"], n + 1)
                    v.tensor_tensor(hF[:, n, :], banks[2 + j][:, 0:T], sgF[:, n % 4, :], ALU.mult) \
                        .then_inc(S["hf_ready"], 1)
            for c in range(DC):
                dve.wait_ge(S["fd_ready"], 2 * c + 2)
                v.tensor_tensor(xT[:, c, :], banks[c % 4][:, 0:T], xT[:, c, :], ALU.add).then_inc(S["xt_ready"], 1)
            norm_dve(2, col["norm_mix_g"] + 8, hT)
            dve.wait_ge(S["h_ready"], 3 * DC)
            dve.wait_ge(S["mix_done"], AC)
            hs = hT[:, :, NP_:T].rearrange("p c (b s) -> p c b s", s=NS)
            xs = xxT[:, :, NP_:T].rearrange("p c (b s) -> p c b s", s=NS)
            v.tensor_copy(lastc[:, :, 0:1], hT[:, :, NP_ - 1:NP_]).then_inc(S["last_cols"], 1)
            v.tensor_copy(lastc[:, :, 1:1 + NB], hs[:, :, :, NS - 1]).then_inc(S["last_cols"], 1)
            v.tensor_tensor(xxT[:, :, 1:NP_], hT[:, :, 0:NP_ - 1], hT[:, :, 1:NP_], ALU.subtract).then_inc(S["xx_ready"], 1)
            v.tensor_scalar(xxT[:, :, 0:1], hT[:, :, 0:1], -1.0, None, ALU.mult).then_inc(S["xx_ready"], 1)
            v.tensor_tensor(xs[:, :, :, 1:NS], hs[:, :, :, 0:NS - 1], hs[:, :, :, 1:NS], ALU.subtract) \
                .then_inc(S["xx_ready"], 1)
            shift = vec[:, col["state_shift"]:col["state_shift"] + 64].rearrange("p (b c) -> p c b", c=DC)
            v.tensor_tensor(xs[:, :, :, 0], shift, hs[:, :, :, 0], ALU.subtract).then_inc(S["xx_ready"], 1)
            dve.wait_ge(S["xx_ready"], 4)
            free_after = (None, None, ("lo1_ready", 1), ("lo1_ready", 2), ("lo1_ready", 3), ("kvr_ready", 8))
            for n, i in enumerate((3, 4, 5, 1, 2, 0)):
                if free_after[n]:
                    dve.wait_ge(S[free_after[n][0]], free_after[n][1])
                for c in range(DC):
                    v.scalar_tensor_tensor(out=mixbuf[n % 2][:, c, :], in0=xxT[:, c, :], scalar=vcol("b_mu", 8 * i + c),
                                           in1=hT[:, c, :], op0=ALU.mult, op1=ALU.add).then_inc(S["mx_ready"], 1)
            dve.wait_ge(S["kvr_done"], DC)
            for c in range(DC):
                v.tensor_scalar(QR[:, c, 0, :], kT[:, c, :], vcol("b_k_k", c), None, ALU.mult).then_inc(S["kk_raw"], 1)
            dve.wait_ge(S["lo2_done"], 16)
            dve.wait_ge(S["mx_ready"], 48)
            for c in range(DC):
                v.tensor_scalar(t1T[:, c, :], aT[:, c, :], vcol("b_k_a", c), omka[:, c:c + 1], ALU.mult, ALU.add) \
                    .then_inc(S["kk_chain"], 1)
            dve.wait_ge(S["kk_chain"], DC)
            v.tensor_tensor(kT, kT, t1T, ALU.mult).then_inc(S["kk_chain"], 1)
            dve.wait_ge(S["kk_chain"], DC + 1)
            dve.wait_ge(S["masks"], 1)
            for c in range(DC):
                v.tensor_tensor_scan(out=t1T[:, c, :], data0=segm, data1=dT[:, c, :], initial=0.0,
                                     op0=ALU.mult, op1=ALU.add).then_inc(S["scan_ready"], 1)
            dve.wait_ge(S["scan_ready"], DC)
            v.tensor_tensor(dT, t1T, dT, ALU.subtract).then_inc(S["scan_ready"], 1)
            dve.wait_ge(S["kn_root"], DC)
            v.tensor_scalar(kkT, kkT, 1e-12, None, ALU.max).then_inc(S["kk_chain"], 1)
            dve.wait_ge(S["kk_chain"], DC + 2)
            v.reciprocal(kkT, kkT).then_inc(S["kk_chain"], 1)
            dve.wait_ge(S["kk_chain"], DC + 3)
            v.tensor_tensor(QR[:, :, 0, :], QR[:, :, 0, :], kkT, ALU.mult).then_inc(S["kk_chain"], 1)
            dve.wait_ge(S["kk_chain"], DC + 4)
            v.tensor_tensor(aT, QR[:, :, 0, :], aT, ALU.mult).then_inc(S["kk_chain"], 1)
            dve.wait_ge(S["kvr_done"], 24)
            for c in range(DC):
                v.scalar_tensor_tensor(out=rkT[:, c, :], in0=QR[:, c, 1, :], scalar=vcol("b_r_k", c), in1=kT[:, c, :],
                                       op0=ALU.mult, op1=ALU.mult).then_inc(S["rk_ready"], 1)
            for c in range(DC):
                dve.wait_ge(S["rb_ready"], c + 1)
                v.tensor_tensor(bonT[:, c, :], banks[4 + c % 4][:, 0:T], vfT[:, c, :], ALU.mult).then_inc(S["bon_ready"], 1)
            dve.wait_ge(S["exp_ready"], 1)
            v.tensor_copy(pc[:, :, 0:4], rkT[:, :, CH - 1:NP_:CH]).then_inc(S["pc_ready"], 1)
            v.tensor_copy(pc[:, :, 4:12], rkT[:, :, NP_ + NS - 1:T:NS]).then_inc(S["pc_ready"], 1)
            v.tensor_tensor(QR[:, :, 1, :], QR[:, :, 1, :], rkT, ALU.mult).then_inc(S["scaled"], 1)
            dve.wait_ge(S["pc_ready"], 2)
            v.tensor_scalar(pcn, pc, -1.0, None, ALU.mult).then_inc(S["pc_ready"], 1)
            dve.wait_ge(S["exp_ready"], 2)
            v.tensor_tensor(QR[:, :, 0, :], QR[:, :, 0, :], dT, ALU.mult).then_inc(S["scaled"], 1)
            dve.wait_ge(S["exp_ready"], 3)
            v.tensor_tensor(kT, kT, t1T, ALU.mult).then_inc(S["scaled"], 1)
            v.tensor_tensor(aT, aT, t1T, ALU.mult).then_inc(S["scaled"], 1)
            dve.wait_ge(S["scaled"], 4)
            dve.wait_ge(S["pc_ready"], 3)
            for src, dst, pe_ in ((kT, KtT, pc), (aT, BtT, pcn)):
                for lo, hi, s0, n, w in ((0, NP_, 0, 4, CH), (NP_, T, 4, NB, NS)):
                    v.tensor_tensor(dst[:, :, lo:hi].rearrange("p c (n s) -> p c n s", n=n),
                                    src[:, :, lo:hi].rearrange("p c (n s) -> p c n s", n=n),
                                    bc(pe_[:, :, s0:s0 + n], 3, [P, DC, n, w]), ALU.mult).then_inc(S["scaled"], 1)
            for n in range(1, 18, 2):
                dve.wait_ge(S["tk_tr"], n + 1)
                m, i, q = n // 6, n % 6 // 2, n % 2
                rows = TILES[i][1]
                v.tensor_copy(tok[0:rows, m, i, 512 * q:512 * q + 512], banks[n % 4][0:rows, :]).then_inc(S["tk_dve"], 1)
            for st in steps:
                k = st[0]
                if k == "score":
                    _, u, f, i = st
                    for hh in range(8):
                        dve.wait_ge(S["sc_ready"], 8 * u + hh + 1)
                        v.tensor_tensor(MS[:, hh], banks[hh % 6][:, :].rearrange("p (m t) -> p m t", m=4), mskA, ALU.mult) \
                            .then_inc(S["ms_ready"], 1)
                elif k == "x0":
                    u = st[1]
                    v.tensor_copy(XX[:, :, 1, :], bc(ident[:, :], 1, [P, 8, P])).then_inc(S["xt0_ready"], 1)
                    dve.wait_ge(S["xt0_ready"], 2 * u + 1)
                    dve.wait_ge(S["ms_ready"], 8 * u + 8)
                    v.copy_predicated(XX[:, :, 1, :], bc(lvl[:, 0, 1, :], 1, [P, 8, P]).bitcast(I32), MS[:, :, BL, :]) \
                        .then_inc(S["xt0_ready"], 1)
                elif k == "xl":
                    _, u, m = st
                    n = 5 * u + m - 1
                    for b in range(2):
                        for j in range(2):
                            dve.wait_ge(S["x_ready"], 4 * n + 2 * b + j + 1)
                            hh = 4 * b + 2 * j
                            v.copy_predicated(XX[:, hh:hh + 2], bc(lvl[:, m], 1, [P, 2, 2, P]).bitcast(I32),
                                              banks[2 + 2 * b + j][:, :].rearrange("p (h x t) -> p h x t", h=2, x=2)) \
                                .then_inc(S["x_done"], 1)
                elif k == "u":
                    _, u, f, i, c = st
                    n, tb = 4 * f + c, 64 * (c % 2)
                    dve.wait_ge(S["u_ready"], n + 1)
                    v.tensor_copy(Us[tb:tb + 64, :], banks[1][tb:tb + 64, :]).then_inc(S["u_done"], 1)
                    for h2 in range(2):
                        hr, hc = hrows(h2), slice(64 * h2, 64 * h2 + 64)
                        v.tensor_tensor(Sbd[hr, (c + 1) % 2, 4 * f:4 * f + 4, hc], Sbd[hr, c % 2, 4 * f:4 * f + 4, hc],
                                        bc(pc[hr, 4 * f:4 * f + 4, c], 2, [64, 4, 64]), ALU.mult).then_inc(S["s_scaled"], 1)
                elif k == "s":
                    _, u, f, i, c = st
                    n = 4 * f + c
                    dve.wait_ge(S["s_ready"], n + 1)
                    dve.wait_ge(S["s_scaled"], 2 * n + 2)
                    for h2 in range(2):
                        hr, hc = hrows(h2), slice(64 * h2, 64 * h2 + 64)
                        so = Sbd[hr, (c + 1) % 2, 4 * f:4 * f + 4, hc]
                        v.tensor_tensor(so, banks[2][:, :].rearrange("p (c i) -> p c i", c=4)[hr, :, hc], so, ALU.add) \
                            .then_inc(S["s_done"], 1)
                elif k == "q_score":
                    p = st[1]
                    for h2 in range(2):
                        q_wait(dve, "q_score", p, h2)
                        v.tensor_tensor(MSq[:, h2], banks[6 + h2][0:SMP, 0:P].rearrange("p (m t) -> p m t", m=4), mskS,
                                        ALU.mult).then_inc(S["q_dve"], 1)
                    v.tensor_copy(XXq[:, :, 1, :], bc(ident[0:SMP, 0:SMP], 1, [SMP, 2, SMP])).then_inc(S["q_dve"], 1)
                    q_wait(dve, "q_xt0", p)
                    q_wait(dve, "q_ms", p, 1)
                    v.copy_predicated(XXq[:, :, 1, :], bc(lvl[0:SMP, 0, 1, 0:SMP], 1, [SMP, 2, SMP]).bitcast(I32),
                                      MSq[:, :, BL, :]).then_inc(S["q_dve"], 1)
                elif k == "q_x2":
                    p = st[1]
                    q_wait(dve, "q_xt2", p)
                    v.copy_predicated(XXq[:, :, 1, :], bc(lvl[0:SMP, 1, 1, 0:SMP], 1, [SMP, 2, SMP]).bitcast(I32),
                                      banks[7][0:SMP, 0:64].rearrange("p (h t) -> p h t", h=2)).then_inc(S["q_dve"], 1)
                elif k == "q_st":
                    p = st[1]
                    if p:
                        q_wait(dve, "q_otr", p - 1)
                    q_wait(dve, "q_s0", p, 1)
                    for h2 in range(2):
                        hr, hc = hrows(h2), slice(64 * h2, 64 * h2 + 64)
                        v.tensor_tensor(Send[hr], S0bd[hr, :, hc], bc(pc[hr, p, 4:12], 2, [64, NB, 64]), ALU.mult) \
                            .then_inc(S["q_dve"], 1)
                    q_wait(dve, "q_st", p)
                    q_wait(dve, "q_stm", p, 1)
                    v.tensor_tensor(Send, banks[7][:, :].rearrange("p (b i) -> p b i", b=NB), Send, ALU.add) \
                        .then_inc(S["q_dve"], 1)
            for c in range(DC):
                dve.wait_ge(S["gn_mean"], c + 1)
                v.scalar_tensor_tensor(out=yT[:, c, :], in0=banks[2 + c % 2][:, 0:T], scalar=-1.0 / HD, in1=yT[:, c, :],
                                       op0=ALU.mult, op1=ALU.add).then_inc(S["gn_yc"], 1)
            for c in range(DC):
                dve.wait_ge(S["gn_root"], c + 1)
                v.reciprocal(t1T[:, c, :], t1T[:, c, :]).then_inc(S["gn_chain"], 1)
                dve.wait_ge(S["gn_chain"], 3 * c + 1)
                v.scalar_tensor_tensor(out=yT[:, c, :], in0=yT[:, c, :], scalar=vcol("b_lnx_g", c), in1=t1T[:, c, :],
                                       op0=ALU.mult, op1=ALU.mult).then_inc(S["gn_chain"], 1)
                dve.wait_ge(S["gn_chain"], 3 * c + 2)
                v.scalar_tensor_tensor(out=yT[:, c, :], in0=yT[:, c, :], scalar=vcol("b_lnx_b", c), in1=bonT[:, c, :],
                                       op0=ALU.add, op1=ALU.add).then_inc(S["gn_chain"], 1)
                dve.wait_ge(S["gn_chain"], 3 * c + 3)
                dve.wait_ge(S["g_ready"], c + 1)
                v.tensor_tensor(yT[:, c, :], banks[6 + c % 2][:, 0:T], yT[:, c, :], ALU.mult).then_inc(S["yg_ready"], 1)
            for c in range(DC):
                dve.wait_ge(S["wo_ready"], c + 1)
                v.tensor_tensor(xT[:, c, :], banks[c % 4][:, 0:T], xT[:, c, :], ALU.add).then_inc(S["xt_ready"], 1)
            norm_dve(3, col["norm_ffn_g"] + 8, tokens(B[8]))
            chain = [0]

            def link(ins):
                chain[0] += 1
                ins.then_inc(S["r_chain"], 1)
                dve.wait_ge(S["r_chain"], chain[0])

            dve.wait_ge(S["r_const"], 4)
            for i, (_, n) in enumerate(TILES):
                dve.wait_ge(S["r_logit"], 3)
                link(v.tensor_copy(logit[0:n, i, 0:8], banks[i // 2][0:n, 8 * i:8 * i + 8]))
                link(v.max(out=top[0:n, i, 0:8], in_=logit[0:n, i, 0:8]))
                v.tensor_tensor(wts[0:n, i, 0:1], top[0:n, i, 1:2], top[0:n, i, 0:1], ALU.subtract).then_inc(S["r_e"], 1)
                link(v.max_index(out=topi[0:n, i, 0:8], in_max=top[0:n, i, 0:8], in_values=logit[0:n, i, 0:8]))
                link(v.tensor_copy(topf[0:n, i, 0:2], topi[0:n, i, 0:2]))
                link(v.tensor_scalar(oh1[0:n, i, 0:8], exp_i[0:n, :], topf[0:n, i, 0:1], None, ALU.is_equal))
                v.scalar_tensor_tensor(out=chosen[0:n, i, 0:8], in0=exp_i[0:n, :], scalar=topf[0:n, i, 1:2],
                                       in1=oh1[0:n, i, 0:8], op0=ALU.is_equal, op1=ALU.add).then_inc(S["r_sel"], 1)
            for n in range(1, 6, 2):
                dve.wait_ge(S["h_tr"], n + 1)
                i, q = n // 2, n % 2
                rows = TILES[i][1]
                v.tensor_copy(htok[0:rows, i, 512 * q:512 * q + 512], banks[2 + n % 4][0:rows, :]).then_inc(S["h_dve"], 1)
            dve.wait_ge(S["r_pos"], 1)
            for i, (_, n) in enumerate(TILES):
                link(v.tensor_copy(place[0:n, i, 0:8], banks[1][0:n, 32 + 8 * i:40 + 8 * i]))
            v.reduce_max(most[:, 0:1], banks[1][:, 64:72], AX_X).then_inc(S["r_most"], 1)
            dve.wait_ge(S["r_most"], 1)
            v.tensor_copy(most_i, most[:, 0:1]).then_inc(S["r_most"], 1)

            def e_slots(e):
                for i, (_, n) in enumerate(TILES):
                    v.tensor_scalar(Sx[0:n, i, :], slots_i[0:n, :], place[0:n, i, bass.ds(e, 1)],
                                    chosen[0:n, i, bass.ds(e, 1)], ALU.is_equal, ALU.mult).then_inc(S["e_sx"], 1)

            def e_gates(e):
                for i, (_, n) in enumerate(TILES):
                    v.tensor_scalar(Sg[0:n, i, :], slots_i[0:n, :], place[0:n, i, bass.ds(e, 1)],
                                    gate[0:n, i, bass.ds(e, 1)], ALU.is_equal, ALU.mult).then_inc(S["e_sgx"], 1)

            def e_gather(n):
                dve.wait_ge(S["e_xg"], 2 * n + 2)
                v.tensor_copy(xgE[:, 4:8, :], banks[7][:, 0:4 * CAP].rearrange("p (c s) -> p c s", c=4)) \
                    .then_inc(S["e_xgd"], 1)

            def e_up(n, q):
                dve.wait_ge(S["e_piece"], n * EPIECES + (2 * q + 2))
                dve.wait_ge(S["e_sg"], n * 11 + (q + 1))
                v.tensor_tensor(hE[:, 2 * q:2 * q + 2, :], banks[2 + q % 2][:, 0:2 * CAP].rearrange("p (j s) -> p j s", j=2),
                                sgE[:, q % 2], ALU.mult).then_inc(S["e_he"], 1)

            def e_down(n):
                dve.wait_ge(S["e_piece"], (n + 1) * EPIECES)
                v.tensor_copy(yE[:, 4:8, :], banks[5][:, 0:4 * CAP].rearrange("p (c s) -> p c s", c=4)) \
                    .then_inc(S["e_ytd"], 1)

            def e_tail(n):
                dve.wait_ge(S["e_ytr"], 2 * n + 2)
                v.tensor_copy(yS[:, 512:1024], banks[7][0:CAP, :]).then_inc(S["e_yd"], 1)

            def e_add(n):
                for c in range(DC):
                    dve.wait_ge(S["e_sc"], n * DC + (c + 1))
                    v.tensor_tensor(xT[:, c, :], banks[6 + c % 2][:, 0:T], xT[:, c, :], ALU.add).then_inc(S["e_xt"], 1)

            e_slots(0)
            dve.wait_ge(S["r_exp"], 3)
            for i, (_, n) in enumerate(TILES):
                link(v.tensor_scalar(wts[0:n, i, 2:3], wts[0:n, i, 1:2], 1.0, None, ALU.add))
                link(v.reciprocal(wts[0:n, i, 3:4], wts[0:n, i, 2:3]))
                link(v.tensor_tensor(wts[0:n, i, 4:5], wts[0:n, i, 1:2], wts[0:n, i, 3:4], ALU.mult))
                link(v.tensor_scalar(oh1[0:n, i, 0:8], oh1[0:n, i, 0:8], wts[0:n, i, 3:4], None, ALU.mult))
                link(v.tensor_scalar(gate[0:n, i, 0:8], exp_i[0:n, :], topf[0:n, i, 1:2], wts[0:n, i, 4:5],
                                     ALU.is_equal, ALU.mult))
                v.tensor_tensor(gate[0:n, i, 0:8], gate[0:n, i, 0:8], oh1[0:n, i, 0:8], ALU.add).then_inc(S["r_gate"], 1)
            dve.wait_ge(S["r_gate"], 3)

            def e_body(n, e, prev, nxt):
                e_gather(n)
                for q in range(11):
                    e_up(n, q)
                    if q == 0 and prev is not None:
                        e_gates(prev)
                    if q == 1 and prev is not None:
                        e_tail(prev)
                    if q == 3 and prev is not None:
                        e_add(prev)
                if nxt is not None:
                    e_slots(nxt)
                e_down(n)

            e_body(0, 0, None, 1)
            with dve.Fori(1, E_) as e:
                e_body(e, e, e - 1, e + 1)
            e_gates(E_ - 1)
            e_tail(E_ - 1)
            e_add(E_ - 1)
            with dve.If(dve.value_load(most_i[0:1, 0:1], min_val=0, max_val=T) > CAP):
                with dve.Fori(0, 2) as ps:
                    dve.wait_ge(S["e_gtr"], E_)
                    v.tensor_scalar(slots_i, slots_i, float(CAP), None, ALU.add).then_inc(S["o_iota"], 1)
                    with dve.Fori(0, E_) as e:
                        n = ps * E_ + e + E_
                        dve.wait_ge(S["o_iota"], ps + 1)
                        e_slots(e)
                        e_body(n, e, None, None)
                        e_gates(e)
                        e_tail(n)
                        e_add(n)
            v.wait_ge(S["rms_ready"], 5)
            v.reciprocal(rinv[:, :], rt[:, :]).then_inc(S["rinv_ready"], 1)
            v.wait_ge(S["rinv_ready"], 5)
            for c in range(DC):
                v.scalar_tensor_tensor(out=h3T[:, c, :], in0=xT[:, c, :], scalar=vcol("norm_out_g", c), in1=rinv[:, :],
                                       op0=ALU.mult, op1=ALU.mult).then_inc(S["h_ready"], 1)
            for n in range(1, 6, 2):
                dve.wait_ge(S["h_tr"], 6 + n + 1)
                i, q = n // 2, n % 2
                rows = TILES[i][1]
                v.tensor_copy(htok[0:rows, i, 512 * q:512 * q + 512], banks[2 + n % 4][0:rows, :]).then_inc(S["h_dve"], 1)

        @block.tensor
        def _(pe):
            t = nc.tensor
            pe.wait_ge(S["const"], 7)
            pe.wait_ge(S["vec_in"], 16 * len(VEC_ROWS))
            t.transpose(banks[7][:, 0:P], vecrows[:, 0, :], ident[:, :])
            t.transpose(banks[7][:, P:VEC_N], vecrows[0:VEC_N - P, 1, :], ident[0:VEC_N - P, 0:VEC_N - P]) \
                .then_inc(S["vec_tr"], 1)
            pe.wait_ge(S["x_in"], 48)
            for c in range(DC):
                if c >= 2:
                    pe.wait_ge(S["xt_ready"], c - 1)
                for i, (t0, n) in enumerate(TILES):
                    mm = t.transpose(banks[c % 2][:, t0:t0 + n], xtok[0:n, i, P * c:P * c + P], ident[0:n, 0:n])
                mm.then_inc(S["tr_ready"], 1)
            pe.wait_ge(S["ws_in"], 16)
            for g_ in range(G):
                mm = t.transpose(banks[4 + g_ // 4][:, P * (g_ % 4):P * (g_ % 4) + P], wsraw[:, g_, :], ident[:, :])
                if g_ % 4 == 3:
                    mm.then_inc(S["ws_tr"], 1)
            norm_pe(0, tokens(B[2]))
            pe.wait_ge(S["ws_copied"], 2)
            n_piece = [0]

            def arrived():
                n = n_piece[0]
                n_piece[0] += 1
                pe.wait_ge(landed[n % RING], arrival[n])
                return n % RING

            def v_transposes(q):
                pe.wait_ge(S["gelu_done"], 4 * q + 4)
                if q:
                    pe.wait_ge(S["v_evac"], 3 * q)
                for i, (t0, n) in enumerate(TILES):
                    for j in range(4):
                        mm = t.transpose(banks[(4, 5, 7)[i]][0:n, P * j:P * j + P], vT[:, 4 * q + j, t0:t0 + n],
                                         ident[:, :])
                mm.then_inc(S["v_tr"], 1)

            pe.wait_ge(S["h_ready"], DC)
            for n in range(16):
                w = slot(arrived(), "p (k n) -> p k n", k=DC)
                for j in range(2):
                    g_ = 2 * n + j
                    if g_ >= 4:
                        pe.wait_ge(S["gelu_done"], g_ - 3)
                    for k in range(DC):
                        mm = t.matmul(banks[g_ % 4][:, 0:T], w[:, k, P * j:P * j + P], hT[:, k, :],
                                      start=(k == 0), stop=(k == DC - 1))
                    mm.then_inc(S["z_ready"], 1)
                if n in (2, 4, 6, 8):
                    v_transposes(n // 2 - 1)
            pe.wait_ge(S["v_norm"], 3)
            pe.wait_ge(S["ws_masked"], 1)
            pe.wait_ge(S["wsS_in"], 16 * NB)
            for c in range(AC):
                if c < 4:
                    pe.wait_ge(S["gelu_done"], 29 + c)
                else:
                    pe.wait_ge(S["mix_add"], c - 3)
                for i, (t0, n) in enumerate(TILES):
                    w = wsT[:, c // 2, :] if i < 2 else wsS[0:SMP, c // 2, :]
                    mm = t.matmul(banks[c % 4][:, t0:t0 + n], vtok[0:n, i, P * c:P * c + P], w,
                                  start=(i == 0), stop=True, skip_group_check=True)
                mm.then_inc(S["mix_ready"], 1)
            pe.wait_ge(S["mix_done"], AC)
            for c in range(DC):
                w = slot(arrived(), "p (k n) -> p k n", k=AC)
                if c >= 4:
                    pe.wait_ge(S["xt_ready"], DC + c - 3)
                for k in range(AC):
                    mm = t.matmul(banks[c % 4][:, 0:T], w[:, k, :], vT[:, k, :], start=(k == 0), stop=(k == AC - 1))
                mm.then_inc(S["ao_ready"], 1)
            norm_pe(1, tokens(B[2]))
            pe.wait_ge(S["h_ready"], 2 * DC)
            for q in range(11):
                for up in range(2):
                    w = slot(arrived(), "p (k n) -> p k n", k=DC)
                    for j in range(2):
                        if q:
                            pe.wait_ge(S["hf_ready" if up else "sg_ready"], 2 * q + j - 1)
                        for k in range(DC):
                            mm = t.matmul(banks[2 * up + j][:, 0:T], w[:, k, P * j:P * j + P], hT[:, k, :],
                                          start=(k == 0), stop=(k == DC - 1))
                        mm.then_inc(S["ffu_ready" if up else "ffg_ready"], 1)
            pe.wait_ge(S["hf_ready"], FC)
            for c in range(DC):
                if c >= 4:
                    pe.wait_ge(S["xt_ready"], 2 * DC + c - 3)
                for hf in range(2):
                    w = slot(arrived(), "p (k n) -> p k n", k=11, n=11 * P)
                    for k in range(11):
                        mm = t.matmul(banks[c % 4][:, 0:T], w[:, k, :], hF[:, 11 * hf + k, :],
                                      start=(hf == 0 and k == 0), stop=(hf == 1 and k == 10))
                    mm.then_inc(S["fd_ready"], 1)
            norm_pe(2, tokens(B[2]))
            pe.wait_ge(S["last_cols"], 2)
            for hf in range(2):
                for j in range(4):
                    mm = t.transpose(banks[4 + hf][0:1 + NB, P * j:P * j + P], lastc[:, 4 * hf + j, :], ident[:, :])
                mm.then_inc(S["last_tr"], 1)

            def project(bank, w, x, ks, inc, first_wait=None):
                for k in range(ks):
                    if first_wait is not None:
                        pe.wait_ge(S["mx_ready"], first_wait + k + 1)
                    mm = t.matmul(bank, w(k), x[:, k, :], start=(k == 0), stop=(k == ks - 1))
                if inc:
                    mm.then_inc(S[inc], 1)

            s_ = arrived()
            w1v = slot(s_, "p (k n) -> p k n", n=512, k=DC)
            a1v = slot(s_, "p (k n) -> p k n", n=512, off=512, k=DC)
            pe.wait_ge(S["xt_ready"], 3 * DC)
            project(banks[0][0:LW, 0:T], lambda k: w1v[:, k, :], m0T, DC, "lo1_ready", 0)
            project(banks[1][0:LW, 0:T], lambda k: a1v[:, k, :], m1T, DC, "lo1_ready", 8)
            s_ = arrived()
            g1v = slot(s_, "p (k n) -> p k n", n=DC * LG, k=DC)
            project(banks[2][:, 0:T], lambda k: g1v[:, k, 0:P], m0T, DC, None, 16)
            project(banks[3][0:LG - P, 0:T], lambda k: g1v[:, k, P:LG], m0T, DC, "lo1_ready", 16)
            s_ = arrived()
            w2v = (slot(s_, None, parts=LW, n=D), slot(s_, None, parts=LW, n=D, off=D))
            pe.wait_ge(S["last_rows"], 2)
            for n in range(16):
                if n % 8 == 0:
                    pe.wait_ge(S["lo1_done"], n // 8 + 1)
                if n >= 4:
                    pe.wait_ge(S["lo2_done"], n - 3)
                c = n % 8
                t.matmul(banks[4 + n % 4][:, 0:T], w2v[n // 8][:, P * c:P * c + P], (lw1, la1)[n // 8],
                         start=True, stop=True).then_inc(S["lo2_ready"], 1)
            pe.wait_ge(S["lo1_done"], 4)
            for n in range(0, 24, 2):
                w = slot(arrived(), "p (k n) -> p k n", k=DC)
                for j in range(2):
                    if n >= 4:
                        pe.wait_ge(S["kvr_done"], n + j - 3)
                    m = n // 8
                    project(banks[(n + j) % 4][:, 0:T], lambda k: w[:, k, P * j:P * j + P], (m1T, m0T, m1T)[m], DC,
                            "kvr_ready", 24 + 8 * m)
                if n == 14:
                    pass
            for c in range(DC):
                pe.wait_ge(S["kk_sq"], c + 1)
                if c < 4:
                    pe.wait_ge(S["lo2_done"], 13 + c)
                else:
                    pe.wait_ge(S["kn_root"], c - 3)
                t.matmul(banks[4 + c % 4][:, 0:T], halves[:, :], kkT[:, c, :], start=True, stop=True) \
                    .then_inc(S["kn_ready"], 1)
            for c in range(DC):
                pe.wait_ge(S["rk_ready"], c + 1)
                if c < 4:
                    pe.wait_ge(S["kn_root"], 5 + c)
                else:
                    pe.wait_ge(S["bon_ready"], c - 3)
                t.matmul(banks[4 + c % 4][:, 0:T], halves[:, :], rkT[:, c, :], start=True, stop=True) \
                    .then_inc(S["rb_ready"], 1)
            pe.wait_ge(S["kvr_done"], 24)
            for n in range(18):
                m, i, q = n // 6, n % 6 // 2, n % 2
                if m == 1:
                    pe.wait_ge(S["scaled"], 6)
                if m == 2:
                    pe.wait_ge(S["scaled"], 8)
                if n >= 4:
                    pe.wait_ge(S["tk_act" if n % 2 == 0 else "tk_dve"], (n - 4) // 2 + 1)
                src = (vfT, KtT, BtT)[m]
                t0, rows = TILES[i]
                for j in range(4):
                    mm = t.transpose(banks[n % 4][0:rows, P * j:P * j + P], src[:, 4 * q + j, t0:t0 + rows], ident[:, :])
                mm.then_inc(S["tk_tr"], 1)
            pe.wait_ge(S["tk_act"], 9)
            pe.wait_ge(S["tk_dve"], 9)
            pe.wait_ge(S["masks"], 1)
            pe.wait_ge(S["memz"], 3)
            pe.wait_ge(S["bon_ready"], DC)
            for st in steps:
                k = st[0]
                if k == "score":
                    _, u, f, i = st
                    t0 = 128 * i
                    for hh in range(8):
                        p, hr = 4 * f + hh // 2, hrows(hh % 2)
                        if hh >= 6:
                            pe.wait_ge(S["ms_ready"], 8 * u + hh - 5)
                        elif u and hh == 0:
                            pe.wait_ge(S["s_done"], 4 * u)
                        elif u and hh == 3:
                            pe.wait_ge(S["y_done"], 2 * u)
                        out_ = banks[hh % 6][:, :].rearrange("p (m r t) -> p m r t", m=2, r=2)
                        for m, src in enumerate((kT, aT)):
                            mm = t.matmul(out_[:, m], src[hr, p, t0:t0 + 128], QR[hr, p, :, t0:t0 + 128],
                                          start=(m == 0), stop=True, skip_group_check=True)
                        mm.then_inc(S["sc_ready"], 1)
                elif k == "x0":
                    u = st[1]
                    pe.wait_ge(S["xt0_ready"], 2 * u + 2)
                    for b in range(2):
                        for j in range(4):
                            mm = t.transpose(banks[b][:, P * j:P * j + P], XX[:, 4 * b + j, 1, :], ident[:, :])
                        mm.then_inc(S["xt_tr"], 1)
                elif k == "t1":
                    _, u, m = st
                    n = 5 * u + m - 1
                    for b in range(2):
                        if m == 1:
                            pe.wait_ge(S["x0_ready"], 2 * u + b + 1)
                        else:
                            pe.wait_ge(S["x_done"], 4 * (n - 1) + 2 * b + 2)
                        for j in range(4):
                            mm = t.matmul(banks[b][:, P * j:P * j + P], MS[:, 4 * b + j, BL, :], XX[:, 4 * b + j, 0, :],
                                          start=(j == 0), stop=True, skip_group_check=True)
                        mm.then_inc(S["t1_ready"], 1)
                elif k == "xl":
                    _, u, m = st
                    n = 5 * u + m - 1
                    for b in range(2):
                        pe.wait_ge(S["t1_done"], 2 * n + b + 1)
                        for j in range(4):
                            hh, bank = 4 * b + j, banks[2 + 2 * b + j // 2]
                            o = 256 * (j % 2)
                            t.matmul(bank[:, o:o + P], XX[:, hh, 1, :], T1[:, b, j, :],
                                     start=(j % 2 == 0), stop=True, skip_group_check=True)
                            mm = t.matmul(bank[:, o + P:o + 2 * P], T1[:, b, j, :], XX[:, hh, 1, :],
                                          start=False, stop=True, skip_group_check=True)
                            if j % 2:
                                mm.then_inc(S["x_ready"], 1)
                elif k == "w1":
                    _, u, f, i, c = st
                    n = 4 * f + c
                    if c % 2 == 0:
                        pe.wait_ge(S["x_done"], 20 * u + 20)
                    for pr in range(4):
                        p = 4 * f + pr
                        for h2 in range(2):
                            o = P * pr + 64 * h2
                            t.matmul(banks[0][:, o:o + 64], MS[:, 2 * pr + h2, KL, :], Vk[:, i, 512 * f + o:512 * f + o + 64],
                                     start=(o == 0), stop=False, skip_group_check=True)
                    if c:
                        pe.wait_ge(S["s_done"], 2 * n)
                    for pr in range(4):
                        p = 4 * f + pr
                        mm = t.matmul(banks[0][:, P * pr:P * pr + P], QR[:, p, 0, 128 * i:128 * i + 128],
                                      Sbd[:, c % 2, p, :], start=False, stop=True, skip_group_check=True)
                    mm.then_inc(S["w1_ready"], 1)
                elif k == "u":
                    _, u, f, i, c = st
                    n, tb = 4 * f + c, 64 * (c % 2)
                    for pr in range(4):
                        o = 512 * f + P * pr
                        t.matmul(banks[2][:, P * pr:P * pr + P], Kk[tb:tb + 64, i, o:o + P], Vk[tb:tb + 64, i, o:o + P],
                                 start=(pr == 0), stop=False, skip_group_check=True)
                    pe.wait_ge(S["w1_done"], n + 1)
                    for hh in range(8):
                        mm = t.matmul(banks[1][:, 64 * hh:64 * hh + 64], XX[:, hh, 1, :], W1[:, 64 * hh:64 * hh + 64],
                                      start=(hh == 0), stop=True, skip_group_check=True)
                    mm.then_inc(S["u_ready"], 1)
                elif k == "s":
                    _, u, f, i, c = st
                    n, tb = 4 * f + c, 64 * (c % 2)
                    pe.wait_ge(S["u_done"], n + 1)
                    for pr in range(4):
                        o = 512 * f + P * pr
                        mm = t.matmul(banks[2][:, P * pr:P * pr + P], Bk[tb:tb + 64, i, o:o + P], Us[tb:tb + 64, P * pr:P * pr + P],
                                      start=False, stop=True, skip_group_check=True)
                    mm.then_inc(S["s_ready"], 1)
                elif k == "y":
                    _, u, f, i, c = st
                    n, tb = 4 * f + c, 64 * (c % 2)
                    bank = banks[3 + c % 2]
                    if n >= 2:
                        pe.wait_ge(S["y_done"], n - 1)
                    for pr in range(4):
                        p, o = 4 * f + pr, 64 * pr
                        t.matmul(bank[:, o:o + 64], Sbd[:, c % 2, p, :], QR[:, p, 1, CH * c:CH * c + CH],
                                 start=(pr == 0), stop=False, skip_group_check=True)
                        for h2 in range(2):
                            hh, hr, vo = 2 * pr + h2, hrows(h2), 512 * f + P * pr + 64 * h2
                            t.matmul(bank[hr, o:o + 64], Vk[:, i, vo:vo + 64], MS[:, hh, KA, tb:tb + 64],
                                     start=False, stop=False, skip_group_check=True)
                            mm = t.matmul(bank[hr, o:o + 64], Us[:, 64 * hh:64 * hh + 64], MS[:, hh, BA, tb:tb + 64],
                                          start=False, stop=True, skip_group_check=True)
                    mm.then_inc(S["y_ready"], 1)
                elif k == "q_score":
                    p = st[1]
                    if p:
                        q_wait(pe, "q_oc", p - 1, 1)
                    for h2 in range(2):
                        hr = hrows(h2)
                        out_ = banks[6 + h2][0:SMP, 0:P].rearrange("p (m r t) -> p m r t", m=2, r=2)
                        for m, src in enumerate((kT, aT)):
                            mm = t.matmul(out_[:, m], src[hr, p, NP_:T], QR[hr, p, :, NP_:T],
                                          start=(m == 0), stop=True, skip_group_check=True)
                        mm.then_inc(S["q_pe"], 1)
                elif k == "q_s0":
                    p = st[1]
                    q_wait(pe, "q_ms", p, 1)
                    pe.wait_ge(S["nat_in"], 16 * 2 * (p + 1))
                    for b in range(NB):
                        mm = t.transpose(banks[6][:, 64 * b:64 * b + 64], nat[:, b, :], ident[0:HD, 0:HD])
                    mm.then_inc(S["q_pe"], 1)
                elif k == "q_x0":
                    p = st[1]
                    q_wait(pe, "q_xt0", p, 1)
                    for h2 in range(2):
                        mm = t.transpose(banks[7][0:SMP, 32 * h2:32 * h2 + 32], XXq[:, h2, 1, :], ident[0:SMP, 0:SMP])
                    mm.then_inc(S["q_pe"], 1)
                elif k == "q_qs":
                    p = st[1]
                    q_wait(pe, "q_s0", p, 1)
                    out_ = banks[6][:, 0:2 * SMP].rearrange("p (r t) -> p r t", r=2)
                    for b in range(NB):
                        t.matmul(out_[:, :, NS * b:NS * b + NS], S0bd[:, b, :], QR[:, p, :, NP_ + NS * b:NP_ + NS * b + NS],
                                 start=(b == 0), stop=False, skip_group_check=True)
                    for h2 in range(2):
                        vo = P * p + 64 * h2
                        mm = t.matmul(banks[6][hrows(h2), 0:2 * SMP].rearrange("p (r t) -> p r t", r=2),
                                      Vk[0:SMP, 2, vo:vo + 64], MSq[:, h2, 0:2, :],
                                      start=False, stop=False, skip_group_check=True)
                    mm.then_inc(S["q_pe"], 1)
                elif k == "q_t1":
                    p = st[1]
                    q_wait(pe, "q_x", p)
                    for h2 in range(2):
                        mm = t.matmul(banks[7][0:SMP, 32 * h2:32 * h2 + 32], MSq[:, h2, BL, :], XXq[:, h2, 0, :],
                                      start=(h2 == 0), stop=True, skip_group_check=True)
                    mm.then_inc(S["q_pe"], 1)
                elif k == "q_x2":
                    p = st[1]
                    q_wait(pe, "q_t1c", p)
                    for h2 in range(2):
                        mm = t.matmul(banks[7][0:SMP, 32 * h2:32 * h2 + 32], T1q[:, h2, :], XXq[:, h2, 1, :],
                                      start=(h2 == 0), stop=True, skip_group_check=True)
                    mm.then_inc(S["q_pe"], 1)
                elif k == "q_w1":
                    p = st[1]
                    q_wait(pe, "q_xt2c", p)
                    q_wait(pe, "q_w1t", p)
                    t.transpose(banks[7][0:SMP, 0:P], W1Tq, ident[:, :]).then_inc(S["q_pe"], 1)
                elif k == "q_u":
                    p = st[1]
                    q_wait(pe, "q_w1", p)
                    for h2 in range(2):
                        mm = t.matmul(banks[7][0:SMP, 64 * h2:64 * h2 + 64], XXq[:, h2, 1, :], W1q[:, 64 * h2:64 * h2 + 64],
                                      start=(h2 == 0), stop=True, skip_group_check=True)
                    mm.then_inc(S["q_pe"], 1)
                elif k == "q_y":
                    p = st[1]
                    q_wait(pe, "q_uc", p)
                    for h2 in range(2):
                        mm = t.matmul(banks[6][hrows(h2), SMP:2 * SMP], Uq[:, 64 * h2:64 * h2 + 64], MSq[:, h2, BA, :],
                                      start=False, stop=True, skip_group_check=True)
                    mm.then_inc(S["q_pe"], 1)
                elif k == "q_st":
                    p = st[1]
                    pe.wait_ge(S["q_vx"], 2 * p + 2)
                    pe.wait_ge(S["q_ux"], 2 * p + 2)
                    for m, (src, x) in enumerate(((Kk, Vexp), (Bk, Uexp))):
                        for h2 in range(2):
                            o = P * p + 64 * h2
                            mm = t.matmul(banks[7][hrows(h2), :], src[0:SMP, 2, o:o + 64],
                                          x[:, h2].rearrange("p b i -> p (b i)"),
                                          start=(m == 0), stop=(m == 1), skip_group_check=True)
                    mm.then_inc(S["q_pe"], 1)
                elif k == "q_out":
                    p = st[1]
                    q_wait(pe, "q_send", p)
                    q_wait(pe, "q_yc", p)
                    for b in range(NB):
                        mm = t.transpose(banks[6 + b // 4][0:HD, P * (b % 4):P * (b % 4) + P], Send[:, b, :], ident[:, :])
                    mm.then_inc(S["q_pe"], 1)
            for hf in range(2):
                if hf == 0:
                    pe.wait_ge(S["s_done"], 16)
                    pe.wait_ge(S["y_done"], 8)
                for j in range(4):
                    mm = t.transpose(banks[hf][:, P * j:P * j + P], Sbd[:, 0, 4 * hf + j, :], ident[:, :])
                mm.then_inc(S["st_tr"], 1)
            q_wait(pe, "q_yc", DC - 1)
            for c in range(DC):
                if c >= 2:
                    pe.wait_ge(S["gn_yc"], c - 1)
                t.matmul(banks[2 + c % 2][:, 0:T], halves[:, :], yT[:, c, :], start=True, stop=True) \
                    .then_inc(S["gn_mean"], 1)
            s_ = arrived()
            g2v = (slot(s_, None, n=D), slot(s_, None, parts=LG - P, n=D, off=D))
            q_wait(pe, "q_oc", DC - 1, 1)
            for c in range(DC):
                pe.wait_ge(S["gn_sq"], c + 1)
                if c >= 2:
                    pe.wait_ge(S["gn_root"], c - 1)
                t.matmul(banks[4 + c % 2][:, 0:T], halves[:, :], rkT[:, c, :], start=True, stop=True) \
                    .then_inc(S["gn_var"], 1)
                if c >= 2:
                    pe.wait_ge(S["yg_ready"], c - 1)
                t.matmul(banks[6 + c % 2][:, 0:T], g2v[0][:, P * c:P * c + P], lg1[:, 0, :], start=True, stop=False)
                t.matmul(banks[6 + c % 2][:, 0:T], g2v[1][:, P * c:P * c + P], lg1[0:LG - P, 1, :], start=False, stop=True) \
                    .then_inc(S["g_ready"], 1)
            pe.wait_ge(S["st_row"], 2)
            pe.wait_ge(S["yg_ready"], DC)
            for q in range(4):
                w = slot(arrived(), "p (k n) -> p k n", k=DC)
                for j in range(2):
                    c = 2 * q + j
                    if c >= 4:
                        pe.wait_ge(S["xt_ready"], 3 * DC + c - 3)
                    for k in range(DC):
                        mm = t.matmul(banks[c % 4][:, 0:T], w[:, k, P * j:P * j + P], yT[:, k, :],
                                      start=(k == 0), stop=(k == DC - 1))
                    mm.then_inc(S["wo_ready"], 1)
            norm_pe(3, tokens(B[9]))
            pe.wait_ge(S["h_ready"], 4 * DC)
            pe.wait_ge(S["router_in"], 16)
            for i, (t0, n) in enumerate(TILES):
                for k in range(DC):
                    mm = t.matmul(banks[i // 2][0:n, 8 * i:8 * i + 8], h3T[:, k, t0:t0 + n], router[:, k, :],
                                  start=(k == 0), stop=(k == DC - 1))
                mm.then_inc(S["r_logit"], 1)
            for n in range(6):
                i, q = n // 2, n % 2
                t0, rows = TILES[i]
                if n >= 4:
                    pe.wait_ge(S["h_act" if n % 2 == 0 else "h_dve"], (n - 4) // 2 + 1)
                for j in range(4):
                    mm = t.transpose(banks[2 + n % 4][0:rows, P * j:P * j + P], h3T[:, 4 * q + j, t0:t0 + rows], ident[:, :])
                mm.then_inc(S["h_tr"], 1)
            pe.wait_ge(S["r_sel"], 3)
            pe.wait_ge(S["r_const"], 4)
            first = True
            for i, (_, n) in enumerate(TILES):
                for j in range(i + 1):
                    nj = TILES[j][1]
                    lhs = tri[0:n, 0:n] if j == i else ones[0:nj, 0:n]
                    t.matmul(banks[1][0:n, 32 + 8 * i:40 + 8 * i], lhs, chosen[0:nj, j, 0:8],
                             start=first, stop=(j == i), skip_group_check=True)
                    first = False
            for j in range(3):
                nj = TILES[j][1]
                mm = t.matmul(banks[1][:, 64:72], ones[0:nj, :], chosen[0:nj, j, 0:8], start=False, stop=(j == 2),
                              skip_group_check=True)
            mm.then_inc(S["r_pos"], 1)
            pe.wait_ge(S["h_act"], 3)
            pe.wait_ge(S["h_dve"], 3)
            pe.wait_ge(S["r_most"], 2)

            def e_gather(n):
                pe.wait_ge(S["e_sx"], 3 * n + 3)
                for q in range(2):
                    for j in range(4):
                        c = 4 * q + j
                        for i, (_, rows) in enumerate(TILES):
                            mm = t.matmul(banks[6 + q][:, CAP * j:CAP * j + CAP], htok[0:rows, i, P * c:P * c + P],
                                          Sx[0:rows, i, :], start=(i == 0), stop=(i == 2), skip_group_check=True)
                    mm.then_inc(S["e_xg"], 1)
                pe.wait_ge(S["e_xga"], n + 1)
                pe.wait_ge(S["e_xgd"], n + 1)

            def e_arrived(n, i):
                pe.wait_ge(eland[i % MRING], n * 48 + 16 * (i // MRING + 1))

            def e_gateup(n, q):
                for up in range(2):
                    e_arrived(n, 2 * q + up)
                    w = slot((2 * q + up) % MRING, "p (k n) -> p k n", k=DC)
                    if q >= 2:
                        pe.wait_ge(S["e_he" if up else "e_sg"], n * 11 + (q - 1))
                    for j in range(2):
                        for k in range(DC):
                            mm = t.matmul(banks[2 * up + q % 2][:, CAP * j:CAP * j + CAP], w[:, k, P * j:P * j + P],
                                          xgE[:, k, :], start=(k == 0), stop=(k == DC - 1), skip_group_check=True)
                    mm.then_inc(S["e_piece"], 1)

            def e_down(n):
                for r in range(11):
                    e_arrived(n, 22 + r)
                    w = slot((22 + r) % MRING, "p (k n) -> p k n", k=2)
                    pe.wait_ge(S["e_he"], n * 11 + (r + 1))
                    for k in range(2):
                        for c in range(DC):
                            mm = t.matmul(banks[4 + c // 4][:, CAP * (c % 4):CAP * (c % 4) + CAP], w[:, k, P * c:P * c + P],
                                          hE[:, 2 * r + k, :], start=(r == 0 and k == 0 and c % 4 == 0),
                                          stop=(r == 10 and k == 1), skip_group_check=True)
                    mm.then_inc(S["e_piece"], 1)

            def e_turn(n):
                pe.wait_ge(S["e_yta"], n + 1)
                pe.wait_ge(S["e_ytd"], n + 1)
                for q in range(2):
                    for j in range(4):
                        mm = t.transpose(banks[6 + q][0:CAP, P * j:P * j + P], yE[:, 4 * q + j, :], ident[:, :])
                    mm.then_inc(S["e_ytr"], 1)
                pe.wait_ge(S["e_sgx"], 3 * n + 3)
                for i, (t0, rows) in enumerate(TILES):
                    mm = t.transpose(banks[4][0:CAP, t0:t0 + rows], Sg[0:rows, i, :], ident[0:rows, 0:rows])
                mm.then_inc(S["e_gtr"], 1)

            def e_scatter(n):
                pe.wait_ge(S["e_ya"], n + 1)
                pe.wait_ge(S["e_yd"], n + 1)
                pe.wait_ge(S["e_gt"], n + 1)
                for c in range(DC):
                    if c >= 2:
                        pe.wait_ge(S["e_xt"], n * DC + (c - 1))
                    t.matmul(banks[6 + c % 2][:, 0:T], yS[:, P * c:P * c + P], GT, start=True, stop=True) \
                        .then_inc(S["e_sc"], 1)

            def e_body(n, prev):
                e_gather(n)
                for q in range(11):
                    e_gateup(n, q)
                    if q == 1 and prev is not None:
                        e_turn(prev)
                    if q == 3 and prev is not None:
                        e_scatter(prev)
                e_down(n)

            e_body(0, None)
            with pe.Fori(1, E_) as e:
                e_body(e, e - 1)
            e_turn(E_ - 1)
            e_scatter(E_ - 1)
            with pe.If(pe.value_load(most_i[0:1, 0:1], min_val=0, max_val=T) > CAP):
                pe.wait_ge(S["e_xt"], DC * E_)
                with pe.Fori(0, 2) as ps:
                    with pe.Fori(0, E_) as e:
                        n = ps * E_ + e + E_
                        e_body(n, None)
                        e_turn(n)
                        e_scatter(n)
                pe.wait_ge(S["e_xt"], DC * 3 * E_)
            sq = tokens(B[9])
            for c in range(DC):
                pe.wait_ge(S["sq_ready"], DC * 4 + c + 1)
                mm = t.matmul(banks[0][:, 0:T], ones[:, :], sq[:, c, :], start=(c == 0), stop=(c == DC - 1))
            mm.then_inc(S["norm_sum"], 1)
            pe.wait_ge(S["h_ready"], 5 * DC)
            for n in range(6):
                i, q = n // 2, n % 2
                t0, rows = TILES[i]
                if n >= 4:
                    pe.wait_ge(S["h_act" if n % 2 == 0 else "h_dve"], 3 + (n - 4) // 2 + 1)
                for j in range(4):
                    mm = t.transpose(banks[2 + n % 4][0:rows, P * j:P * j + P], h3T[:, 4 * q + j, t0:t0 + rows], ident[:, :])
                mm.then_inc(S["h_tr"], 1)


OUTS = {"y_prompt": (1, NP_, D), "y_sample": (NB, NS, D), "chunk_v": (1, NB, NS, AW), "shift_prompt": (1, 1, D),
        "wkv_prompt": (1, 1, H, HD, HD), "shift_sample": (1, NB, D), "wkv_sample": (1, NB, H, HD, HD)}


def kernel(**inputs):
    import numpy as np
    import concourse.bacc as bacc
    from concourse.bass_utils import run_bass_kernel_spmd

    nc = bacc.Bacc("TRN2", target_bir_lowering=False, num_devices=1)
    arrays, a = {}, {}
    for name, value in inputs.items():
        value = np.ascontiguousarray(value)
        if value.size == 0:
            continue
        arrays[name] = value
        a[name] = nc.dram_tensor(name, value.shape, mybir.dt.from_np(value.dtype), kind="ExternalInput").ap()
    out = {name: nc.dram_tensor("out_" + name, shape, F32, kind="ExternalOutput").ap() for name, shape in OUTS.items()}
    trunk_kernel(nc, a, out)
    got = run_bass_kernel_spmd(nc, [arrays], core_ids=[0]).results[0]
    return tuple(got["out_" + name] for name in OUTS)
```

```python
from contextlib import ExitStack

import concourse.bass as bass
from concourse import mybir

ALU = mybir.AluOpType
ACT = mybir.ActivationFunctionType
AX_X = mybir.AxisListType.X
F32 = mybir.dt.float32
F32R = mybir.dt.float32r
I32 = mybir.dt.int32
U32 = mybir.dt.uint32

P = 128
D, DC = 1024, 8
NP_, NB, NS = 256, 8, 4
SMP = NB * NS
T = NP_ + SMP
TILES = ((0, 128), (128, 128), (256, 32))
AW, AC = 2048, 16
G = 8
FF, FC = 2816, 22
H, HD = 16, 64
LW, LG = 64, 160
E_, CAP = 8, 96
CH = 64
RMS_EPS, LN_EPS, GN_EPS = 1e-6, 1e-5, 64e-5
DECAY = 0.6065306597126334
LEVELS = (1, 2, 4, 8, 16, 32)

SLOT = 2048
RING = 4
MRING = 11
ARENA = 49328
FRING = 3
HRING = 3
EPIECES = 33


def trunk_kernel(nc, a, out):
    with ExitStack() as ctx:
        def sb(name, shape, dt=F32):
            return ctx.enter_context(nc.sbuf_tensor(name, shape, dt))

        def sem(name):
            return ctx.enter_context(nc.semaphore(name))

        banks = [ctx.enter_context(nc.psum_tensor(f"bank{i}", [P, 512], F32)) for i in range(8)]

        xT = sb("xT", [P, DC, T])
        vec = sb("vec", [P, 256])
        vecrows = sb("vecrows", [P, 2, P])
        omka = sb("omka", [P, DC])
        ident = sb("ident", [P, P])
        ones = sb("ones", [P, P])
        halves = sb("halves", [P, P])
        eps = sb("eps", [P, 3])
        rt = sb("rt", [P, T])
        rinv = sb("rinv", [P, T])
        with nc.sbuf_tensor("arena", [P, ARENA], F32) as arena:
            pass
        with ExitStack() as ff:
            def sbf(name, shape, dt=F32R):
                return ff.enter_context(nc.sbuf_tensor(name, shape, dt))

            fring = sbf("fring", [P, RING, SLOT], F32)
            fxH, fxL = sbf("fxH", [P, DC, T]), sbf("fxL", [P, DC, T])
            fhH, fhL = sbf("fhH", [P, FC, T]), sbf("fhL", [P, FC, T])
            fwH, fwL = sbf("fwH", [P, FRING, SLOT]), sbf("fwL", [P, FRING, SLOT])
            sgF = sbf("sgF", [P, 4, T], F32)
            hfF = sbf("hfF", [P, 4, T], F32)
        ering = sb("ering", [P, MRING, SLOT])
        wH = sb("wH", [P, HRING, SLOT], F32R)
        wL = sb("wL", [P, HRING, SLOT], F32R)
        xgH, xgL = [sb(name, [P, DC, CAP], F32R) for name in ("xgH", "xgL")]
        hH, hL = [sb(name, [P, FC, CAP], F32R) for name in ("hH", "hL")]
        emem = sb("emem", [P, 8752])

        def view(off, n, pattern=None, parts=P, mem=None, **kw):
            v = (arena if mem is None else mem)[0:parts, off:off + n]
            return v.rearrange(pattern, **kw) if pattern else v

        def tokens(off, chunks=DC):
            return view(off, chunks * T, "p (c t) -> p c t", c=chunks)

        def slot(i, pattern, parts=P, n=SLOT, off=0, **kw):
            return view(i * SLOT + off, n, pattern, parts=parts, **kw)

        B = [RING * SLOT + DC * T * k for k in range(10)]
        TOK = B[9] + DC * T
        CHN = TOK + 9 * D

        VEC_ROWS = [("norm_mix_g", 16), ("norm_ffn_g", 16), ("norm_out_g", 8), ("a_b_in", 32),
                    ("b_mu", 48), ("b_w0", 8), ("b_a0", 8), ("b_k_k", 8), ("b_k_a", 8), ("b_r_k", 8),
                    ("b_lnx_g", 8), ("b_lnx_b", 8), ("state_shift", 64)]
        col, at = {}, 0
        for name, n in VEC_ROWS:
            col[name] = at
            at += n
        VEC_N = at

        def vcol(name, c):
            return vec[:, col[name] + c:col[name] + c + 1]

        hT = tokens(B[0])
        uT = tokens(B[3], AC)
        vT = tokens(B[5], AC)
        mixT = tokens(B[1])
        lnG = view(B[7], AW)
        lnB = view(B[7] + AW, AW)
        bsB = tokens(B[9])
        vtok = view(TOK, 3 * AW, "p (i n) -> p i n", i=3)
        xtok = view(TOK + 3 * AW, 3 * D, "p (i n) -> p i n", i=3)
        wsT = view(CHN, G * P, "p (g t) -> p g t", g=G)
        wsraw = view(CHN + G * P, G * P, "p (g t) -> p g t", g=G)
        wsS = view(CHN + 2 * G * P, G * SMP, "p (g t) -> p g t", g=G)
        lnst = view(CHN + 2 * G * P + G * SMP, 3 * 4 * 6, "p (i q s) -> p i q s", i=3, q=4)
        lnmv = view(CHN + 2 * G * P + G * SMP + 72, 6, "p (i s) -> p i s", i=3)
        lnrs = view(CHN + 2 * G * P + G * SMP + 78, 6, "p (i s) -> p i s", i=3)
        hF = tokens(B[3])

        xxT, m0T, m1T = tokens(B[1]), tokens(B[2]), tokens(B[3])
        mixbuf = (m0T, m1T)
        QR = view(B[4], 2 * DC * T, "p (c r t) -> p c r t", c=DC, r=2)
        kT, vfT, aT, dT = tokens(B[6]), tokens(B[7]), tokens(B[8]), tokens(B[9])
        kkT = tokens(B[1])
        t1T = tokens(B[0])
        rkT = tokens(B[2])
        bonT = tokens(B[3])
        yT = tokens(B[7])
        KtT, BtT = tokens(B[1]), tokens(B[9])
        tok = view(TOK, 9 * D, "p (m i n) -> p m i n", m=3, i=3)
        Vk, Kk, Bk = tok[:, 0], tok[:, 1], tok[:, 2]
        MS = view(B[0], 8 * 512, "p (h m t) -> p h m t", h=8, m=4)
        XX = view(B[0] + 4096, 8 * 256, "p (h x t) -> p h x t", h=8, x=2)
        KL, KA, BL, BA = range(4)
        Sbd = view(CHN, 2 * D, "p (b c i) -> p b c i", b=2, c=DC)
        W1 = view(CHN + 2048, 512)
        Us = view(CHN + 2560, 512)
        mskA = view(CHN + 3072, 512, "p (m t) -> p m t", m=4)
        lvl = view(CHN + 3584, 6 * 256, "p (l x t) -> p l x t", l=6, x=2)
        T1 = view(CHN + 5120, 1024, "p (b h t) -> p b h t", b=2, h=4)
        lw1 = view(CHN + 5120, T, parts=LW)
        la1 = view(CHN + 5120 + T, T, parts=LW)
        lg1 = view(CHN + 6144, 2 * T, "p (k t) -> p k t", k=2)
        segm = view(CHN + 6144 + 2 * T, T)
        pc = view(CHN + 7008, 96, "p (c s) -> p c s", c=DC)
        pcn = view(CHN + 7104, 96, "p (c s) -> p c s", c=DC)
        W1Tq = view(CHN + 7200, 32)
        W1q = view(CHN + 7232, P, parts=SMP)
        T1q = view(CHN + 7360, 64, "p (h t) -> p h t", parts=SMP, h=2)
        mskS = view(CHN + 7424, 128, "p (m t) -> p m t", parts=SMP, m=4)
        bmask = view(CHN + 7552, NB, parts=SMP)
        router = view(CHN + 7560, 64, "p (k e) -> p k e", k=DC)
        S0bd = view(CHN + 7680, NB * P, "p (b i) -> p b i", b=NB)
        lastc = view(CHN, 72, "p (c n) -> p c n", c=DC)
        shrow = view(CHN + 128, D, parts=1 + NB)
        nat = view(B[9], 1024, "p (b j) -> p b j", parts=HD, b=NB)
        Uexp = view(B[9], 1024, "p (h b i) -> p h b i", parts=SMP, h=2, b=NB)
        Vexp = view(B[9] + 1024, 1024, "p (h b i) -> p h b i", parts=SMP, h=2, b=NB)
        Sout = view(B[9] + 1024, 1024, "p (b j) -> p b j", parts=HD, b=NB)
        MSq = view(B[9] + 2048, 256, "p (h m t) -> p h m t", parts=SMP, h=2, m=4)
        Send = view(B[0] + 6144, 512, "p (b i) -> p b i", b=NB)
        XXq = view(B[0] + 6656, 128, "p (h x t) -> p h x t", parts=SMP, h=2, x=2)
        Uq = view(B[0] + 6784, P, parts=SMP)
        wkvo = view(B[0], 8 * P, "p (c j) -> p c j", c=DC)

        h3T = tokens(B[8])

        def eview(off, n, pattern=None, parts=P, **kw):
            return view(off, n, pattern, parts=parts, mem=emem, **kw)

        tri = eview(0, P)
        slots_i = eview(128, CAP)
        exp_i = eview(224, E_)
        htok = eview(1024, 3 * D, "p (i n) -> p i n", i=3)
        Sx = eview(4096, 3 * CAP, "p (i s) -> p i s", i=3)
        Sg = eview(4384, 3 * CAP, "p (i s) -> p i s", i=3)
        GT = eview(4672, T, parts=CAP)
        sgE = eview(4960, 512, "p (b n) -> p b n", parts=CAP, b=2)
        hS = eview(5472, 512, "p (b n) -> p b n", parts=CAP, b=2)
        yS = eview(5984, D, parts=CAP)

        rbase = 256

        def rt3(k, dt=F32):
            v_ = eview(rbase + 32 * k, 27, "p (i e) -> p i e", i=3)
            return v_ if dt is F32 else v_.bitcast(dt)

        logit, top, topi, topf = rt3(0), rt3(1), rt3(2, U32), rt3(3)
        oh1, gate, chosen, place, wts = rt3(4), rt3(5), rt3(6), rt3(7), rt3(8)
        most = eview(rbase + 300, 2)
        most_i = eview(rbase + 302, 1).bitcast(I32)

        S = {}
        for name in """const pool_order vec_in x_in ws_in wsS_in router_in vec_ready tr_ready xt_ready sq_ready
            norm_sum rms_ready rinv_ready h_ready f_hi f_lo f_xh f_xl ws_tr ws_copied ws_masked z_ready gelu_done
            v_tr v_evac v_aggr v_std v_rstd v_norm mix_ready mix_add mix_done ao_ready ffg_ready ffu_ready
            sg_ready hf_ready fd_ready masks memz last_cols last_tr last_rows shift_out xx_ready mx_ready
            lo1_ready lo1_done lo2_ready lo2_done kvr_ready kvr_done kk_raw kk_sq kn_ready kn_root kk_chain
            rk_ready rb_ready bon_ready scan_ready pc_ready tk_tr tk_act tk_dve sc_ready ms_ready xt0_ready
            xt_tr x0_ready t1_ready t1_done x_ready x_done w1_ready w1_done u_ready u_done s_ready s_scaled
            s_done y_ready y_done st_tr st_row st_out nat_in q_vx q_ux q_out gn_mean gn_yc gn_sq gn_var
            gn_root g_ready yg_ready wo_ready r_const r_logit r_chain r_exp r_e r_sel r_pos r_most r_gate
            h_tr h_act h_dve e_sx e_xg e_xga e_xgd e_piece e_hi e_lo e_sg e_he e_htr e_hh e_hl e_sgx e_gtr e_ya e_yd
            e_gt e_sc e_xt o_iota chunkv_out y_out q_pe q_act q_dve exp_ready scaled rows_in""".split():
            S[name] = sem(name)
        landed = [sem(f"landed{i}") for i in range(RING)]

        eland = [sem(f"expert_landed{i}") for i in range(MRING)]

        pieces = []

        def piece(loads, sem_name, value):
            pieces.append((loads, sem_name, value))

        w_in = a["a_w_in"][0].rearrange("(k p) n -> p k n", p=P)
        for n in range(16):
            q = (n + 8) % 16
            piece([(lambda s: slot(s, "p (k n) -> p k n", k=DC), w_in[:, :, 256 * q:256 * q + 256])],
                  "z_ready", 2 * n + 2)
        w_ao = a["a_w_out"][0].rearrange("(k p) n -> p k n", p=P)
        for c in range(DC):
            piece([(lambda s: slot(s, "p (k n) -> p k n", k=AC), w_ao[:, :, P * c:P * c + P])],
                  "ao_ready", c + 1)
        w_g = a["f_w_gate"][0].rearrange("(k p) n -> p k n", p=P)
        w_u = a["f_w_up"][0].rearrange("(k p) n -> p k n", p=P)
        for q in range(11):
            for w, name in ((w_g, "ffg_ready"), (w_u, "ffu_ready")):
                piece([(lambda s: fring[:, s, :].rearrange("p (k n) -> p k n", k=DC), w[:, :, 256 * q:256 * q + 256])],
                      "f_lo", 2 * q + (name == "ffu_ready") + 1)
        w_d = a["f_w_down"][0].rearrange("(k p) n -> p k n", p=P)
        for c in range(DC):
            for hf in range(2):
                piece([(lambda s: fring[:, s, 0:11 * P].rearrange("p (k n) -> p k n", k=11),
                        w_d[:, 11 * hf:11 * hf + 11, P * c:P * c + P])], "f_lo", 22 + 2 * c + hf + 1)
        piece([(lambda s: slot(s, "p (k n) -> p k n", n=512, k=DC), a["b_w1"][0].rearrange("(k p) n -> p k n", p=P)),
               (lambda s: slot(s, "p (k n) -> p k n", n=512, off=512, k=DC),
                a["b_a1"][0].rearrange("(k p) n -> p k n", p=P))], "lo1_ready", 2)
        piece([(lambda s: slot(s, "p (k n) -> p k n", n=DC * LG, k=DC), a["b_g1"][0].rearrange("(k p) n -> p k n", p=P))],
              "lo1_ready", 3)
        piece([(lambda s: slot(s, None, parts=LW, n=D), a["b_w2"][0]),
               (lambda s: slot(s, None, parts=LW, n=D, off=D), a["b_a2"][0])], "lo2_ready", 16)
        for m, i in enumerate((1, 2, 0)):
            w = a["b_w_rkv"][0, i].rearrange("(k p) n -> p k n", p=P)
            for q in range(4):
                piece([(lambda s: slot(s, "p (k n) -> p k n", k=DC), w[:, :, 256 * q:256 * q + 256])],
                      "kvr_ready", 8 * m + 2 * q + 2)
        piece([(lambda s: slot(s, None, n=D), a["b_g2"][0, 0:P]),
               (lambda s: slot(s, None, parts=LG - P, n=D, off=D), a["b_g2"][0, P:LG])], "g_ready", DC)
        w = a["b_w_out"][0].rearrange("(k p) n -> p k n", p=P)
        for q in range(4):
            piece([(lambda s: slot(s, "p (k n) -> p k n", k=DC), w[:, :, 256 * q:256 * q + 256])],
                  "wo_ready", 2 * q + 2)
        sums, arrival = [0] * RING, []
        for n, (loads, _, _) in enumerate(pieces):
            sums[n % RING] += 16 * len(loads)
            arrival.append(sums[n % RING])
        F_GU, FPIECES = 24, 38

        def f_words(n):
            return SLOT if n < 22 else 11 * P

        def f_used(n):
            return ("ffu_ready" if n % 2 else "ffg_ready", n - n % 2 + 2) if n < 22 else ("fd_ready", n - 21)

        def norm_pe(k, sq):
            for c in range(DC):
                nc.tensor.wait_ge(S["sq_ready"], DC * k + c + 1)
                mm = nc.tensor.matmul(banks[6][:, 0:T], ones[:, :], sq[:, c, :],
                                      start=(c == 0), stop=(c == DC - 1))
            mm.then_inc(S["norm_sum"], 1)

        def norm_act(k, sq):
            for c in range(DC):
                nc.scalar.wait_ge(S["xt_ready"], DC * k + c + 1)
                nc.scalar.activation(sq[:, c, :], xT[:, c, :], ACT.Square).then_inc(S["sq_ready"], 1)
            nc.scalar.wait_ge(S["norm_sum"], k + 1)
            nc.scalar.activation(rt[:, :], banks[6][:, 0:T], ACT.Sqrt, bias=eps[:, 0:1],
                                 scale=1.0 / D).then_inc(S["rms_ready"], 1)

        def norm_dve(k, gain, dst):
            nc.vector.wait_ge(S["rms_ready"], k + 1)
            nc.vector.reciprocal(rinv[:, :], rt[:, :]).then_inc(S["rinv_ready"], 1)
            nc.vector.wait_ge(S["rinv_ready"], k + 1)
            for c in range(DC):
                nc.vector.scalar_tensor_tensor(
                    out=dst[:, c, :], in0=xT[:, c, :], scalar=vec[:, gain + c:gain + c + 1],
                    in1=rinv[:, :], op0=ALU.mult, op1=ALU.mult).then_inc(S["h_ready"], 1)

        steps = []
        q_steps = [(kind, p) for p in range(DC)
                   for kind in ("q_score", "q_s0", "q_x0", "q_qs", "q_t1", "q_x2", "q_w1", "q_u", "q_y", "q_st", "q_out")]
        q_at = [0]

        def gap():
            if q_at[0] < len(q_steps):
                steps.append(q_steps[q_at[0]])
                q_at[0] += 1

        u_ = 0
        for f in range(2):
            for i in range(2):
                steps.append(("score", u_, f, i))
                gap()
                steps.append(("x0", u_, f, i))
                gap()
                for m in range(1, 6):
                    steps.append(("t1", u_, m))
                    gap()
                    steps.append(("xl", u_, m))
                    gap()
                for c in (2 * i, 2 * i + 1):
                    steps.append(("w1", u_, f, i, c))
                    gap()
                    steps.append(("u", u_, f, i, c))
                    gap()
                    steps.append(("s", u_, f, i, c))
                    steps.append(("y", u_, f, i, c))
                    gap()
                u_ += 1
        while q_at[0] < len(q_steps):
            gap()

        def expert_load(sp, e, i, used=None):
            dst = ering[:, i % MRING, :].rearrange("p (k n) -> p k n", k=DC if i < 22 else 2)
            if i < 22:
                w = a["m_w_up" if i % 2 else "m_w_gate"][0, e].rearrange("(k p) n -> p k n", p=P)
                src = w[:, :, 256 * (i // 2):256 * (i // 2) + 256]
            else:
                src = a["m_w_down"][0].rearrange("e (r k p) n -> (e r) p k n", k=2, p=P)[e * 11 + (i - 22)]
            if used is not None:
                sp.wait_ge(S["e_lo"], used)
            sp.dma_start(dst, src).then_inc(eland[i % MRING], 16)

        Q_PE = ("q_score", "q_score", "q_s0t", "q_xtr", "q_qs", "q_t1", "q_xt2", "q_w1r", "q_u", "q_y", "q_st", "q_otr")
        Q_ACT = ("q_s0", "q_s0", "q_x", "q_w1t", "q_t1c", "q_w1", "q_uc", "q_yc", "q_oc", "q_oc")
        Q_DVE = ("q_ms", "q_ms", "q_xt0", "q_xt0", "q_xt2c", "q_stm", "q_stm", "q_send")

        def q_wait(eng, what, p, nth=0):
            for name, order in (("q_pe", Q_PE), ("q_act", Q_ACT), ("q_dve", Q_DVE)):
                if what in order:
                    eng.wait_ge(S[name], len(order) * p + order.index(what) + nth + 1)

        def hrows(h2):
            return slice(64 * h2, 64 * h2 + 64)

        def bc(ap, axis, shape):
            return ap.unsqueeze(axis).to_broadcast(shape)

        block = ctx.enter_context(nc.Block())

        @block.sync
        def _(sp):
            sp.dma_start(xtok[:, 0, :], a["x_prompt"][0, 0:128, :]).then_inc(S["x_in"], 16)
            sp.dma_start(xtok[:, 1, :], a["x_prompt"][0, 128:256, :]).then_inc(S["x_in"], 16)
            sp.dma_start(xtok[0:SMP, 2, :], a["x_sample"].rearrange("b t d -> (b t) d")).then_inc(S["x_in"], 16)
            def stream(lo, hi):
                for n in range(lo, hi):
                    if n >= RING:
                        _, name, value = pieces[n - RING]
                        sp.wait_ge(S[name], value)
                    for dst, src in pieces[n][0]:
                        sp.dma_start(dst(n % RING), src).then_inc(landed[n % RING], 16)

            stream(0, 24)
            sp.wait_ge(S["v_norm"], 3)
            sp.dma_start(out["chunk_v"].rearrange("a b t n -> (a b t) n"), vtok[0:SMP, 2, :]).then_inc(S["chunkv_out"], 16)
            stream(24, 65)
            sp.wait_ge(S["last_rows"], 2)
            sp.dma_start(out["shift_prompt"].rearrange("a b d -> (a b) d"), shrow[0:1, :]).then_inc(S["shift_out"], 16)
            sp.dma_start(out["shift_sample"].rearrange("a b d -> (a b) d"), shrow[1:1 + NB, :]).then_inc(S["shift_out"], 16)
            stream(65, len(pieces) - 1)
            for st in steps:
                if st[0] == "q_score":
                    p = st[1]
                    if p:
                        q_wait(sp, "q_st", p - 1)
                    else:
                        sp.wait_ge(S["tk_act"], 9)
                        sp.wait_ge(S["tk_dve"], 9)
                    for h2 in range(2):
                        sp.dma_start(nat[:, :, 64 * h2:64 * h2 + 64],
                                     a["state_wkv"][0, :, 2 * p + h2].rearrange("b i j -> i b j")).then_inc(S["nat_in"], 16)
                if st[0] == "q_out":
                    p = st[1]
                    q_wait(sp, "q_oc", p, 1)
                    for h2 in range(2):
                        sp.dma_start(out["wkv_sample"][0, :, 2 * p + h2].rearrange("b i j -> i b j"),
                                     Sout[:, :, 64 * h2:64 * h2 + 64]).then_inc(S["q_out"], 16)
            sp.wait_ge(S["st_row"], 2)
            for h2 in range(2):
                sp.dma_start(out["wkv_prompt"][0, 0].rearrange("(c h) i j -> h i c j", h=2)[h2],
                             wkvo[64 * h2:64 * h2 + 64, :, 64 * h2:64 * h2 + 64]).then_inc(S["st_out"], 16)
            stream(len(pieces) - 1, len(pieces))
            sp.wait_ge(S["wo_ready"], DC)
            sp.wait_ge(S["yg_ready"], DC)
            for i in range(MRING):
                expert_load(sp, 0, i)
            with sp.Fori(0, E_ - 1) as e:
                for i in range(MRING, EPIECES + MRING):
                    expert_load(sp, e + i // EPIECES, i % EPIECES, e * EPIECES + (i - MRING + 1))
            for i in range(MRING, EPIECES):
                expert_load(sp, E_ - 1, i, (E_ - 1) * EPIECES + i - MRING + 1)
            sp.wait_ge(S["r_most"], 2)
            with sp.If(sp.value_load(most_i[0:1, 0:1], min_val=0, max_val=T) > CAP):
                with sp.Fori(0, 2) as ps:
                    with sp.Fori(0, E_) as e:
                        for i in range(EPIECES):
                            expert_load(sp, e, i, (ps * E_ + e) * EPIECES + (E_ * EPIECES + i - MRING + 1))
            for n in range(6):
                sp.wait_ge(S["h_act" if n % 2 == 0 else "h_dve"], 3 + n // 2 + 1)
                i, q = n // 2, n % 2
                dst = out["y_sample"].rearrange("b t d -> (b t) d") if i == 2 else out["y_prompt"][0, P * i:P * i + P, :]
                sp.dma_start(dst[:, 512 * q:512 * q + 512], htok[0:TILES[i][1], i, 512 * q:512 * q + 512]) \
                    .then_inc(S["y_out"], 16)
            sp.wait_ge(S["chunkv_out"], 16)
            sp.wait_ge(S["shift_out"], 32)
            sp.wait_ge(S["q_out"], 16 * 2 * DC)
            sp.wait_ge(S["st_out"], 32)
            sp.wait_ge(S["y_out"], 16 * 6)

        @block.gpsimd
        def _(pool):
            g = nc.gpsimd
            count = [0]

            def step(ins):
                count[0] += 1
                ins.then_inc(S["pool_order"], 1)
                pool.wait_ge(S["pool_order"], count[0])

            step(g.memset(ident[:, :], 0.0))
            g.affine_select(out=ident[:, :], in_=ident[:, :], compare_op=ALU.not_equal, fill=1.0, base=0,
                            pattern=[[-1, P]], channel_multiplier=1).then_inc(S["const"], 1)
            g.memset(ones[:, :], 1.0).then_inc(S["const"], 1)
            g.memset(eps[:, 0:1], RMS_EPS).then_inc(S["const"], 1)
            g.memset(eps[:, 1:2], LN_EPS).then_inc(S["const"], 1)
            g.memset(eps[:, 2:3], GN_EPS).then_inc(S["const"], 1)
            step(g.memset(halves[:, :], 0.0))
            g.memset(halves[0:64, 0:64], 1.0).then_inc(S["const"], 1)
            g.memset(halves[64:128, 64:128], 1.0).then_inc(S["const"], 1)
            step(g.memset(wsS[0:SMP], 0.0))
            pool.wait_ge(S["ws_copied"], 2)
            g.affine_select(out=wsT, in_=wsT, compare_op=ALU.is_ge, fill=0.0, base=0,
                            pattern=[[0, G], [1, P]], channel_multiplier=-1).then_inc(S["ws_masked"], 1)
            pool.wait_ge(S["ws_masked"], 1)
            for b in range(NB):
                pool.dma_start(wsS[NS * b:NS * b + NS, :, NS * b:NS * b + NS],
                               wsT[0:NS, :, 0:NS]).then_inc(S["wsS_in"], 16)

            step(g.memset(lvl, 0.0))
            for l, m in enumerate(LEVELS):
                xs = lvl[:, l, 0, :].rearrange("p (n k s) -> p n k s", k=2, s=m)[:, :, 0, :]
                xt = lvl[:, l, 1, :].rearrange("p (n k s) -> p n k s", k=2, s=m)[:, :, 1, :]
                n = P // (2 * m)
                step(g.memset(xs, 1.0))
                step(g.memset(xt, 1.0))
                step(g.affine_select(out=xs, in_=xs, compare_op=ALU.is_ge, fill=0.0, base=-m,
                                     pattern=[[-2 * m, n], [0, m]], channel_multiplier=1))
                step(g.affine_select(out=xs, in_=xs, compare_op=ALU.is_ge, fill=0.0, base=2 * m - 1,
                                     pattern=[[2 * m, n], [0, m]], channel_multiplier=-1))
                step(g.affine_select(out=xt, in_=xt, compare_op=ALU.is_ge, fill=0.0, base=0,
                                     pattern=[[-2 * m, n], [0, m]], channel_multiplier=1))
                step(g.affine_select(out=xt, in_=xt, compare_op=ALU.is_ge, fill=0.0, base=m - 1,
                                     pattern=[[2 * m, n], [0, m]], channel_multiplier=-1))
            for msk, width, ch in ((mskA, P, CH), (mskS, SMP, NS)):
                step(g.memset(msk[:, 0:2, :], 1.0))
                step(g.memset(msk[:, 2:4, :], -1.0))
                v4 = msk.rearrange("p m (n s) -> p m n s", s=ch)
                for m in range(4):
                    step(g.affine_select(out=v4[:, m], in_=v4[:, m], compare_op=ALU.is_ge, fill=0.0,
                                         base=0, pattern=[[-ch, width // ch], [0, ch]], channel_multiplier=1))
                    step(g.affine_select(out=msk[:, m, :], in_=msk[:, m, :],
                                         compare_op=ALU.is_gt if m % 2 == 0 else ALU.is_ge, fill=0.0, base=0,
                                         pattern=[[1, width]], channel_multiplier=-1))
            step(g.memset(bmask, 1.0))
            step(g.affine_select(out=bmask, in_=bmask, compare_op=ALU.is_ge, fill=0.0, base=0,
                                 pattern=[[-NS, NB]], channel_multiplier=1))
            step(g.affine_select(out=bmask, in_=bmask, compare_op=ALU.is_ge, fill=0.0, base=NS - 1,
                                 pattern=[[NS, NB]], channel_multiplier=-1))
            step(g.memset(segm, 1.0))
            step(g.memset(segm[:, 0:NP_].rearrange("p (n s) -> p n s", s=CH)[:, :, 0:1], 0.0))
            step(g.memset(segm[:, NP_:T].rearrange("p (n s) -> p n s", s=NS)[:, :, 0:1], 0.0))
            g.memset(S0bd, 0.0).then_inc(S["masks"], 1)
            pool.wait_ge(S["shift_out"], 32)
            g.memset(Sbd, 0.0).then_inc(S["memz"], 1)
            g.memset(W1, 0.0).then_inc(S["memz"], 1)
            g.memset(Us, 0.0).then_inc(S["memz"], 1)
            for st in steps:
                if st[0] == "q_score":
                    p = st[1]
                    if p:
                        pool.wait_ge(S["q_out"], 16 * 2 * p)
                    else:
                        pool.wait_ge(S["tk_act"], 9)
                        pool.wait_ge(S["tk_dve"], 9)
                    for h2 in range(2):
                        vv = Vk[0:SMP, 2, P * p + 64 * h2:P * p + 64 * h2 + 64]
                        g.tensor_tensor(Vexp[:, h2], bc(vv, 1, [SMP, NB, HD]), bc(bmask, 2, [SMP, NB, HD]), ALU.mult) \
                            .then_inc(S["q_vx"], 1)
                if st[0] == "q_u":
                    p = st[1]
                    q_wait(pool, "q_uc", p)
                    for h2 in range(2):
                        uu = Uq[:, 64 * h2:64 * h2 + 64]
                        g.tensor_tensor(Uexp[:, h2], bc(uu, 1, [SMP, NB, HD]), bc(bmask, 2, [SMP, NB, HD]), ALU.mult) \
                            .then_inc(S["q_ux"], 1)

            pool.wait_ge(S["y_done"], 8)
            pool.wait_ge(S["st_tr"], 2)
            step(g.memset(tri, 1.0))
            step(g.affine_select(out=tri, in_=tri, compare_op=ALU.is_gt, fill=0.0, base=0,
                                 pattern=[[1, P]], channel_multiplier=-1))
            g.iota(slots_i, pattern=[[1, CAP]], base=0, channel_multiplier=0,
                   allow_small_or_imprecise_dtypes=True).then_inc(S["r_const"], 1)
            g.iota(exp_i, pattern=[[1, E_]], base=0, channel_multiplier=0,
                   allow_small_or_imprecise_dtypes=True).then_inc(S["r_const"], 1)
            g.memset(chosen, 0.0).then_inc(S["r_const"], 1)
            g.memset(place, 0.0).then_inc(S["r_const"], 1)

        @block.scalar
        def _(act):
            at = 0
            for name, n in VEC_ROWS:
                src = a[name]
                flat = {"b_mu": lambda: src.rearrange("a i (c p) -> (a i c) p", p=P),
                        "b_r_k": lambda: src.rearrange("a (c h) n -> (a c) (h n)", h=2),
                        "state_shift": lambda: src.rearrange("a b (c p) -> (a b c) p", p=P),
                        "norm_out_g": lambda: src.rearrange("(c p) -> c p", p=P)}.get(
                            name, lambda: src.rearrange("a (c p) -> (a c) p", p=P))()
                act.dma_start(vecrows[at % P:at % P + n, at // P, :], flat).then_inc(S["vec_in"], 16)
                at += n
            act.dma_start(wsraw, a["a_w_s"][0].rearrange("g t s -> t g s")).then_inc(S["ws_in"], 16)
            act.dma_start(lnG, a["a_ln_g"].to_broadcast([P, AW])).then_inc(S["rows_in"], 16)
            act.dma_start(lnB, a["a_ln_b"].to_broadcast([P, AW])).then_inc(S["rows_in"], 16)
            for i in range(2):
                act.dma_start(bsB[:, :, P * i:P * i + P],
                              a["a_b_s"].to_broadcast([P, G, P])).then_inc(S["rows_in"], 16)
            for b in range(NB):
                t0 = NP_ + NS * b
                act.dma_start(bsB[:, :, t0:t0 + NS],
                              a["a_b_s"][:, :, 0:NS].to_broadcast([P, G, NS])).then_inc(S["rows_in"], 16)
            act.dma_start(router, a["m_router"][0].rearrange("(k p) e -> p k e", p=P)).then_inc(S["router_in"], 16)
            act.wait_ge(S["const"], 7)
            norm_act(0, tokens(B[2]))
            for g_ in range(32):
                act.wait_ge(S["z_ready"], g_ + 1)
                c = (g_ + 16) % 32
                dst = uT[:, c, :] if c < 16 else vT[:, c - 16, :]
                nc.scalar.activation(dst, banks[g_ % 4][:, 0:T], ACT.Gelu,
                                     bias=vcol("a_b_in", c)).then_inc(S["gelu_done"], 1)
                if g_ == 20:
                    act.wait_ge(S["v_aggr"], 3)
                    for i, (_, n) in enumerate(TILES):
                        nc.scalar.activation(lnrs[0:n, i, 0:1], lnmv[0:n, i, 1:2], ACT.Sqrt,
                                             bias=eps[0:n, 1:2]).then_inc(S["v_std"], 1)

            def f_w_high(n):
                act.wait_ge(landed[(F_GU + n) % RING], arrival[F_GU + n])
                if n >= FRING:
                    act.wait_ge(S[f_used(n - FRING)[0]], f_used(n - FRING)[1])
                w = f_words(n)
                nc.scalar.activation(fwH[:, n % FRING, 0:w], fring[:, (F_GU + n) % RING, 0:w], ACT.Copy) \
                    .then_inc(S["f_hi"], 1)

            act.wait_ge(S["mix_done"], AC)
            act.wait_ge(S["chunkv_out"], 16)
            f_w_high(0)
            f_w_high(1)
            norm_act(1, tokens(B[2]))
            for c in range(DC):
                act.wait_ge(S["h_ready"], DC + c + 1)
                nc.scalar.activation(fxH[:, c, :], hF[:, c, :], ACT.Copy).then_inc(S["f_xh"], 1)
            for n in range(FPIECES):
                if n and n % 2 == 0 and n <= 22:
                    for j in range(2):
                        m = n - 2 + j
                        act.wait_ge(S["hf_ready"], m + 1)
                        nc.scalar.activation(fhH[:, m, :], hfF[:, m % 4, :], ACT.Copy).then_inc(S["f_xh"], 1)
                if n % 2 == 1 and n < 22:
                    for j in range(2):
                        m = n - 1 + j
                        act.wait_ge(S["ffg_ready"], m + 1)
                        if m >= 4:
                            act.wait_ge(S["hf_ready"], m - 3)
                        nc.scalar.activation(sgF[:, m % 4, :], banks[j][:, 0:T], ACT.Silu).then_inc(S["sg_ready"], 1)
                if n + 2 < FPIECES:
                    f_w_high(n + 2)
            norm_act(2, tokens(B[1]))
            s_ = nc.scalar
            for hf in range(2):
                act.wait_ge(S["last_tr"], hf + 1)
                s_.activation(shrow[:, 512 * hf:512 * hf + 512], banks[4 + hf][0:1 + NB, :], ACT.Copy) \
                    .then_inc(S["last_rows"], 1)
            act.wait_ge(S["lo1_ready"], 1)
            s_.activation(lw1, banks[0][0:LW, 0:T], ACT.Tanh).then_inc(S["lo1_done"], 1)
            act.wait_ge(S["lo1_ready"], 2)
            s_.activation(la1, banks[1][0:LW, 0:T], ACT.Copy).then_inc(S["lo1_done"], 1)
            act.wait_ge(S["lo1_ready"], 3)
            s_.activation(lg1[:, 0, :], banks[2][:, 0:T], ACT.Sigmoid).then_inc(S["lo1_done"], 1)
            s_.activation(lg1[0:LG - P, 1, :], banks[3][0:LG - P, 0:T], ACT.Sigmoid).then_inc(S["lo1_done"], 1)
            for n in range(16):
                act.wait_ge(S["lo2_ready"], n + 1)
                dst, name = (dT, "b_w0") if n < 8 else (aT, "b_a0")
                s_.activation(dst[:, n % 8, :], banks[4 + n % 4][:, 0:T], ACT.Sigmoid, bias=vcol(name, n % 8)) \
                    .then_inc(S["lo2_done"], 1)
            for n in range(24):
                act.wait_ge(S["kvr_ready"], n + 1)
                dst = (kT[:, n % 8, :], vfT[:, n % 8, :], QR[:, n % 8, 1, :])[n // 8]
                s_.activation(dst, banks[n % 4][:, 0:T], ACT.Copy).then_inc(S["kvr_done"], 1)
                if n == 15:
                    for c in range(DC):
                        act.wait_ge(S["kk_raw"], c + 1)
                        s_.activation(kkT[:, c, :], QR[:, c, 0, :], ACT.Square).then_inc(S["kk_sq"], 1)
                if n == 21:
                    act.wait_ge(S["kn_root"], DC)
                    s_.activation(kkT, kkT, ACT.Ln).then_inc(S["kn_root"], 1)
                    act.wait_ge(S["kn_root"], DC + 1)
                    s_.activation(kkT, kkT, ACT.Exp, scale=-0.5).then_inc(S["kn_root"], 1)
            act.wait_ge(S["scan_ready"], DC + 1)
            act.wait_ge(S["kk_chain"], DC + 2)
            s_.activation(kkT, t1T, ACT.Exp, scale=-DECAY).then_inc(S["exp_ready"], 1)
            s_.activation(dT, dT, ACT.Exp, scale=-DECAY).then_inc(S["exp_ready"], 1)
            act.wait_ge(S["exp_ready"], 1)
            s_.activation(t1T, t1T, ACT.Exp, scale=DECAY).then_inc(S["exp_ready"], 1)
            for n in range(0, 18, 2):
                act.wait_ge(S["tk_tr"], n + 1)
                m, i, q = n // 6, n % 6 // 2, n % 2
                rows = TILES[i][1]
                s_.activation(tok[0:rows, (0, 2, 1)[m], i, 512 * q:512 * q + 512], banks[n % 4][0:rows, :], ACT.Copy) \
                    .then_inc(S["tk_act"], 1)
            for st in steps:
                k = st[0]
                if k == "x0":
                    u = st[1]
                    for b in range(2):
                        act.wait_ge(S["xt_tr"], 2 * u + b + 1)
                        s_.activation(XX[:, 4 * b:4 * b + 4, 0, :], banks[b][:, :].rearrange("p (h t) -> p h t", h=4),
                                      ACT.Copy).then_inc(S["x0_ready"], 1)
                elif k == "t1":
                    n = 5 * st[1] + st[2] - 1
                    for b in range(2):
                        act.wait_ge(S["t1_ready"], 2 * n + b + 1)
                        s_.activation(T1[:, b], banks[b][:, :].rearrange("p (h t) -> p h t", h=4), ACT.Copy) \
                            .then_inc(S["t1_done"], 1)
                elif k == "w1":
                    _, u, f, i, c = st
                    n, tb = 4 * f + c, 64 * (c % 2)
                    act.wait_ge(S["w1_ready"], n + 1)
                    s_.activation(W1[tb:tb + 64, :], banks[0][tb:tb + 64, :], ACT.Copy).then_inc(S["w1_done"], 1)
                elif k == "y":
                    _, u, f, i, c = st
                    n = 4 * f + c
                    act.wait_ge(S["y_ready"], n + 1)
                    s_.activation(yT[:, 4 * f:4 * f + 4, CH * c:CH * c + CH],
                                  banks[3 + c % 2][:, 0:4 * CH].rearrange("p (c t) -> p c t", c=4), ACT.Copy) \
                        .then_inc(S["y_done"], 1)
                elif k == "q_s0":
                    p = st[1]
                    q_wait(act, "q_s0t", p)
                    if p == 0:
                        act.wait_ge(S["masks"], 1)
                    else:
                        q_wait(act, "q_send", p - 1)
                    for h2 in range(2):
                        s_.activation(S0bd[hrows(h2), :, 64 * h2:64 * h2 + 64],
                                      banks[6][hrows(h2), :].rearrange("p (b i) -> p b i", b=NB), ACT.Copy) \
                            .then_inc(S["q_act"], 1)
                elif k == "q_x0":
                    p = st[1]
                    q_wait(act, "q_xtr", p)
                    s_.activation(XXq[:, :, 0, :], banks[7][0:SMP, 0:64].rearrange("p (h t) -> p h t", h=2), ACT.Copy) \
                        .then_inc(S["q_act"], 1)
                elif k == "q_qs":
                    p = st[1]
                    q_wait(act, "q_qs", p)
                    s_.activation(W1Tq, banks[6][:, 0:SMP], ACT.Copy).then_inc(S["q_act"], 1)
                elif k == "q_t1":
                    p = st[1]
                    q_wait(act, "q_t1", p)
                    s_.activation(T1q, banks[7][0:SMP, 0:64].rearrange("p (h t) -> p h t", h=2), ACT.Copy) \
                        .then_inc(S["q_act"], 1)
                elif k == "q_w1":
                    p = st[1]
                    q_wait(act, "q_w1r", p)
                    s_.activation(W1q, banks[7][0:SMP, 0:P], ACT.Copy).then_inc(S["q_act"], 1)
                elif k == "q_u":
                    p = st[1]
                    q_wait(act, "q_u", p)
                    s_.activation(Uq, banks[7][0:SMP, 0:P], ACT.Copy).then_inc(S["q_act"], 1)
                elif k == "q_y":
                    p = st[1]
                    q_wait(act, "q_y", p)
                    s_.activation(yT[:, p, NP_:T], banks[6][:, SMP:2 * SMP], ACT.Copy).then_inc(S["q_act"], 1)
                elif k == "q_out":
                    p = st[1]
                    q_wait(act, "q_otr", p)
                    for hf in range(2):
                        s_.activation(Sout[:, 4 * hf:4 * hf + 4, :],
                                      banks[6 + hf][0:HD, :].rearrange("p (b j) -> p b j", b=4), ACT.Copy) \
                            .then_inc(S["q_act"], 1)
            for hf in range(2):
                act.wait_ge(S["st_tr"], hf + 1)
                s_.activation(wkvo[:, 4 * hf:4 * hf + 4, :], banks[hf][:, :].rearrange("p (c j) -> p c j", c=4), ACT.Copy) \
                    .then_inc(S["st_row"], 1)
            for c in range(DC):
                act.wait_ge(S["gn_yc"], c + 1)
                s_.activation(rkT[:, c, :], yT[:, c, :], ACT.Square).then_inc(S["gn_sq"], 1)
            act.wait_ge(S["st_out"], 32)
            for c in range(DC):
                act.wait_ge(S["gn_var"], c + 1)
                s_.activation(t1T[:, c, :], banks[4 + c % 2][:, 0:T], ACT.Sqrt, bias=eps[:, 2:3], scale=1.0 / HD) \
                    .then_inc(S["gn_root"], 1)
            act.wait_ge(S["q_out"], 16 * 2 * DC)
            norm_act(3, tokens(B[9]))
            for n in range(0, 6, 2):
                act.wait_ge(S["h_tr"], n + 1)
                i, q = n // 2, n % 2
                rows = TILES[i][1]
                s_.activation(htok[0:rows, i, 512 * q:512 * q + 512], banks[2 + n % 4][0:rows, :], ACT.Copy) \
                    .then_inc(S["h_act"], 1)
            act.wait_ge(S["r_e"], 3)
            for i, (_, n) in enumerate(TILES):
                s_.activation(wts[0:n, i, 1:2], wts[0:n, i, 0:1], ACT.Exp).then_inc(S["r_exp"], 1)

            def e_w_high(n, i):
                j = i % EPIECES
                act.wait_ge(eland[j % MRING], (n + i // EPIECES) * 48 + 16 * (j // MRING + 1))
                if not (isinstance(n, int) and EPIECES * n + i < HRING):
                    act.wait_ge(S["e_piece"], n * EPIECES + (i - HRING + 1))
                s_.activation(wH[:, j % HRING, :], ering[:, j % MRING, :], ACT.Copy).then_inc(S["e_hi"], 1)

            def e_x_high(n):
                for q in range(2):
                    act.wait_ge(S["e_xg"], 2 * n + (q + 1))
                    s_.activation(xgH[:, 4 * q:4 * q + 4, :], banks[6 + q][:, 0:4 * CAP].rearrange("p (c s) -> p c s", c=4),
                                  ACT.Copy).then_inc(S["e_xga"], 1)

            def e_prologue(n):
                e_w_high(n, 0)
                e_x_high(n)
                e_w_high(n, 1)

            def e_result(n):
                act.wait_ge(S["e_piece"], (n + 1) * EPIECES)
                s_.activation(yS[:, 0:512], banks[4][0:CAP, :], ACT.Copy).then_inc(S["e_ya"], 1)

            def e_gates(n):
                act.wait_ge(S["e_gtr"], n + 1)
                s_.activation(GT, banks[4][0:CAP, 0:T], ACT.Copy).then_inc(S["e_gt"], 1)

            def e_body(n, prev, nxt):
                for i in range(EPIECES):
                    if i == 0 and prev is not None:
                        e_result(prev)
                    if i % 2 and i < 22:
                        q = i // 2
                        act.wait_ge(S["e_piece"], n * EPIECES + i)
                        if q >= 2:
                            act.wait_ge(S["e_he"], n * 11 + (q - 1))
                        s_.activation(sgE[:, q % 2], banks[0][0:CAP, 0:256], ACT.Silu).then_inc(S["e_sg"], 1)
                    if i % 2 and 3 <= i <= 23:
                        q = (i - 3) // 2
                        act.wait_ge(S["e_htr"], n * 11 + (q + 1))
                        s_.activation(hH[:, 2 * q:2 * q + 2, :], banks[1 + 2 * (q % 2)][:, 0:2 * CAP]
                                      .rearrange("p (j s) -> p j s", j=2), ACT.Copy).then_inc(S["e_hh"], 1)
                    if i == 6 and prev is not None:
                        e_gates(prev)
                    if i == 28 and nxt is not None:
                        e_x_high(nxt)
                    if i + 2 < EPIECES or nxt is not None:
                        e_w_high(n, i + 2)

            e_prologue(0)
            e_body(0, None, 1)
            with act.Fori(1, E_ - 1) as e:
                e_body(e, e - 1, e + 1)
            e_body(E_ - 1, E_ - 2, None)
            e_result(E_ - 1)
            e_gates(E_ - 1)
            with act.If(act.value_load(most_i[0:1, 0:1], min_val=0, max_val=T) > CAP):
                with act.Fori(0, 2) as ps:
                    with act.Fori(0, E_) as e:
                        n = ps * E_ + e + E_
                        e_prologue(n)
                        e_body(n, None, None)
                        e_result(n)
                        e_gates(n)
                act.wait_ge(S["e_xt"], DC * 3 * E_)
            sq = tokens(B[9])
            for c in range(DC):
                act.wait_ge(S["e_xt"], DC * (E_ - 1) + c + 1)
                s_.activation(sq[:, c, :], xT[:, c, :], ACT.Square).then_inc(S["sq_ready"], 1)
            act.wait_ge(S["norm_sum"], 5)
            s_.activation(rt[:, :], banks[0][:, 0:T], ACT.Sqrt, bias=eps[:, 0:1], scale=1.0 / D).then_inc(S["rms_ready"], 1)
            for n in range(0, 6, 2):
                act.wait_ge(S["h_tr"], 6 + n + 1)
                i, q = n // 2, n % 2
                rows = TILES[i][1]
                s_.activation(htok[0:rows, i, 512 * q:512 * q + 512], banks[2 + n % 4][0:rows, :], ACT.Copy) \
                    .then_inc(S["h_act"], 1)

        @block.vector
        def _(dve):
            v = nc.vector
            dve.wait_ge(S["tr_ready"], 1)
            v.tensor_copy(vec[:, 0:VEC_N], banks[7][:, 0:VEC_N]).then_inc(S["vec_ready"], 1)
            for c in range(DC):
                dve.wait_ge(S["tr_ready"], c + 2)
                v.tensor_copy(xT[:, c, :], banks[c % 2][:, 0:T]).then_inc(S["xt_ready"], 1)
            for hf in range(2):
                dve.wait_ge(S["ws_tr"], hf + 1)
                v.tensor_copy(wsT[:, 4 * hf:4 * hf + 4, :], banks[4 + hf][:, :].rearrange("p (g t) -> p g t", g=4)) \
                    .then_inc(S["ws_copied"], 1)
            dve.wait_ge(S["vec_ready"], 1)
            v.tensor_scalar(omka[:, :], vec[:, col["b_k_a"]:col["b_k_a"] + DC], -1.0, 1.0, ALU.mult, ALU.add)
            norm_dve(0, col["norm_mix_g"], hT)
            tb = (4, 5, 7)
            for q in range(4):
                dve.wait_ge(S["v_tr"], q + 1)
                for i, (_, n) in enumerate(TILES):
                    v.tensor_copy(vtok[0:n, i, 512 * q:512 * q + 512], banks[tb[i]][0:n, :])
                    v.bn_stats(lnst[0:n, i, q, :], banks[tb[i]][0:n, :]).then_inc(S["v_evac"], 1)
            dve.wait_ge(S["v_evac"], 12)
            for i, (_, n) in enumerate(TILES):
                v.bn_aggr(lnmv[0:n, i, :], lnst[0:n, i].rearrange("p q s -> p (q s)")).then_inc(S["v_aggr"], 1)
            dve.wait_ge(S["v_std"], 3)
            for i, (_, n) in enumerate(TILES):
                v.reciprocal(lnrs[0:n, i, 1:2], lnrs[0:n, i, 0:1]).then_inc(S["v_rstd"], 1)
            dve.wait_ge(S["rows_in"], 16 * (4 + NB))
            for i, (_, n) in enumerate(TILES):
                v.scalar_tensor_tensor(out=vtok[0:n, i, :], in0=vtok[0:n, i, :], scalar=lnmv[0:n, i, 0:1],
                                       in1=lnG[0:n, :], op0=ALU.subtract, op1=ALU.mult).then_inc(S["v_rstd"], 1)
                dve.wait_ge(S["v_rstd"], 4 + i)
                v.scalar_tensor_tensor(out=vtok[0:n, i, :], in0=vtok[0:n, i, :], scalar=lnrs[0:n, i, 1:2],
                                       in1=lnB[0:n, :], op0=ALU.mult, op1=ALU.add).then_inc(S["v_norm"], 1)
            dve.wait_ge(S["gelu_done"], 32)
            for c in range(AC):
                dve.wait_ge(S["mix_ready"], c + 1)
                v.tensor_tensor(mixT[:, c % 8, :], banks[c % 4][:, 0:T], bsB[:, c // 2, :], ALU.add) \
                    .then_inc(S["mix_add"], 1)
                if c:
                    dve.wait_ge(S["mix_add"], c)
                    v.tensor_tensor(vT[:, c - 1, :], mixT[:, (c - 1) % 8, :], uT[:, c - 1, :], ALU.mult) \
                        .then_inc(S["mix_done"], 1)
            dve.wait_ge(S["mix_add"], AC)
            v.tensor_tensor(vT[:, AC - 1, :], mixT[:, 7, :], uT[:, AC - 1, :], ALU.mult).then_inc(S["mix_done"], 1)
            for c in range(DC):
                dve.wait_ge(S["ao_ready"], c + 1)
                v.tensor_tensor(xT[:, c, :], banks[c % 4][:, 0:T], xT[:, c, :], ALU.add).then_inc(S["xt_ready"], 1)

            def f_w_low(n):
                dve.wait_ge(S["f_hi"], n + 1)
                w = f_words(n)
                v.tensor_tensor(fwL[:, n % FRING, 0:w], fring[:, (F_GU + n) % RING, 0:w],
                                fwH[:, n % FRING, 0:w].bitcast(F32), ALU.subtract).then_inc(S["f_lo"], 1)

            f_w_low(0)
            f_w_low(1)
            norm_dve(1, col["norm_ffn_g"], hF)
            for c in range(DC):
                dve.wait_ge(S["f_xh"], c + 1)
                v.tensor_tensor(fxL[:, c, :], hF[:, c, :], fxH[:, c, :].bitcast(F32), ALU.subtract).then_inc(S["f_xl"], 1)
            for n in range(FPIECES):
                if n and n % 2 == 0 and n <= 22:
                    for j in range(2):
                        m = n - 2 + j
                        dve.wait_ge(S["ffu_ready"], m + 1)
                        dve.wait_ge(S["sg_ready"], m + 1)
                        if m >= 4:
                            dve.wait_ge(S["f_xl"], DC + m - 3)
                        v.tensor_tensor(hfF[:, m % 4, :], banks[2 + j][:, 0:T], sgF[:, m % 4, :], ALU.mult) \
                            .then_inc(S["hf_ready"], 1)
                    for j in range(2):
                        m = n - 2 + j
                        dve.wait_ge(S["f_xh"], DC + m + 1)
                        v.tensor_tensor(fhL[:, m, :], hfF[:, m % 4, :], fhH[:, m, :].bitcast(F32), ALU.subtract) \
                            .then_inc(S["f_xl"], 1)
                if n >= 24 and n % 2 == 0:
                    c = (n - 24) // 2
                    dve.wait_ge(S["fd_ready"], 2 * c + 2)
                    v.tensor_tensor(xT[:, c, :], banks[c % 4][:, 0:T], xT[:, c, :], ALU.add).then_inc(S["xt_ready"], 1)
                if n + 2 < FPIECES:
                    f_w_low(n + 2)
            dve.wait_ge(S["fd_ready"], 2 * DC)
            v.tensor_tensor(xT[:, DC - 1, :], banks[(DC - 1) % 4][:, 0:T], xT[:, DC - 1, :], ALU.add).then_inc(S["xt_ready"], 1)
            norm_dve(2, col["norm_mix_g"] + 8, hT)
            dve.wait_ge(S["h_ready"], 3 * DC)
            dve.wait_ge(S["mix_done"], AC)
            hs = hT[:, :, NP_:T].rearrange("p c (b s) -> p c b s", s=NS)
            xs = xxT[:, :, NP_:T].rearrange("p c (b s) -> p c b s", s=NS)
            v.tensor_copy(lastc[:, :, 0:1], hT[:, :, NP_ - 1:NP_]).then_inc(S["last_cols"], 1)
            v.tensor_copy(lastc[:, :, 1:1 + NB], hs[:, :, :, NS - 1]).then_inc(S["last_cols"], 1)
            v.tensor_tensor(xxT[:, :, 1:NP_], hT[:, :, 0:NP_ - 1], hT[:, :, 1:NP_], ALU.subtract).then_inc(S["xx_ready"], 1)
            v.tensor_scalar(xxT[:, :, 0:1], hT[:, :, 0:1], -1.0, None, ALU.mult).then_inc(S["xx_ready"], 1)
            v.tensor_tensor(xs[:, :, :, 1:NS], hs[:, :, :, 0:NS - 1], hs[:, :, :, 1:NS], ALU.subtract) \
                .then_inc(S["xx_ready"], 1)
            shift = vec[:, col["state_shift"]:col["state_shift"] + 64].rearrange("p (b c) -> p c b", c=DC)
            v.tensor_tensor(xs[:, :, :, 0], shift, hs[:, :, :, 0], ALU.subtract).then_inc(S["xx_ready"], 1)
            dve.wait_ge(S["xx_ready"], 4)
            free_after = (None, None, ("lo1_ready", 1), ("lo1_ready", 2), ("lo1_ready", 3), ("kvr_ready", 8))
            for n, i in enumerate((3, 4, 5, 1, 2, 0)):
                if free_after[n]:
                    dve.wait_ge(S[free_after[n][0]], free_after[n][1])
                for c in range(DC):
                    v.scalar_tensor_tensor(out=mixbuf[n % 2][:, c, :], in0=xxT[:, c, :], scalar=vcol("b_mu", 8 * i + c),
                                           in1=hT[:, c, :], op0=ALU.mult, op1=ALU.add).then_inc(S["mx_ready"], 1)
            dve.wait_ge(S["kvr_done"], DC)
            for c in range(DC):
                v.tensor_scalar(QR[:, c, 0, :], kT[:, c, :], vcol("b_k_k", c), None, ALU.mult).then_inc(S["kk_raw"], 1)
            dve.wait_ge(S["lo2_done"], 16)
            dve.wait_ge(S["mx_ready"], 48)
            for c in range(DC):
                v.tensor_scalar(t1T[:, c, :], aT[:, c, :], vcol("b_k_a", c), omka[:, c:c + 1], ALU.mult, ALU.add) \
                    .then_inc(S["kk_chain"], 1)
            dve.wait_ge(S["kk_chain"], DC)
            v.tensor_tensor(kT, kT, t1T, ALU.mult).then_inc(S["kk_chain"], 1)
            dve.wait_ge(S["kk_chain"], DC + 1)
            for c in range(DC):
                dve.wait_ge(S["kn_ready"], c + 1)
                v.tensor_scalar(kkT[:, c, :], banks[4 + c % 4][:, 0:T], 1e-24, None, ALU.max) \
                    .then_inc(S["kn_root"], 1)
            dve.wait_ge(S["masks"], 1)
            for c in range(DC):
                v.tensor_tensor_scan(out=t1T[:, c, :], data0=segm, data1=dT[:, c, :], initial=0.0,
                                     op0=ALU.mult, op1=ALU.add).then_inc(S["scan_ready"], 1)
            dve.wait_ge(S["scan_ready"], DC)
            v.tensor_tensor(dT, t1T, dT, ALU.subtract).then_inc(S["scan_ready"], 1)
            dve.wait_ge(S["kn_root"], DC + 2)
            v.tensor_tensor(QR[:, :, 0, :], QR[:, :, 0, :], kkT, ALU.mult).then_inc(S["kk_chain"], 1)
            dve.wait_ge(S["kk_chain"], DC + 2)
            v.tensor_tensor(aT, QR[:, :, 0, :], aT, ALU.mult).then_inc(S["kk_chain"], 1)
            def at_ends(src, dst, ends):
                for lo, hi, s0, n, w in ((0, NP_, 0, 4, CH), (NP_, T, 4, NB, NS)):
                    v.tensor_tensor(dst[:, :, lo:hi].rearrange("p c (n s) -> p c n s", n=n),
                                    src[:, :, lo:hi].rearrange("p c (n s) -> p c n s", n=n),
                                    bc(ends[:, :, s0:s0 + n], 3, [P, DC, n, w]), ALU.mult).then_inc(S["scaled"], 1)

            dve.wait_ge(S["exp_ready"], 1)
            v.tensor_copy(pc[:, :, 0:4], kkT[:, :, CH - 1:NP_:CH]).then_inc(S["pc_ready"], 1)
            v.tensor_copy(pc[:, :, 4:12], kkT[:, :, NP_ + NS - 1:T:NS]).then_inc(S["pc_ready"], 1)
            dve.wait_ge(S["pc_ready"], 2)
            v.tensor_scalar(pcn, pc, -1.0, None, ALU.mult).then_inc(S["pc_ready"], 1)
            dve.wait_ge(S["kk_chain"], DC + 3)
            dve.wait_ge(S["exp_ready"], 2)
            v.tensor_tensor(QR[:, :, 0, :], QR[:, :, 0, :], dT, ALU.mult).then_inc(S["scaled"], 1)
            dve.wait_ge(S["exp_ready"], 3)
            v.tensor_tensor(aT, aT, t1T, ALU.mult).then_inc(S["scaled"], 1)
            dve.wait_ge(S["scaled"], 2)
            dve.wait_ge(S["pc_ready"], 3)
            at_ends(aT, BtT, pcn)
            dve.wait_ge(S["kvr_done"], 24)
            for c in range(DC):
                v.scalar_tensor_tensor(out=rkT[:, c, :], in0=QR[:, c, 1, :], scalar=vcol("b_r_k", c), in1=kT[:, c, :],
                                       op0=ALU.mult, op1=ALU.mult).then_inc(S["rk_ready"], 1)
            dve.wait_ge(S["rk_ready"], DC)
            v.tensor_tensor(kT, kT, t1T, ALU.mult).then_inc(S["scaled"], 1)
            for c in range(DC):
                dve.wait_ge(S["rb_ready"], c + 1)
                v.tensor_tensor(bonT[:, c, :], banks[4 + c % 4][:, 0:T], vfT[:, c, :], ALU.mult).then_inc(S["bon_ready"], 1)
            v.tensor_tensor(QR[:, :, 1, :], QR[:, :, 1, :], kkT, ALU.mult).then_inc(S["scaled"], 1)
            dve.wait_ge(S["scaled"], 6)
            at_ends(kT, KtT, pc)
            for n in range(1, 18, 2):
                dve.wait_ge(S["tk_tr"], n + 1)
                m, i, q = n // 6, n % 6 // 2, n % 2
                rows = TILES[i][1]
                v.tensor_copy(tok[0:rows, (0, 2, 1)[m], i, 512 * q:512 * q + 512], banks[n % 4][0:rows, :]).then_inc(S["tk_dve"], 1)
            for st in steps:
                k = st[0]
                if k == "score":
                    _, u, f, i = st
                    for hh in range(8):
                        dve.wait_ge(S["sc_ready"], 8 * u + hh + 1)
                        v.tensor_tensor(MS[:, hh], banks[hh % 6][:, :].rearrange("p (m t) -> p m t", m=4), mskA, ALU.mult) \
                            .then_inc(S["ms_ready"], 1)
                elif k == "x0":
                    u = st[1]
                    v.tensor_copy(XX[:, :, 1, :], bc(ident[:, :], 1, [P, 8, P])).then_inc(S["xt0_ready"], 1)
                    dve.wait_ge(S["xt0_ready"], 2 * u + 1)
                    dve.wait_ge(S["ms_ready"], 8 * u + 8)
                    v.copy_predicated(XX[:, :, 1, :], bc(lvl[:, 0, 1, :], 1, [P, 8, P]).bitcast(I32), MS[:, :, BL, :]) \
                        .then_inc(S["xt0_ready"], 1)
                elif k == "xl":
                    _, u, m = st
                    n = 5 * u + m - 1
                    for b in range(2):
                        for j in range(2):
                            dve.wait_ge(S["x_ready"], 4 * n + 2 * b + j + 1)
                            hh = 4 * b + 2 * j
                            v.copy_predicated(XX[:, hh:hh + 2], bc(lvl[:, m], 1, [P, 2, 2, P]).bitcast(I32),
                                              banks[2 + 2 * b + j][:, :].rearrange("p (h x t) -> p h x t", h=2, x=2)) \
                                .then_inc(S["x_done"], 1)
                elif k == "u":
                    _, u, f, i, c = st
                    n, tb = 4 * f + c, 64 * (c % 2)
                    dve.wait_ge(S["u_ready"], n + 1)
                    v.tensor_copy(Us[tb:tb + 64, :], banks[1][tb:tb + 64, :]).then_inc(S["u_done"], 1)
                    for h2 in range(2):
                        hr, hc = hrows(h2), slice(64 * h2, 64 * h2 + 64)
                        v.tensor_tensor(Sbd[hr, (c + 1) % 2, 4 * f:4 * f + 4, hc], Sbd[hr, c % 2, 4 * f:4 * f + 4, hc],
                                        bc(pc[hr, 4 * f:4 * f + 4, c], 2, [64, 4, 64]), ALU.mult).then_inc(S["s_scaled"], 1)
                elif k == "s":
                    _, u, f, i, c = st
                    n = 4 * f + c
                    dve.wait_ge(S["s_ready"], n + 1)
                    dve.wait_ge(S["s_scaled"], 2 * n + 2)
                    for h2 in range(2):
                        hr, hc = hrows(h2), slice(64 * h2, 64 * h2 + 64)
                        so = Sbd[hr, (c + 1) % 2, 4 * f:4 * f + 4, hc]
                        v.tensor_tensor(so, banks[2][:, :].rearrange("p (c i) -> p c i", c=4)[hr, :, hc], so, ALU.add) \
                            .then_inc(S["s_done"], 1)
                elif k == "q_score":
                    p = st[1]
                    for h2 in range(2):
                        q_wait(dve, "q_score", p, h2)
                        v.tensor_tensor(MSq[:, h2], banks[6 + h2][0:SMP, 0:P].rearrange("p (m t) -> p m t", m=4), mskS,
                                        ALU.mult).then_inc(S["q_dve"], 1)
                    v.tensor_copy(XXq[:, :, 1, :], bc(ident[0:SMP, 0:SMP], 1, [SMP, 2, SMP])).then_inc(S["q_dve"], 1)
                    q_wait(dve, "q_xt0", p)
                    q_wait(dve, "q_ms", p, 1)
                    v.copy_predicated(XXq[:, :, 1, :], bc(lvl[0:SMP, 0, 1, 0:SMP], 1, [SMP, 2, SMP]).bitcast(I32),
                                      MSq[:, :, BL, :]).then_inc(S["q_dve"], 1)
                elif k == "q_x2":
                    p = st[1]
                    q_wait(dve, "q_xt2", p)
                    v.copy_predicated(XXq[:, :, 1, :], bc(lvl[0:SMP, 1, 1, 0:SMP], 1, [SMP, 2, SMP]).bitcast(I32),
                                      banks[7][0:SMP, 0:64].rearrange("p (h t) -> p h t", h=2)).then_inc(S["q_dve"], 1)
                elif k == "q_st":
                    p = st[1]
                    if p:
                        q_wait(dve, "q_otr", p - 1)
                    q_wait(dve, "q_s0", p, 1)
                    for h2 in range(2):
                        hr, hc = hrows(h2), slice(64 * h2, 64 * h2 + 64)
                        v.tensor_tensor(Send[hr], S0bd[hr, :, hc], bc(pc[hr, p, 4:12], 2, [64, NB, 64]), ALU.mult) \
                            .then_inc(S["q_dve"], 1)
                    q_wait(dve, "q_st", p)
                    q_wait(dve, "q_stm", p, 1)
                    v.tensor_tensor(Send, banks[7][:, :].rearrange("p (b i) -> p b i", b=NB), Send, ALU.add) \
                        .then_inc(S["q_dve"], 1)
            for c in range(DC):
                dve.wait_ge(S["gn_mean"], c + 1)
                v.scalar_tensor_tensor(out=yT[:, c, :], in0=banks[2 + c % 2][:, 0:T], scalar=-1.0 / HD, in1=yT[:, c, :],
                                       op0=ALU.mult, op1=ALU.add).then_inc(S["gn_yc"], 1)
            for c in range(DC):
                dve.wait_ge(S["gn_root"], c + 1)
                v.reciprocal(t1T[:, c, :], t1T[:, c, :]).then_inc(S["r_chain"], 1)
                dve.wait_ge(S["r_chain"], 3 * c + 1)
                v.scalar_tensor_tensor(out=yT[:, c, :], in0=yT[:, c, :], scalar=vcol("b_lnx_g", c), in1=t1T[:, c, :],
                                       op0=ALU.mult, op1=ALU.mult).then_inc(S["r_chain"], 1)
                dve.wait_ge(S["r_chain"], 3 * c + 2)
                v.scalar_tensor_tensor(out=yT[:, c, :], in0=yT[:, c, :], scalar=vcol("b_lnx_b", c), in1=bonT[:, c, :],
                                       op0=ALU.add, op1=ALU.add).then_inc(S["r_chain"], 1)
                dve.wait_ge(S["r_chain"], 3 * c + 3)
                dve.wait_ge(S["g_ready"], c + 1)
                v.tensor_tensor(yT[:, c, :], banks[6 + c % 2][:, 0:T], yT[:, c, :], ALU.mult).then_inc(S["yg_ready"], 1)
            for c in range(DC):
                dve.wait_ge(S["wo_ready"], c + 1)
                v.tensor_tensor(xT[:, c, :], banks[c % 4][:, 0:T], xT[:, c, :], ALU.add).then_inc(S["xt_ready"], 1)
            norm_dve(3, col["norm_ffn_g"] + 8, tokens(B[8]))
            chain = [3 * DC]

            def link(ins):
                chain[0] += 1
                ins.then_inc(S["r_chain"], 1)
                dve.wait_ge(S["r_chain"], chain[0])

            dve.wait_ge(S["r_const"], 4)
            for i, (_, n) in enumerate(TILES):
                dve.wait_ge(S["r_logit"], 3)
                link(v.tensor_copy(logit[0:n, i, 0:8], banks[i // 2][0:n, 8 * i:8 * i + 8]))
                link(v.max(out=top[0:n, i, 0:8], in_=logit[0:n, i, 0:8]))
                v.tensor_tensor(wts[0:n, i, 0:1], top[0:n, i, 1:2], top[0:n, i, 0:1], ALU.subtract).then_inc(S["r_e"], 1)
                link(v.max_index(out=topi[0:n, i, 0:8], in_max=top[0:n, i, 0:8], in_values=logit[0:n, i, 0:8]))
                link(v.tensor_copy(topf[0:n, i, 0:2], topi[0:n, i, 0:2]))
                link(v.tensor_scalar(oh1[0:n, i, 0:8], exp_i[0:n, :], topf[0:n, i, 0:1], None, ALU.is_equal))
                v.scalar_tensor_tensor(out=chosen[0:n, i, 0:8], in0=exp_i[0:n, :], scalar=topf[0:n, i, 1:2],
                                       in1=oh1[0:n, i, 0:8], op0=ALU.is_equal, op1=ALU.add).then_inc(S["r_sel"], 1)
            for n in range(1, 6, 2):
                dve.wait_ge(S["h_tr"], n + 1)
                i, q = n // 2, n % 2
                rows = TILES[i][1]
                v.tensor_copy(htok[0:rows, i, 512 * q:512 * q + 512], banks[2 + n % 4][0:rows, :]).then_inc(S["h_dve"], 1)
            dve.wait_ge(S["r_pos"], 1)
            for i, (_, n) in enumerate(TILES):
                link(v.tensor_copy(place[0:n, i, 0:8], banks[1][0:n, 32 + 8 * i:40 + 8 * i]))
            v.reduce_max(most[:, 0:1], banks[1][:, 64:72], AX_X).then_inc(S["r_most"], 1)
            dve.wait_ge(S["r_most"], 1)
            v.tensor_copy(most_i, most[:, 0:1]).then_inc(S["r_most"], 1)

            def e_slots(e):
                for i, (_, n) in enumerate(TILES):
                    v.tensor_scalar(Sx[0:n, i, :], slots_i[0:n, :], place[0:n, i, bass.ds(e, 1)],
                                    chosen[0:n, i, bass.ds(e, 1)], ALU.is_equal, ALU.mult).then_inc(S["e_sx"], 1)

            def e_gates(e):
                for i, (_, n) in enumerate(TILES):
                    v.tensor_scalar(Sg[0:n, i, :], slots_i[0:n, :], place[0:n, i, bass.ds(e, 1)],
                                    gate[0:n, i, bass.ds(e, 1)], ALU.is_equal, ALU.mult).then_inc(S["e_sgx"], 1)

            def e_w_low(n, i):
                dve.wait_ge(S["e_hi"], n * EPIECES + (i + 1))
                j = i % EPIECES
                v.tensor_tensor(wL[:, j % HRING, :], ering[:, j % MRING, :], wH[:, j % HRING, :].bitcast(F32),
                                ALU.subtract).then_inc(S["e_lo"], 1)

            def e_x_low(n):
                for q in range(2):
                    dve.wait_ge(S["e_xga"], 2 * n + (q + 1))
                    v.tensor_tensor(xgL[:, 4 * q:4 * q + 4, :],
                                    banks[6 + q][:, 0:4 * CAP].rearrange("p (c s) -> p c s", c=4),
                                    xgH[:, 4 * q:4 * q + 4, :].bitcast(F32), ALU.subtract).then_inc(S["e_xgd"], 1)

            def e_prologue(n, e):
                e_slots(e)
                e_w_low(n, 0)
                e_x_low(n)
                e_w_low(n, 1)

            def e_result(n):
                dve.wait_ge(S["e_piece"], (n + 1) * EPIECES)
                v.tensor_copy(yS[:, 512:1024], banks[5][0:CAP, :]).then_inc(S["e_yd"], 1)

            def e_add(n, c):
                dve.wait_ge(S["e_sc"], n * DC + (c + 1))
                v.tensor_tensor(xT[:, c, :], banks[6 + c % 2][:, 0:T], xT[:, c, :], ALU.add).then_inc(S["e_xt"], 1)

            for i, (_, n) in enumerate(TILES):
                dve.wait_ge(S["r_exp"], 3)
                link(v.tensor_scalar(wts[0:n, i, 2:3], wts[0:n, i, 1:2], 1.0, None, ALU.add))
                link(v.reciprocal(wts[0:n, i, 3:4], wts[0:n, i, 2:3]))
                link(v.tensor_tensor(wts[0:n, i, 4:5], wts[0:n, i, 1:2], wts[0:n, i, 3:4], ALU.mult))
                link(v.tensor_scalar(oh1[0:n, i, 0:8], oh1[0:n, i, 0:8], wts[0:n, i, 3:4], None, ALU.mult))
                link(v.tensor_scalar(gate[0:n, i, 0:8], exp_i[0:n, :], topf[0:n, i, 1:2], wts[0:n, i, 4:5],
                                     ALU.is_equal, ALU.mult))
                v.tensor_tensor(gate[0:n, i, 0:8], gate[0:n, i, 0:8], oh1[0:n, i, 0:8], ALU.add).then_inc(S["r_gate"], 1)
            dve.wait_ge(S["r_gate"], 3)

            def e_body(n, prev, nxt):
                for i in range(EPIECES):
                    if i == 0 and prev is not None:
                        e_result(prev)
                    if i % 2 == 0 and 2 <= i <= 22:
                        q = (i - 2) // 2
                        dve.wait_ge(S["e_piece"], n * EPIECES + i)
                        dve.wait_ge(S["e_sg"], n * 11 + (q + 1))
                        if q >= 2:
                            dve.wait_ge(S["e_htr"], n * 11 + (q - 1))
                        v.tensor_tensor(hS[:, q % 2], banks[2][0:CAP, 0:256], sgE[:, q % 2], ALU.mult) \
                            .then_inc(S["e_he"], 1)
                    if i % 2 and 3 <= i <= 23:
                        q = (i - 3) // 2
                        dve.wait_ge(S["e_hh"], n * 11 + (q + 1))
                        v.tensor_tensor(hL[:, 2 * q:2 * q + 2, :], banks[1 + 2 * (q % 2)][:, 0:2 * CAP]
                                        .rearrange("p (j s) -> p j s", j=2), hH[:, 2 * q:2 * q + 2, :].bitcast(F32),
                                        ALU.subtract).then_inc(S["e_hl"], 1)
                    if i == 2 and prev is not None:
                        e_gates(prev)
                    if 8 <= i < 16 and prev is not None:
                        e_add(prev, i - 8)
                    if i == 24 and nxt is not None:
                        e_slots(nxt)
                    if i == 28 and nxt is not None:
                        e_x_low(nxt)
                    if i + 2 < EPIECES or nxt is not None:
                        e_w_low(n, i + 2)

            def e_tail(n, e):
                e_result(n)
                e_gates(e)
                for c in range(DC):
                    e_add(n, c)

            e_prologue(0, 0)
            e_body(0, None, 1)
            with dve.Fori(1, E_ - 1) as e:
                e_body(e, e - 1, e + 1)
            e_body(E_ - 1, E_ - 2, None)
            e_tail(E_ - 1, E_ - 1)
            with dve.If(dve.value_load(most_i[0:1, 0:1], min_val=0, max_val=T) > CAP):
                with dve.Fori(0, 2) as ps:
                    dve.wait_ge(S["e_gtr"], E_)
                    v.tensor_scalar(slots_i, slots_i, float(CAP), None, ALU.add).then_inc(S["o_iota"], 1)
                    with dve.Fori(0, E_) as e:
                        n = ps * E_ + e + E_
                        dve.wait_ge(S["o_iota"], ps + 1)
                        e_prologue(n, e)
                        e_body(n, None, None)
                        e_tail(n, e)
            v.wait_ge(S["rms_ready"], 5)
            v.reciprocal(rinv[:, :], rt[:, :]).then_inc(S["rinv_ready"], 1)
            v.wait_ge(S["rinv_ready"], 5)
            for c in range(DC):
                v.scalar_tensor_tensor(out=h3T[:, c, :], in0=xT[:, c, :], scalar=vcol("norm_out_g", c), in1=rinv[:, :],
                                       op0=ALU.mult, op1=ALU.mult).then_inc(S["h_ready"], 1)
            for n in range(1, 6, 2):
                dve.wait_ge(S["h_tr"], 6 + n + 1)
                i, q = n // 2, n % 2
                rows = TILES[i][1]
                v.tensor_copy(htok[0:rows, i, 512 * q:512 * q + 512], banks[2 + n % 4][0:rows, :]).then_inc(S["h_dve"], 1)

        @block.tensor
        def _(pe):
            t = nc.tensor
            pe.wait_ge(S["const"], 7)
            pe.wait_ge(S["vec_in"], 16 * len(VEC_ROWS))
            t.transpose(banks[7][:, 0:P], vecrows[:, 0, :], ident[:, :])
            t.transpose(banks[7][:, P:VEC_N], vecrows[0:VEC_N - P, 1, :], ident[0:VEC_N - P, 0:VEC_N - P]) \
                .then_inc(S["tr_ready"], 1)
            pe.wait_ge(S["x_in"], 48)
            for c in range(DC):
                if c >= 2:
                    pe.wait_ge(S["xt_ready"], c - 1)
                for i, (t0, n) in enumerate(TILES):
                    mm = t.transpose(banks[c % 2][:, t0:t0 + n], xtok[0:n, i, P * c:P * c + P], ident[0:n, 0:n])
                mm.then_inc(S["tr_ready"], 1)
            pe.wait_ge(S["ws_in"], 16)
            for g_ in range(G):
                mm = t.transpose(banks[4 + g_ // 4][:, P * (g_ % 4):P * (g_ % 4) + P], wsraw[:, g_, :], ident[:, :])
                if g_ % 4 == 3:
                    mm.then_inc(S["ws_tr"], 1)
            norm_pe(0, tokens(B[2]))
            pe.wait_ge(S["ws_copied"], 2)
            n_piece = [0]

            def arrived():
                n = n_piece[0]
                n_piece[0] += 1
                pe.wait_ge(landed[n % RING], arrival[n])
                return n % RING

            def v_transposes(q):
                pe.wait_ge(S["gelu_done"], 4 * q + 4)
                if q:
                    pe.wait_ge(S["v_evac"], 3 * q)
                for i, (t0, n) in enumerate(TILES):
                    for j in range(4):
                        mm = t.transpose(banks[(4, 5, 7)[i]][0:n, P * j:P * j + P], vT[:, 4 * q + j, t0:t0 + n],
                                         ident[:, :])
                mm.then_inc(S["v_tr"], 1)

            pe.wait_ge(S["h_ready"], DC)
            for n in range(16):
                w = slot(arrived(), "p (k n) -> p k n", k=DC)
                for j in range(2):
                    g_ = 2 * n + j
                    if g_ >= 4:
                        pe.wait_ge(S["gelu_done"], g_ - 3)
                    for k in range(DC):
                        mm = t.matmul(banks[g_ % 4][:, 0:T], w[:, k, P * j:P * j + P], hT[:, k, :],
                                      start=(k == 0), stop=(k == DC - 1))
                    mm.then_inc(S["z_ready"], 1)
                if n in (2, 4, 6, 8):
                    v_transposes(n // 2 - 1)
            pe.wait_ge(S["v_norm"], 3)
            pe.wait_ge(S["ws_masked"], 1)
            pe.wait_ge(S["wsS_in"], 16 * NB)
            for c in range(AC):
                if c < 4:
                    pe.wait_ge(S["gelu_done"], 29 + c)
                else:
                    pe.wait_ge(S["mix_add"], c - 3)
                for i, (t0, n) in enumerate(TILES):
                    w = wsT[:, c // 2, :] if i < 2 else wsS[0:SMP, c // 2, :]
                    mm = t.matmul(banks[c % 4][:, t0:t0 + n], vtok[0:n, i, P * c:P * c + P], w,
                                  start=(i == 0), stop=True, skip_group_check=True)
                mm.then_inc(S["mix_ready"], 1)
            pe.wait_ge(S["mix_done"], AC)
            for c in range(DC):
                w = slot(arrived(), "p (k n) -> p k n", k=AC)
                if c >= 4:
                    pe.wait_ge(S["xt_ready"], DC + c - 3)
                for k in range(AC):
                    mm = t.matmul(banks[c % 4][:, 0:T], w[:, k, :], vT[:, k, :], start=(k == 0), stop=(k == AC - 1))
                mm.then_inc(S["ao_ready"], 1)
            norm_pe(1, tokens(B[2]))

            def f_product(bank, w2, x2, k, start, stop):
                for m, (l, r) in enumerate(((0, 0), (1, 0), (0, 1))):
                    mm = t.matmul(bank[:, 0:T], w2[l], x2[r][:, k, :], start=(start and m == 0), stop=(stop and m == 2))
                return mm

            for n in range(22):
                q, up = n // 2, n % 2
                n_piece[0] += 1
                pe.wait_ge(S["f_lo"], n + 1)
                w2 = [x[:, n % FRING, :].rearrange("p (k n) -> p k n", k=DC) for x in (fwH, fwL)]
                for j in range(2):
                    if q:
                        pe.wait_ge(S["hf_ready" if up else "sg_ready"], 2 * q + j - 1)
                    for k in range(DC):
                        if n == 0 and j == 0:
                            pe.wait_ge(S["f_xl"], k + 1)
                        mm = f_product(banks[2 * up + j], [x[:, k, P * j:P * j + P] for x in w2], (fxH, fxL), k,
                                       k == 0, k == DC - 1)
                    mm.then_inc(S["ffu_ready" if up else "ffg_ready"], 1)
            for n in range(22, FPIECES):
                c, hf = (n - 22) // 2, n % 2
                n_piece[0] += 1
                if c >= 4:
                    pe.wait_ge(S["xt_ready"], 2 * DC + c - 3)
                elif c == 0 and hf == 0:
                    pe.wait_ge(S["sg_ready"], FC)
                elif c >= 2 and hf == 0:
                    pe.wait_ge(S["hf_ready"], FC)
                pe.wait_ge(S["f_lo"], n + 1)
                w2 = [x[:, n % FRING, 0:11 * P].rearrange("p (k n) -> p k n", k=11) for x in (fwH, fwL)]
                for k in range(11):
                    if c == 0:
                        pe.wait_ge(S["f_xl"], DC + 11 * hf + k + 1)
                    mm = f_product(banks[c % 4], [x[:, k, :] for x in w2], (fhH, fhL), 11 * hf + k,
                                   hf == 0 and k == 0, hf == 1 and k == 10)
                mm.then_inc(S["fd_ready"], 1)
            norm_pe(2, tokens(B[1]))
            pe.wait_ge(S["last_cols"], 2)
            for hf in range(2):
                for j in range(4):
                    mm = t.transpose(banks[4 + hf][0:1 + NB, P * j:P * j + P], lastc[:, 4 * hf + j, :], ident[:, :])
                mm.then_inc(S["last_tr"], 1)

            def project(bank, w, x, ks, inc, first_wait=None):
                for k in range(ks):
                    if first_wait is not None:
                        pe.wait_ge(S["mx_ready"], first_wait + k + 1)
                    mm = t.matmul(bank, w(k), x[:, k, :], start=(k == 0), stop=(k == ks - 1))
                if inc:
                    mm.then_inc(S[inc], 1)

            s_ = arrived()
            w1v = slot(s_, "p (k n) -> p k n", n=512, k=DC)
            a1v = slot(s_, "p (k n) -> p k n", n=512, off=512, k=DC)
            pe.wait_ge(S["xt_ready"], 3 * DC)
            project(banks[0][0:LW, 0:T], lambda k: w1v[:, k, :], m0T, DC, "lo1_ready", 0)
            project(banks[1][0:LW, 0:T], lambda k: a1v[:, k, :], m1T, DC, "lo1_ready", 8)
            s_ = arrived()
            g1v = slot(s_, "p (k n) -> p k n", n=DC * LG, k=DC)
            project(banks[2][:, 0:T], lambda k: g1v[:, k, 0:P], m0T, DC, None, 16)
            project(banks[3][0:LG - P, 0:T], lambda k: g1v[:, k, P:LG], m0T, DC, "lo1_ready", 16)
            s_ = arrived()
            w2v = (slot(s_, None, parts=LW, n=D), slot(s_, None, parts=LW, n=D, off=D))
            pe.wait_ge(S["last_rows"], 2)
            for n in range(16):
                if n % 8 == 0:
                    pe.wait_ge(S["lo1_done"], n // 8 + 1)
                if n >= 4:
                    pe.wait_ge(S["lo2_done"], n - 3)
                c = n % 8
                t.matmul(banks[4 + n % 4][:, 0:T], w2v[n // 8][:, P * c:P * c + P], (lw1, la1)[n // 8],
                         start=True, stop=True).then_inc(S["lo2_ready"], 1)
            pe.wait_ge(S["lo1_done"], 4)
            for n in range(0, 24, 2):
                w = slot(arrived(), "p (k n) -> p k n", k=DC)
                for j in range(2):
                    if n >= 4:
                        pe.wait_ge(S["kvr_done"], n + j - 3)
                    m = n // 8
                    project(banks[(n + j) % 4][:, 0:T], lambda k: w[:, k, P * j:P * j + P], (m1T, m0T, m1T)[m], DC,
                            "kvr_ready", 24 + 8 * m)
                if n == 18:
                    for c in range(DC):
                        pe.wait_ge(S["kk_sq"], c + 1)
                        if c < 4:
                            pe.wait_ge(S["lo2_done"], 13 + c)
                        else:
                            pe.wait_ge(S["kn_root"], c - 3)
                        t.matmul(banks[4 + c % 4][:, 0:T], halves[:, :], kkT[:, c, :], start=True, stop=True) \
                            .then_inc(S["kn_ready"], 1)
            for c in range(DC):
                pe.wait_ge(S["rk_ready"], c + 1)
                if c < 4:
                    pe.wait_ge(S["kn_root"], DC)
                else:
                    pe.wait_ge(S["bon_ready"], c - 3)
                t.matmul(banks[4 + c % 4][:, 0:T], halves[:, :], rkT[:, c, :], start=True, stop=True) \
                    .then_inc(S["rb_ready"], 1)
            pe.wait_ge(S["kvr_done"], 24)
            for n in range(18):
                m, i, q = n // 6, n % 6 // 2, n % 2
                if m == 1:
                    pe.wait_ge(S["scaled"], 4)
                if m == 2:
                    pe.wait_ge(S["scaled"], 8)
                if n >= 4:
                    pe.wait_ge(S["tk_act" if n % 2 == 0 else "tk_dve"], (n - 4) // 2 + 1)
                src = (vfT, BtT, KtT)[m]
                t0, rows = TILES[i]
                for j in range(4):
                    mm = t.transpose(banks[n % 4][0:rows, P * j:P * j + P], src[:, 4 * q + j, t0:t0 + rows], ident[:, :])
                mm.then_inc(S["tk_tr"], 1)
            pe.wait_ge(S["tk_act"], 9)
            pe.wait_ge(S["tk_dve"], 9)
            pe.wait_ge(S["masks"], 1)
            pe.wait_ge(S["memz"], 3)
            pe.wait_ge(S["bon_ready"], DC)
            for st in steps:
                k = st[0]
                if k == "score":
                    _, u, f, i = st
                    t0 = 128 * i
                    for hh in range(8):
                        p, hr = 4 * f + hh // 2, hrows(hh % 2)
                        if hh >= 6:
                            pe.wait_ge(S["ms_ready"], 8 * u + hh - 5)
                        elif u and hh == 0:
                            pe.wait_ge(S["s_done"], 4 * u)
                        elif u and hh == 3:
                            pe.wait_ge(S["y_done"], 2 * u)
                        out_ = banks[hh % 6][:, :].rearrange("p (m r t) -> p m r t", m=2, r=2)
                        for m, src in enumerate((kT, aT)):
                            mm = t.matmul(out_[:, m], src[hr, p, t0:t0 + 128], QR[hr, p, :, t0:t0 + 128],
                                          start=(m == 0), stop=True, skip_group_check=True)
                        mm.then_inc(S["sc_ready"], 1)
                elif k == "x0":
                    u = st[1]
                    pe.wait_ge(S["xt0_ready"], 2 * u + 2)
                    for b in range(2):
                        for j in range(4):
                            mm = t.transpose(banks[b][:, P * j:P * j + P], XX[:, 4 * b + j, 1, :], ident[:, :])
                        mm.then_inc(S["xt_tr"], 1)
                elif k == "t1":
                    _, u, m = st
                    n = 5 * u + m - 1
                    for b in range(2):
                        if m == 1:
                            pe.wait_ge(S["x0_ready"], 2 * u + b + 1)
                        else:
                            pe.wait_ge(S["x_done"], 4 * (n - 1) + 2 * b + 2)
                        for j in range(4):
                            mm = t.matmul(banks[b][:, P * j:P * j + P], MS[:, 4 * b + j, BL, :], XX[:, 4 * b + j, 0, :],
                                          start=(j == 0), stop=True, skip_group_check=True)
                        mm.then_inc(S["t1_ready"], 1)
                elif k == "xl":
                    _, u, m = st
                    n = 5 * u + m - 1
                    for b in range(2):
                        pe.wait_ge(S["t1_done"], 2 * n + b + 1)
                        for j in range(4):
                            hh, bank = 4 * b + j, banks[2 + 2 * b + j // 2]
                            o = 256 * (j % 2)
                            t.matmul(bank[:, o:o + P], XX[:, hh, 1, :], T1[:, b, j, :],
                                     start=(j % 2 == 0), stop=True, skip_group_check=True)
                            mm = t.matmul(bank[:, o + P:o + 2 * P], T1[:, b, j, :], XX[:, hh, 1, :],
                                          start=False, stop=True, skip_group_check=True)
                            if j % 2:
                                mm.then_inc(S["x_ready"], 1)
                elif k == "w1":
                    _, u, f, i, c = st
                    n = 4 * f + c
                    if c % 2 == 0:
                        pe.wait_ge(S["x_done"], 20 * u + 20)
                    for pr in range(4):
                        p = 4 * f + pr
                        for h2 in range(2):
                            o = P * pr + 64 * h2
                            t.matmul(banks[0][:, o:o + 64], MS[:, 2 * pr + h2, KL, :], Vk[:, i, 512 * f + o:512 * f + o + 64],
                                     start=(o == 0), stop=False, skip_group_check=True)
                    if c:
                        pe.wait_ge(S["s_done"], 2 * n)
                    for pr in range(4):
                        p = 4 * f + pr
                        mm = t.matmul(banks[0][:, P * pr:P * pr + P], QR[:, p, 0, 128 * i:128 * i + 128],
                                      Sbd[:, c % 2, p, :], start=False, stop=True, skip_group_check=True)
                    mm.then_inc(S["w1_ready"], 1)
                elif k == "u":
                    _, u, f, i, c = st
                    n, tb = 4 * f + c, 64 * (c % 2)
                    for pr in range(4):
                        o = 512 * f + P * pr
                        t.matmul(banks[2][:, P * pr:P * pr + P], Kk[tb:tb + 64, i, o:o + P], Vk[tb:tb + 64, i, o:o + P],
                                 start=(pr == 0), stop=False, skip_group_check=True)
                    pe.wait_ge(S["w1_done"], n + 1)
                    for hh in range(8):
                        mm = t.matmul(banks[1][:, 64 * hh:64 * hh + 64], XX[:, hh, 1, :], W1[:, 64 * hh:64 * hh + 64],
                                      start=(hh == 0), stop=True, skip_group_check=True)
                    mm.then_inc(S["u_ready"], 1)
                elif k == "s":
                    _, u, f, i, c = st
                    n, tb = 4 * f + c, 64 * (c % 2)
                    pe.wait_ge(S["u_done"], n + 1)
                    for pr in range(4):
                        o = 512 * f + P * pr
                        mm = t.matmul(banks[2][:, P * pr:P * pr + P], Bk[tb:tb + 64, i, o:o + P], Us[tb:tb + 64, P * pr:P * pr + P],
                                      start=False, stop=True, skip_group_check=True)
                    mm.then_inc(S["s_ready"], 1)
                elif k == "y":
                    _, u, f, i, c = st
                    n, tb = 4 * f + c, 64 * (c % 2)
                    bank = banks[3 + c % 2]
                    if n >= 2:
                        pe.wait_ge(S["y_done"], n - 1)
                    for pr in range(4):
                        p, o = 4 * f + pr, 64 * pr
                        t.matmul(bank[:, o:o + 64], Sbd[:, c % 2, p, :], QR[:, p, 1, CH * c:CH * c + CH],
                                 start=(pr == 0), stop=False, skip_group_check=True)
                        for h2 in range(2):
                            hh, hr, vo = 2 * pr + h2, hrows(h2), 512 * f + P * pr + 64 * h2
                            t.matmul(bank[hr, o:o + 64], Vk[:, i, vo:vo + 64], MS[:, hh, KA, tb:tb + 64],
                                     start=False, stop=False, skip_group_check=True)
                            mm = t.matmul(bank[hr, o:o + 64], Us[:, 64 * hh:64 * hh + 64], MS[:, hh, BA, tb:tb + 64],
                                          start=False, stop=True, skip_group_check=True)
                    mm.then_inc(S["y_ready"], 1)
                elif k == "q_score":
                    p = st[1]
                    if p:
                        q_wait(pe, "q_oc", p - 1, 1)
                    for h2 in range(2):
                        hr = hrows(h2)
                        out_ = banks[6 + h2][0:SMP, 0:P].rearrange("p (m r t) -> p m r t", m=2, r=2)
                        for m, src in enumerate((kT, aT)):
                            mm = t.matmul(out_[:, m], src[hr, p, NP_:T], QR[hr, p, :, NP_:T],
                                          start=(m == 0), stop=True, skip_group_check=True)
                        mm.then_inc(S["q_pe"], 1)
                elif k == "q_s0":
                    p = st[1]
                    q_wait(pe, "q_ms", p, 1)
                    pe.wait_ge(S["nat_in"], 16 * 2 * (p + 1))
                    for b in range(NB):
                        mm = t.transpose(banks[6][:, 64 * b:64 * b + 64], nat[:, b, :], ident[0:HD, 0:HD])
                    mm.then_inc(S["q_pe"], 1)
                elif k == "q_x0":
                    p = st[1]
                    q_wait(pe, "q_xt0", p, 1)
                    for h2 in range(2):
                        mm = t.transpose(banks[7][0:SMP, 32 * h2:32 * h2 + 32], XXq[:, h2, 1, :], ident[0:SMP, 0:SMP])
                    mm.then_inc(S["q_pe"], 1)
                elif k == "q_qs":
                    p = st[1]
                    q_wait(pe, "q_s0", p, 1)
                    out_ = banks[6][:, 0:2 * SMP].rearrange("p (r t) -> p r t", r=2)
                    for b in range(NB):
                        t.matmul(out_[:, :, NS * b:NS * b + NS], S0bd[:, b, :], QR[:, p, :, NP_ + NS * b:NP_ + NS * b + NS],
                                 start=(b == 0), stop=False, skip_group_check=True)
                    for h2 in range(2):
                        vo = P * p + 64 * h2
                        mm = t.matmul(banks[6][hrows(h2), 0:2 * SMP].rearrange("p (r t) -> p r t", r=2),
                                      Vk[0:SMP, 2, vo:vo + 64], MSq[:, h2, 0:2, :],
                                      start=False, stop=False, skip_group_check=True)
                    mm.then_inc(S["q_pe"], 1)
                elif k == "q_t1":
                    p = st[1]
                    q_wait(pe, "q_x", p)
                    for h2 in range(2):
                        mm = t.matmul(banks[7][0:SMP, 32 * h2:32 * h2 + 32], MSq[:, h2, BL, :], XXq[:, h2, 0, :],
                                      start=(h2 == 0), stop=True, skip_group_check=True)
                    mm.then_inc(S["q_pe"], 1)
                elif k == "q_x2":
                    p = st[1]
                    q_wait(pe, "q_t1c", p)
                    for h2 in range(2):
                        mm = t.matmul(banks[7][0:SMP, 32 * h2:32 * h2 + 32], T1q[:, h2, :], XXq[:, h2, 1, :],
                                      start=(h2 == 0), stop=True, skip_group_check=True)
                    mm.then_inc(S["q_pe"], 1)
                elif k == "q_w1":
                    p = st[1]
                    q_wait(pe, "q_xt2c", p)
                    q_wait(pe, "q_w1t", p)
                    t.transpose(banks[7][0:SMP, 0:P], W1Tq, ident[:, :]).then_inc(S["q_pe"], 1)
                elif k == "q_u":
                    p = st[1]
                    q_wait(pe, "q_w1", p)
                    for h2 in range(2):
                        mm = t.matmul(banks[7][0:SMP, 64 * h2:64 * h2 + 64], XXq[:, h2, 1, :], W1q[:, 64 * h2:64 * h2 + 64],
                                      start=(h2 == 0), stop=True, skip_group_check=True)
                    mm.then_inc(S["q_pe"], 1)
                elif k == "q_y":
                    p = st[1]
                    q_wait(pe, "q_uc", p)
                    for h2 in range(2):
                        mm = t.matmul(banks[6][hrows(h2), SMP:2 * SMP], Uq[:, 64 * h2:64 * h2 + 64], MSq[:, h2, BA, :],
                                      start=False, stop=True, skip_group_check=True)
                    mm.then_inc(S["q_pe"], 1)
                elif k == "q_st":
                    p = st[1]
                    pe.wait_ge(S["q_vx"], 2 * p + 2)
                    pe.wait_ge(S["q_ux"], 2 * p + 2)
                    for m, (src, x) in enumerate(((Kk, Vexp), (Bk, Uexp))):
                        for h2 in range(2):
                            o = P * p + 64 * h2
                            mm = t.matmul(banks[7][hrows(h2), :], src[0:SMP, 2, o:o + 64],
                                          x[:, h2].rearrange("p b i -> p (b i)"),
                                          start=(m == 0), stop=(m == 1), skip_group_check=True)
                    mm.then_inc(S["q_pe"], 1)
                elif k == "q_out":
                    p = st[1]
                    q_wait(pe, "q_send", p)
                    q_wait(pe, "q_yc", p)
                    for b in range(NB):
                        mm = t.transpose(banks[6 + b // 4][0:HD, P * (b % 4):P * (b % 4) + P], Send[:, b, :], ident[:, :])
                    mm.then_inc(S["q_pe"], 1)
            for hf in range(2):
                if hf == 0:
                    pe.wait_ge(S["s_done"], 16)
                    pe.wait_ge(S["y_done"], 8)
                for j in range(4):
                    mm = t.transpose(banks[hf][:, P * j:P * j + P], Sbd[:, 0, 4 * hf + j, :], ident[:, :])
                mm.then_inc(S["st_tr"], 1)
            q_wait(pe, "q_yc", DC - 1)
            for c in range(DC):
                if c >= 2:
                    pe.wait_ge(S["gn_yc"], c - 1)
                t.matmul(banks[2 + c % 2][:, 0:T], halves[:, :], yT[:, c, :], start=True, stop=True) \
                    .then_inc(S["gn_mean"], 1)
            s_ = arrived()
            g2v = (slot(s_, None, n=D), slot(s_, None, parts=LG - P, n=D, off=D))
            q_wait(pe, "q_oc", DC - 1, 1)
            for c in range(DC):
                pe.wait_ge(S["gn_sq"], c + 1)
                if c >= 2:
                    pe.wait_ge(S["gn_root"], c - 1)
                t.matmul(banks[4 + c % 2][:, 0:T], halves[:, :], rkT[:, c, :], start=True, stop=True) \
                    .then_inc(S["gn_var"], 1)
                if c >= 2:
                    pe.wait_ge(S["yg_ready"], c - 1)
                t.matmul(banks[6 + c % 2][:, 0:T], g2v[0][:, P * c:P * c + P], lg1[:, 0, :], start=True, stop=False)
                t.matmul(banks[6 + c % 2][:, 0:T], g2v[1][:, P * c:P * c + P], lg1[0:LG - P, 1, :], start=False, stop=True) \
                    .then_inc(S["g_ready"], 1)
            pe.wait_ge(S["st_row"], 2)
            pe.wait_ge(S["yg_ready"], DC)
            for q in range(4):
                w = slot(arrived(), "p (k n) -> p k n", k=DC)
                for j in range(2):
                    c = 2 * q + j
                    if c >= 4:
                        pe.wait_ge(S["xt_ready"], 3 * DC + c - 3)
                    for k in range(DC):
                        mm = t.matmul(banks[c % 4][:, 0:T], w[:, k, P * j:P * j + P], yT[:, k, :],
                                      start=(k == 0), stop=(k == DC - 1))
                    mm.then_inc(S["wo_ready"], 1)
            norm_pe(3, tokens(B[9]))
            pe.wait_ge(S["h_ready"], 4 * DC)
            pe.wait_ge(S["router_in"], 16)
            for i, (t0, n) in enumerate(TILES):
                for k in range(DC):
                    mm = t.matmul(banks[i // 2][0:n, 8 * i:8 * i + 8], h3T[:, k, t0:t0 + n], router[:, k, :],
                                  start=(k == 0), stop=(k == DC - 1))
                mm.then_inc(S["r_logit"], 1)
            for n in range(6):
                i, q = n // 2, n % 2
                t0, rows = TILES[i]
                if n >= 4:
                    pe.wait_ge(S["h_act" if n % 2 == 0 else "h_dve"], (n - 4) // 2 + 1)
                for j in range(4):
                    mm = t.transpose(banks[2 + n % 4][0:rows, P * j:P * j + P], h3T[:, 4 * q + j, t0:t0 + rows], ident[:, :])
                mm.then_inc(S["h_tr"], 1)
            pe.wait_ge(S["r_sel"], 3)
            pe.wait_ge(S["r_const"], 4)
            first = True
            for i, (_, n) in enumerate(TILES):
                for j in range(i + 1):
                    nj = TILES[j][1]
                    lhs = tri[0:n, 0:n] if j == i else ones[0:nj, 0:n]
                    t.matmul(banks[1][0:n, 32 + 8 * i:40 + 8 * i], lhs, chosen[0:nj, j, 0:8],
                             start=first, stop=(j == i), skip_group_check=True)
                    first = False
            for j in range(3):
                nj = TILES[j][1]
                mm = t.matmul(banks[1][:, 64:72], ones[0:nj, :], chosen[0:nj, j, 0:8], start=False, stop=(j == 2),
                              skip_group_check=True)
            mm.then_inc(S["r_pos"], 1)
            pe.wait_ge(S["h_act"], 3)
            pe.wait_ge(S["h_dve"], 3)
            pe.wait_ge(S["r_most"], 2)

            def e_gather(n):
                pe.wait_ge(S["e_sx"], 3 * n + 3)
                for q in range(2):
                    for j in range(4):
                        c = 4 * q + j
                        for i, (_, rows) in enumerate(TILES):
                            mm = t.matmul(banks[6 + q][:, CAP * j:CAP * j + CAP], htok[0:rows, i, P * c:P * c + P],
                                          Sx[0:rows, i, :], start=(i == 0), stop=(i == 2), skip_group_check=True)
                    mm.then_inc(S["e_xg"], 1)

            def product(dst, lhs, rhs, k, start, stop):
                for m, (l, r) in enumerate(((0, 0), (0, 1), (1, 0))):
                    mm = t.matmul(dst, lhs[l][:, k, :], rhs[r], start=(start and m == 0), stop=(stop and m == 2),
                                  skip_group_check=True)
                return mm

            def e_gates(n):
                pe.wait_ge(S["e_ya"], n + 1)
                pe.wait_ge(S["e_sgx"], 3 * n + 3)
                for i, (t0, rows) in enumerate(TILES):
                    mm = t.transpose(banks[4][0:CAP, t0:t0 + rows], Sg[0:rows, i, :], ident[0:rows, 0:rows])
                mm.then_inc(S["e_gtr"], 1)

            def e_scatter(n, c):
                if c == 0:
                    pe.wait_ge(S["e_yd"], n + 1)
                    pe.wait_ge(S["e_gt"], n + 1)
                if c >= 2:
                    pe.wait_ge(S["e_xt"], n * DC + (c - 1))
                t.matmul(banks[6 + c % 2][:, 0:T], yS[:, P * c:P * c + P], GT, start=True, stop=True) \
                    .then_inc(S["e_sc"], 1)

            def e_body(n, prev, nxt):
                pe.wait_ge(S["e_xgd"], 2 * n + 2)
                for i in range(EPIECES):
                    pe.wait_ge(S["e_lo"], n * EPIECES + (i + 1))
                    w2 = (wH[:, i % HRING, :], wL[:, i % HRING, :])
                    if i < 22:
                        q = i // 2
                        if q:
                            pe.wait_ge(S["e_he" if i % 2 else "e_sg"], n * 11 + q)
                        parts = [x.rearrange("p (k n) -> p k n", k=DC) for x in w2]
                        for k in range(DC):
                            mm = product(banks[2 * (i % 2)][0:CAP, 0:256], (xgH, xgL), [x[:, k, :] for x in parts], k,
                                         k == 0, k == DC - 1)
                    else:
                        r = i - 22
                        pe.wait_ge(S["e_hl"], n * 11 + (r + 1))
                        parts = [x.rearrange("p (k n) -> p k n", k=2) for x in w2]
                        for k in range(2):
                            for hf in range(2):
                                mm = product(banks[4 + hf][0:CAP, :], (hH, hL),
                                             [x[:, k, 512 * hf:512 * hf + 512] for x in parts], 2 * r + k,
                                             i == 22 and k == 0, i == 32 and k == 1)
                    mm.then_inc(S["e_piece"], 1)
                    if i % 2 == 0 and 2 <= i <= 22:
                        q = (i - 2) // 2
                        pe.wait_ge(S["e_he"], n * 11 + (q + 1))
                        if q >= 2:
                            pe.wait_ge(S["e_hl"], n * 11 + (q - 1))
                        for j in range(2):
                            mm = t.transpose(banks[1 + 2 * (q % 2)][:, CAP * j:CAP * j + CAP],
                                             hS[:, q % 2, P * j:P * j + P], ident[0:CAP, 0:CAP])
                        mm.then_inc(S["e_htr"], 1)
                    if i == 3 and prev is not None:
                        e_gates(prev)
                    if 7 <= i < 15 and prev is not None:
                        e_scatter(prev, i - 7)
                    if i == 26 and nxt is not None:
                        if prev is not None:
                            pe.wait_ge(S["e_xt"], prev * DC + DC)
                        e_gather(nxt)

            def e_tail(n):
                e_gates(n)
                for c in range(DC):
                    e_scatter(n, c)

            e_gather(0)
            e_body(0, None, 1)
            with pe.Fori(1, E_ - 1) as e:
                e_body(e, e - 1, e + 1)
            e_body(E_ - 1, E_ - 2, None)
            e_tail(E_ - 1)
            with pe.If(pe.value_load(most_i[0:1, 0:1], min_val=0, max_val=T) > CAP):
                pe.wait_ge(S["e_xt"], DC * E_)
                with pe.Fori(0, 2) as ps:
                    with pe.Fori(0, E_) as e:
                        n = ps * E_ + e + E_
                        e_gather(n)
                        e_body(n, None, None)
                        e_tail(n)
                pe.wait_ge(S["e_xt"], DC * 3 * E_)
            sq = tokens(B[9])
            for c in range(DC):
                pe.wait_ge(S["sq_ready"], DC * 4 + c + 1)
                mm = t.matmul(banks[0][:, 0:T], ones[:, :], sq[:, c, :], start=(c == 0), stop=(c == DC - 1))
            mm.then_inc(S["norm_sum"], 1)
            pe.wait_ge(S["h_ready"], 5 * DC)
            for n in range(6):
                i, q = n // 2, n % 2
                t0, rows = TILES[i]
                if n >= 4:
                    pe.wait_ge(S["h_act" if n % 2 == 0 else "h_dve"], 3 + (n - 4) // 2 + 1)
                for j in range(4):
                    mm = t.transpose(banks[2 + n % 4][0:rows, P * j:P * j + P], h3T[:, 4 * q + j, t0:t0 + rows], ident[:, :])
                mm.then_inc(S["h_tr"], 1)


OUTS = {"y_prompt": (1, NP_, D), "y_sample": (NB, NS, D), "chunk_v": (1, NB, NS, AW), "shift_prompt": (1, 1, D),
        "wkv_prompt": (1, 1, H, HD, HD), "shift_sample": (1, NB, D), "wkv_sample": (1, NB, H, HD, HD)}


def kernel(**inputs):
    import numpy as np
    import concourse.bacc as bacc
    from concourse.bass_utils import run_bass_kernel_spmd

    nc = bacc.Bacc("TRN2", target_bir_lowering=False, num_devices=1)
    arrays, a = {}, {}
    for name, value in inputs.items():
        value = np.ascontiguousarray(value)
        if value.size == 0:
            continue
        arrays[name] = value
        a[name] = nc.dram_tensor(name, value.shape, mybir.dt.from_np(value.dtype), kind="ExternalInput").ap()
    out = {name: nc.dram_tensor("out_" + name, shape, F32, kind="ExternalOutput").ap() for name, shape in OUTS.items()}
    trunk_kernel(nc, a, out)
    got = run_bass_kernel_spmd(nc, [arrays], core_ids=[0]).results[0]
    return tuple(got["out_" + name] for name in OUTS)
```
